# Optimizing a Trainium2 kernel written in Bass

```python
import jax, jax.numpy as jnp
from jax import lax
import numpy as np

D_MODEL = 1024
BATCH = 1
SEQ = 512
DEPTH = 2

N_MEM = 256
RMS_EPS = 1e-6
N_SUBNORMS = 6

ML_HEADS = 4
ML_QK_DIM = D_MODEL // 2 // ML_HEADS
ML_V_DIM = D_MODEL // ML_HEADS
ML_CHUNK = 64
ML_GATE_CAP = 15.0
ML_IN_WIDTH = 2 * ML_HEADS * ML_QK_DIM + 2 * D_MODEL + 2 * ML_HEADS

SB_HEADS = 16
SB_HEAD_DIM = D_MODEL // SB_HEADS
SB_BLOCK = 128

XA_HEADS = 4
XA_HEAD_DIM = D_MODEL // XA_HEADS

D_FF = -(-8 * D_MODEL // (3 * 256)) * 256

N_ML_LAYERS = (DEPTH + 1) // 2
N_SB_LAYERS = DEPTH // 2


def rms_norm(x, gain):
    x32 = x.astype(jnp.float32)
    y = x32 * lax.rsqrt(jnp.mean(x32 * x32, axis=-1, keepdims=True) + RMS_EPS)
    return (y * gain.astype(jnp.float32)).astype(x.dtype)

def mlstm_mixer(h, w_in, b_gate, head_gain, w_out):
    B, S, _ = h.shape
    H, dk, dv, L = ML_HEADS, ML_QK_DIM, ML_V_DIM, ML_CHUNK
    nc = S // L
    qk = H * dk
    proj = h @ w_in
    q, k, v, o, gates = jnp.split(proj, [qk, 2 * qk, 2 * qk + D_MODEL, 2 * qk + 2 * D_MODEL], axis=-1)
    gates = gates.astype(jnp.float32) + b_gate.astype(jnp.float32)
    gates = ML_GATE_CAP * jnp.tanh(gates / ML_GATE_CAP)
    ig = gates[..., :H]
    lf = jax.nn.log_sigmoid(gates[..., H:])

    def to_chunks(t, d):
        return t.astype(jnp.float32).reshape(B, nc, L, H, d).transpose(1, 0, 3, 2, 4)

    def gate_chunks(t):
        return t.reshape(B, nc, L, H).transpose(1, 0, 3, 2)

    qc = to_chunks(q, dk)
    kc = to_chunks(k, dk) * (dk ** -0.5)
    vc = to_chunks(v, dv)
    igc, lfc = gate_chunks(ig), gate_chunks(lf)
    causal = jnp.tril(jnp.ones((L, L), dtype=bool))

    def step(carry, inp):
        C, n, m = carry
        qb, kb, vb, igb, lfb = inp
        b = jnp.cumsum(lfb, axis=-1)
        log_d = jnp.where(causal, b[..., :, None] - b[..., None, :] + igb[..., None, :], -jnp.inf)
        m_inter = b + m[..., None]
        m_t = jnp.maximum(jnp.max(log_d, axis=-1), m_inter)
        d = jnp.exp(log_d - m_t[..., None])
        s = jnp.einsum('bhtd,bhsd->bhts', qb, kb) * d
        inter = jnp.exp(m_inter - m_t)
        num = jnp.einsum('bhts,bhsv->bhtv', s, vb) + inter[..., None] * jnp.einsum('bhvd,bhtd->bhtv', C, qb)
        den = jnp.sum(s, axis=-1) + inter * jnp.einsum('bhd,bhtd->bht', n, qb)
        h_out = num / jnp.maximum(jnp.abs(den), jnp.exp(-m_t))[..., None]
        b_last = b[..., -1]
        g = b_last[..., None] - b + igb
        m_new = jnp.maximum(b_last + m, jnp.max(g, axis=-1))
        w = jnp.exp(g - m_new[..., None])
        decay = jnp.exp(b_last + m - m_new)
        C = decay[..., None, None] * C + jnp.einsum('bhs,bhsv,bhsd->bhvd', w, vb, kb)
        n = decay[..., None] * n + jnp.einsum('bhs,bhsd->bhd', w, kb)
        return (C, n, m_new), h_out

    init = (jnp.zeros((B, H, dv, dk), jnp.float32),
            jnp.zeros((B, H, dk), jnp.float32),
            jnp.zeros((B, H), jnp.float32))
    _, hs = lax.scan(step, init, (qc, kc, vc, igc, lfc))
    hs = hs.transpose(1, 0, 3, 2, 4).reshape(B, S, H, dv)
    hs = rms_norm(hs, head_gain.reshape(H, dv))
    og = jax.nn.sigmoid(o.astype(jnp.float32)).reshape(B, S, H, dv)
    out = (hs * og).reshape(B, S, D_MODEL).astype(h.dtype)
    return out @ w_out

def stick_breaking_mixer(h, w_qkv, w_out):
    B, S, _ = h.shape
    H, dh = SB_HEADS, SB_HEAD_DIM
    qkv = (h @ w_qkv).reshape(B, S, 3, H, dh).astype(jnp.float32)
    q = qkv[:, :, 0].transpose(0, 2, 1, 3)
    k = qkv[:, :, 1].transpose(0, 2, 1, 3)
    v = qkv[:, :, 2].transpose(0, 2, 1, 3)
    scale = dh ** -0.5
    outs = []
    for blk in range(S // SB_BLOCK):
        q0 = blk * SB_BLOCK
        kend = q0 + SB_BLOCK
        qb = q[:, :, q0:kend]
        kb = k[:, :, :kend]
        vb = v[:, :, :kend]
        z = jnp.einsum('bhtd,bhsd->bhts', qb, kb) * scale
        t_idx = q0 + jnp.arange(SB_BLOCK)[:, None]
        s_idx = jnp.arange(kend)[None, :]
        strict = s_idx < t_idx
        log_1m = jnp.where(strict, jax.nn.log_sigmoid(-z), 0.0)
        suffix = lax.cumsum(log_1m, axis=3, reverse=True) - log_1m
        a = jnp.where(strict, jnp.exp(jax.nn.log_sigmoid(z) + suffix), 0.0)
        outs.append(jnp.einsum('bhts,bhsd->bhtd', a, vb))
    o = jnp.concatenate(outs, axis=2)
    o = o.transpose(0, 2, 1, 3).reshape(B, S, D_MODEL).astype(h.dtype)
    return o @ w_out

def memory_cross_attention(h, mem_n, w_q, w_kv, w_o):
    B, S, _ = h.shape
    q = (h @ w_q).reshape(B, S, XA_HEADS, XA_HEAD_DIM)
    kv = (mem_n @ w_kv).reshape(B, mem_n.shape[1], 2, XA_HEADS, XA_HEAD_DIM)
    k, v = kv[:, :, 0], kv[:, :, 1]
    s = jnp.einsum('bthd,bmhd->bhtm', q, k).astype(jnp.float32) * (XA_HEAD_DIM ** -0.5)
    p = jax.nn.softmax(s, axis=-1).astype(v.dtype)
    o = jnp.einsum('bhtm,bmhd->bthd', p, v).reshape(B, S, D_MODEL)
    return o @ w_o

def swiglu_ffn(h, w_gate_up, w_down):
    gate, up = jnp.split(h @ w_gate_up, 2, axis=-1)
    return (jax.nn.silu(gate) * up) @ w_down

def first_inputs(seed: int = 0) -> dict:
    key = jax.random.key(seed)
    ks = jax.random.split(key, 16)

    def w(k, shape, fan_in):
        return jax.random.normal(k, shape, jnp.float32) * (fan_in ** -0.5)

    x = jax.random.normal(ks[0], (BATCH, SEQ, D_MODEL), jnp.float32)
    mem = jax.random.normal(ks[1], (BATCH, N_MEM, D_MODEL), jnp.float32)
    mem_norm_gain = 1.0 + 0.02 * jax.random.normal(ks[2], (D_MODEL,), jnp.float32)
    norm_gains = 1.0 + 0.02 * jax.random.normal(ks[3], (DEPTH, N_SUBNORMS, D_MODEL), jnp.float32)
    ml_w_in = w(ks[4], (N_ML_LAYERS, D_MODEL, ML_IN_WIDTH), D_MODEL)
    kb1, kb2 = jax.random.split(ks[5])
    b_in = 0.01 * jax.random.normal(kb1, (N_ML_LAYERS, ML_HEADS), jnp.float32)
    b_f = jnp.linspace(3.0, 6.0, ML_HEADS)[None, :] + 0.01 * jax.random.normal(kb2, (N_ML_LAYERS, ML_HEADS), jnp.float32)
    ml_b_gate = jnp.concatenate([b_in, b_f], axis=-1)
    ml_head_gain = 1.0 + 0.02 * jax.random.normal(ks[6], (N_ML_LAYERS, D_MODEL), jnp.float32)
    ml_w_out = w(ks[7], (N_ML_LAYERS, D_MODEL, D_MODEL), D_MODEL)
    sb_w_qkv = w(ks[8], (N_SB_LAYERS, D_MODEL, 3 * D_MODEL), D_MODEL)
    sb_w_out = w(ks[9], (N_SB_LAYERS, D_MODEL, D_MODEL), D_MODEL)
    xa_w_q = w(ks[10], (DEPTH, D_MODEL, D_MODEL), D_MODEL)
    xa_w_kv = w(ks[11], (DEPTH, D_MODEL, 2 * D_MODEL), D_MODEL)
    xa_w_o = w(ks[12], (DEPTH, D_MODEL, D_MODEL), D_MODEL)
    ffn_w_gate_up = w(ks[13], (DEPTH, D_MODEL, 2 * D_FF), D_MODEL)
    ffn_w_down = w(ks[14], (DEPTH, D_FF, D_MODEL), D_FF)
    return {"x": x, "mem": mem, "mem_norm_gain": mem_norm_gain, "norm_gains": norm_gains,
            "ml_w_in": ml_w_in, "ml_b_gate": ml_b_gate, "ml_head_gain": ml_head_gain, "ml_w_out": ml_w_out,
            "sb_w_qkv": sb_w_qkv, "sb_w_out": sb_w_out,
            "xa_w_q": xa_w_q, "xa_w_kv": xa_w_kv, "xa_w_o": xa_w_o,
            "ffn_w_gate_up": ffn_w_gate_up, "ffn_w_down": ffn_w_down}

def first_block(x, mem, mem_norm_gain, norm_gains, ml_w_in, ml_b_gate, ml_head_gain, ml_w_out,
              sb_w_qkv, sb_w_out, xa_w_q, xa_w_kv, xa_w_o, ffn_w_gate_up, ffn_w_down):
    mem_n = rms_norm(mem, mem_norm_gain)
    for layer in range(DEPTH):
        g = norm_gains[layer]
        j = layer // 2
        hn = rms_norm(x, g[0])
        if layer % 2 == 0:
            y = mlstm_mixer(hn, ml_w_in[j], ml_b_gate[j], ml_head_gain[j], ml_w_out[j])
        else:
            y = stick_breaking_mixer(hn, sb_w_qkv[j], sb_w_out[j])
        x = x + rms_norm(y, g[1])
        y = memory_cross_attention(rms_norm(x, g[2]), mem_n, xa_w_q[layer], xa_w_kv[layer], xa_w_o[layer])
        x = x + rms_norm(y, g[3])
        y = swiglu_ffn(rms_norm(x, g[4]), ffn_w_gate_up[layer], ffn_w_down[layer])
        x = x + rms_norm(y, g[5])
    return x


DEPTH_2 = 1

N_META = 16
HGRN_HEAD_V = 128
HGRN_WIDTH = D_MODEL // 2
HGRN_HEADS = HGRN_WIDTH // HGRN_HEAD_V
HGRN_EXPAND = 128
HGRN_KDIM = HGRN_HEADS * HGRN_EXPAND
CHUNK = 64
POOL_WINDOWS = (2, 4, 8, 16)
POOL_GROUPS = len(POOL_WINDOWS)
POOL_WIDTH = D_MODEL // 2
POOL_GROUP_DIM = POOL_WIDTH // POOL_GROUPS
D_FF_2 = 2816
CONV_WIDTH = 3
EPS = 1e-6
LOG_FLOOR = 1e-30
SPLITS = (HGRN_KDIM, HGRN_KDIM, HGRN_WIDTH, HGRN_WIDTH, POOL_WIDTH, D_MODEL, D_MODEL)
IN_COLS = sum(SPLITS)


def rmsnorm(x, gain):
    xf = x.astype(jnp.float32)
    y = xf * lax.rsqrt(jnp.mean(xf * xf, axis=-1, keepdims=True) + EPS)
    return (y * gain.astype(jnp.float32)).astype(x.dtype)

def _hgrn2_chunk_step(state, xs):
    q, k, v, lf = xs
    c = q.shape[2]
    b = jnp.cumsum(lf, axis=2)
    o_inter = jnp.einsum('bhtk,bhkv->bhtv', q * jnp.exp(b), state)
    diff = b[:, :, :, None, :] - b[:, :, None, :, :]
    causal = (jnp.arange(c)[:, None] >= jnp.arange(c)[None, :])[None, None, :, :, None]
    decay = jnp.where(causal, jnp.exp(jnp.where(causal, diff, 0.0)), 0.0)
    scores = jnp.einsum('bhtk,bhtsk,bhsk->bhts', q, decay, k)
    o_intra = jnp.einsum('bhts,bhsv->bhtv', scores, v)
    b_last = b[:, :, -1, :]
    k_dec = k * jnp.exp(b_last[:, :, None, :] - b)
    new_state = jnp.exp(b_last)[..., None] * state + jnp.einsum('bhsk,bhsv->bhkv', k_dec, v)
    return new_state, o_inter + o_intra

def hgrn2(q, f_logit, i, g, lb, out_gain):
    bsz, L, _ = q.shape
    lb = lb.astype(jnp.float32)
    fl = f_logit.astype(jnp.float32)
    f = lb + (1.0 - lb) * jax.nn.sigmoid(fl)
    log_f = jnp.log(jnp.maximum(f, LOG_FLOOR))
    k = (1.0 - lb) * jax.nn.sigmoid(-fl)
    pad = CHUNK - N_META
    def prep(t, d):
        t = jnp.pad(t.astype(jnp.float32), ((0, 0), (pad, 0), (0, 0)))
        n = t.shape[1] // CHUNK
        return t.reshape(bsz, n, CHUNK, HGRN_HEADS, d).transpose(1, 0, 3, 2, 4)
    xs = (prep(q, HGRN_EXPAND), prep(k, HGRN_EXPAND), prep(i, HGRN_HEAD_V), prep(log_f, HGRN_EXPAND))
    state0 = jnp.zeros((bsz, HGRN_HEADS, HGRN_EXPAND, HGRN_HEAD_V), jnp.float32)
    _, o = lax.scan(_hgrn2_chunk_step, state0, xs)
    o = o.transpose(1, 0, 3, 2, 4).reshape(bsz, -1, HGRN_HEADS, HGRN_HEAD_V)[:, pad:]
    o = o * lax.rsqrt(jnp.mean(o * o, axis=-1, keepdims=True) + EPS)
    o = o.reshape(bsz, L, HGRN_WIDTH) * out_gain.astype(jnp.float32)
    return o * jax.nn.sigmoid(g.astype(jnp.float32))

def multiscale_pool(v, proj, scale):
    bsz, L, _ = v.shape
    vg = v.astype(jnp.float32).reshape(bsz, L, POOL_GROUPS, POOL_GROUP_DIM)
    cs0 = jnp.pad(jnp.cumsum(vg, axis=1), ((0, 0), (1, 0), (0, 0), (0, 0)))
    t1 = jnp.arange(1, L + 1)
    outs = []
    for gi, w in enumerate(POOL_WINDOWS):
        hi = cs0[:, 1:, gi]
        lo = jnp.pad(cs0[:, :L + 1 - w, gi], ((0, 0), (w - 1, 0), (0, 0)))
        cnt = jnp.minimum(t1, w).astype(jnp.float32)[None, :, None]
        outs.append((hi - lo) / cnt - vg[:, :, gi])
    pooled = jnp.stack(outs, axis=2)
    y = jnp.einsum('blgc,gcd->blgd', pooled, proj.astype(jnp.float32))
    return y.reshape(bsz, L, POOL_WIDTH) * scale.astype(jnp.float32)

def causal_dwconv(x, w, b):
    L = x.shape[1]
    xp = jnp.pad(x, ((0, 0), (CONV_WIDTH - 1, 0), (0, 0)))
    y = b
    for j in range(CONV_WIDTH):
        y = y + xp[:, j:j + L] * w[j]
    return y

def second_inputs(seed: int = 0) -> dict:
    key = jax.random.key(seed)
    ks = jax.random.split(key, 24)
    nrm = lambda k, shape, s: jax.random.normal(k, shape, jnp.float32) * s
    gain = lambda k, shape: 1.0 + nrm(k, shape, 0.05)
    return {
        "x": nrm(ks[0], (BATCH, SEQ, D_MODEL), 1.0),
        "meta_tokens": nrm(ks[1], (N_META, D_MODEL), 1.0),
        "mix_norm_pre": gain(ks[2], (DEPTH_2, D_MODEL)),
        "mix_norm_post": gain(ks[3], (DEPTH_2, D_MODEL)),
        "w_in": nrm(ks[4], (DEPTH_2, D_MODEL, IN_COLS), D_MODEL ** -0.5),
        "hgrn_lower_bounds": nrm(ks[5], (DEPTH_2, HGRN_KDIM), 0.5),
        "hgrn_out_norm": gain(ks[6], (DEPTH_2, HGRN_WIDTH)),
        "w_branch_hgrn": nrm(ks[7], (DEPTH_2, HGRN_WIDTH, D_MODEL), HGRN_WIDTH ** -0.5),
        "pool_proj": nrm(ks[8], (DEPTH_2, POOL_GROUPS, POOL_GROUP_DIM, POOL_GROUP_DIM), POOL_GROUP_DIM ** -0.5),
        "pool_scale": gain(ks[9], (DEPTH_2, POOL_WIDTH)),
        "w_branch_pool": nrm(ks[10], (DEPTH_2, POOL_WIDTH, D_MODEL), POOL_WIDTH ** -0.5),
        "w_out": nrm(ks[11], (DEPTH_2, D_MODEL, D_MODEL), D_MODEL ** -0.5),
        "ffn_norm_pre": gain(ks[12], (DEPTH_2, D_MODEL)),
        "ffn_norm_post": gain(ks[13], (DEPTH_2, D_MODEL)),
        "ffn_w_gate": nrm(ks[14], (DEPTH_2, D_MODEL, D_FF_2), D_MODEL ** -0.5),
        "ffn_w_up": nrm(ks[15], (DEPTH_2, D_MODEL, D_FF_2), D_MODEL ** -0.5),
        "ffn_conv_w": nrm(ks[16], (DEPTH_2, CONV_WIDTH, D_FF_2), CONV_WIDTH ** -0.5),
        "ffn_conv_b": nrm(ks[17], (DEPTH_2, D_FF_2), 0.02),
        "ffn_w_down": nrm(ks[18], (DEPTH_2, D_FF_2, D_MODEL), D_FF_2 ** -0.5),
    }

def second_block(x, meta_tokens, mix_norm_pre, mix_norm_post, w_in, hgrn_lower_bounds, hgrn_out_norm,
              w_branch_hgrn, pool_proj, pool_scale, w_branch_pool, w_out, ffn_norm_pre, ffn_norm_post,
              ffn_w_gate, ffn_w_up, ffn_conv_w, ffn_conv_b, ffn_w_down):
    bsz = x.shape[0]
    meta = jnp.broadcast_to(meta_tokens[None].astype(x.dtype), (bsz, N_META, D_MODEL))
    h = jnp.concatenate([meta, x], axis=1)
    gam = jax.nn.softmax(hgrn_lower_bounds.astype(jnp.float32), axis=0)
    lbs = jnp.clip(jnp.cumsum(gam, axis=0) - gam[0], 0.0, 1.0)
    cuts = list(np.cumsum(SPLITS)[:-1])
    for l in range(DEPTH_2):
        u = rmsnorm(h, mix_norm_pre[l])
        proj = u @ w_in[l]
        q, f_logit, i_in, g_out, v_pool, gate_a, gate_b = jnp.split(proj, cuts, axis=-1)
        a = hgrn2(q, f_logit, i_in, g_out, lbs[l], hgrn_out_norm[l])
        p = multiscale_pool(v_pool, pool_proj[l], pool_scale[l])
        z = (jax.nn.sigmoid(gate_a.astype(jnp.float32)) * (a @ w_branch_hgrn[l])
             + jax.nn.sigmoid(gate_b.astype(jnp.float32)) * (p @ w_branch_pool[l]))
        h = h + rmsnorm(z @ w_out[l], mix_norm_post[l])
        u = rmsnorm(h, ffn_norm_pre[l])
        gt = causal_dwconv(u @ ffn_w_gate[l], ffn_conv_w[l], ffn_conv_b[l])
        y = (jax.nn.gelu(gt, approximate=True) * (u @ ffn_w_up[l])) @ ffn_w_down[l]
        h = h + rmsnorm(y, ffn_norm_post[l])
    return h[:, N_META:]


def setup_inputs(seed=0):
    out = dict(first_inputs(seed))
    for name, value in second_inputs(seed + 1).items():
        if name != "x":
            out[name + "_2"] = value
    return out


def reference(
    x, mem, mem_norm_gain, norm_gains, ml_w_in, ml_b_gate, ml_head_gain, ml_w_out, sb_w_qkv,
    sb_w_out, xa_w_q, xa_w_kv, xa_w_o, ffn_w_gate_up, ffn_w_down, meta_tokens_2, mix_norm_pre_2,
    mix_norm_post_2, w_in_2, hgrn_lower_bounds_2, hgrn_out_norm_2, w_branch_hgrn_2, pool_proj_2,
    pool_scale_2, w_branch_pool_2, w_out_2, ffn_norm_pre_2, ffn_norm_post_2, ffn_w_gate_2,
    ffn_w_up_2, ffn_conv_w_2, ffn_conv_b_2, ffn_w_down_2,
):
    x = first_block(
        x, mem, mem_norm_gain, norm_gains, ml_w_in, ml_b_gate, ml_head_gain, ml_w_out, sb_w_qkv,
        sb_w_out, xa_w_q, xa_w_kv, xa_w_o, ffn_w_gate_up, ffn_w_down,
    )
    return second_block(
        x, meta_tokens_2, mix_norm_pre_2, mix_norm_post_2, w_in_2, hgrn_lower_bounds_2,
        hgrn_out_norm_2, w_branch_hgrn_2, pool_proj_2, pool_scale_2, w_branch_pool_2, w_out_2,
        ffn_norm_pre_2, ffn_norm_post_2, ffn_w_gate_2, ffn_w_up_2, ffn_conv_w_2, ffn_conv_b_2,
        ffn_w_down_2,
    )


_drawn_inputs = setup_inputs


def setup_inputs(seed=0):
    import zlib

    import numpy as np

    out = dict(_drawn_inputs(seed))
    spreads = {}
    factors = {'ml_head_gain': 2.762,
     'meta_tokens_2': 2.862,
     'mix_norm_post_2': 3.044,
     'hgrn_out_norm_2': 5.481,
     'pool_scale_2': 4.024,
     'ffn_norm_post_2': 3.34,
     'ffn_conv_b_2': 8.0}
    for name, (base, spread) in spreads.items():
        noise = np.random.default_rng([zlib.crc32(name.encode()), seed]).standard_normal(out[name].shape)
        drawn = base * np.exp(spread * noise) if base else spread * noise
        out[name] = __import__('jax').numpy.asarray(drawn.astype(out[name].dtype))
    for name, factor in factors.items():
        out[name] = (out[name] * factor).astype(out[name].dtype)
    return out
```

```python
from contextlib import ExitStack, contextmanager

import numpy as np

import concourse.bass as bass
from concourse import mybir
from concourse.alu_op_type import AluOpType as ALU

F32 = mybir.dt.float32
F32R = mybir.dt.float32r
I32 = mybir.dt.int32
ACT = mybir.ActivationFunctionType
AX = mybir.AxisListType

P = 128
D = 1024
DT = D // P
S = 512
META = 16
N = S + META
HALF = N // 2
MEM = 256
FF = 2816
FT = FF // P
EPS = 1e-6

ML_H, ML_DK, ML_DV = 4, 128, 256
GATE_CAP = 15.0
SB_H, SB_D = 16, 64
XA_H, XA_D = 4, 256
HG_H = 4
CONV = 3
WINDOWS = (2, 4, 8, 16)

UT = 8
RING = 4
LAND = 2
LEAD = 3
DONE0 = 1
DOWN_UNITS = -(-FT // UT)

VEC = {}
for _l in range(2):
    for _n in range(6):
        VEC[f"g{_l}{_n}"] = len(VEC)
for _n in ("mem", "ml_head", "mix_pre", "mix_post", "ffn_pre", "ffn_post"):
    VEC[_n] = len(VEC)
HALF_VEC = {"hg_out": 0, "pool_scale": 1, "lower": 2}


class Tok:

    def __init__(self, counter, value, step=0, i=None):
        self.counter, self.value, self.step, self.i = counter, value, step, i

    def wait(self, eng):
        v = self.value if self.i is None or not self.step else self.i * self.step + self.value
        eng.wait_ge(self.counter.sem, v)


def wait_all(eng, toks):
    top = {}
    for t in toks:
        if t is not None:
            key = (id(t.counter), t.i is None)
            if key not in top or top[key].value < t.value:
                top[key] = t
    for t in top.values():
        t.wait(eng)


class Counter:

    def __init__(self, sem):
        self.sem, self.n, self.step, self.i = sem, 0, 0, None

    def add(self, ins):
        if ins is not None:
            ins.then_inc(self.sem, 1)
        self.n += 1
        return Tok(self, self.n, self.step, self.i)


class Program:
    def __init__(self, nc, ctx, n_units):
        self.nc, self.ctx = nc, ctx
        self.pe, self.act, self.dve, self.pool, self.sp = nc.tensor, nc.scalar, nc.vector, nc.gpsimd, nc.sync
        sem = lambda name: ctx.enter_context(nc.semaphore(name))
        self.c_pe, self.c_act = Counter(sem("pe_done")), Counter(sem("act_done"))
        self.c_dve, self.c_pool = Counter(sem("dve_done")), Counter(sem("pool_done"))
        self.counters = [self.c_pe, self.c_act, self.c_dve, self.c_pool]
        self.landed = [sem(f"unit_landed{j}") for j in range(LAND)]
        self.hi_done, self.lo_done = sem("unit_hi_done"), sem("unit_lo_done")
        self.unit_done = sem("unit_multiplied")
        self.dry = False
        self.n_units, self.unit = n_units, 0

    def op(self, eng, counter, after, make):
        if self.dry:
            return counter.add(None)
        wait_all(eng, after)
        return counter.add(make(eng))

    def P(self, after, make):
        return self.op(self.pe, self.c_pe, after, make)

    def A(self, after, make):
        return self.op(self.act, self.c_act, after, make)

    def V(self, after, make):
        return self.op(self.dve, self.c_dve, after, make)

    def G(self, after, make):
        return self.op(self.pool, self.c_pool, after, make)

    def mms(self, after, out, pairs, start=True, stop=True):
        if self.dry:
            return self.c_pe.add(None)
        wait_all(self.pe, after)
        for n, (a, b) in enumerate(pairs):
            ins = self.pe.matmul(out, a, b, start=start and n == 0, stop=stop and n == len(pairs) - 1,
                                 skip_group_check=not (start and stop))
        return self.c_pe.add(ins)

    def loop(self, n, body, engines=None):
        counts = [c.n for c in self.counters]
        kept = {}
        self.dry, unit = True, self.unit
        body(0, lambda name: None, lambda name, t: kept.__setitem__(name, (t.counter, t.value)))
        self.dry = False
        steps = [c.n - n0 for c, n0 in zip(self.counters, counts)]
        units = self.unit - unit
        self.unit = unit
        step_of = dict(zip([id(c) for c in self.counters], steps))
        for c, n0, st in zip(self.counters, counts, steps):
            c.n, c.step = n0, st
        with self.nc.Fori(0, n) as i:
            for c in self.counters:
                c.i = i
            self.unit_i, self.unit_step = i, units
            prev = lambda name: Tok(kept[name][0], kept[name][1] - step_of[id(kept[name][0])],
                                    step_of[id(kept[name][0])], i)
            body(i, prev, lambda name, t: None)
        for c, n0, st in zip(self.counters, counts, steps):
            assert c.n == n0 + st
            c.n, c.step, c.i = n0 + st * n, 0, None
        self.unit, self.unit_i, self.unit_step = unit + units * n, None, 0
        return {k: Tok(c, v + step_of[id(c)] * (n - 1)) for k, (c, v) in kept.items()}

    def now(self, counter):
        return Tok(counter, counter.n)

    def all_done(self):
        return [self.now(c) for c in self.counters]

    unit_i, unit_step = None, 0

    def unit_wait(self, eng, sem, u, each=1):
        v = (u + 1) * each
        if self.unit_i is not None:
            v = self.unit_i * (self.unit_step * each) + v
        eng.wait_ge(sem, v)


def dslice(i, step, j, size):
    if isinstance(i, int):
        return slice(i * step + j, i * step + j + size)
    return bass.ds(i * step + j, size)


class Map:

    def __init__(self, nc):
        self.nc = nc
        self.at = -(-nc.sbuf_base // 64) * 64

    def place(self, name, shape, dt=F32, over=None):
        size = 4 * int(np.prod(shape[1:]))
        at = self.at if over is None else over
        if over is None:
            self.at += -(-size // 64) * 64
            assert self.at <= self.nc.sbuf_usable_end, (name, self.at)
        return self.nc.alloc_sbuf_tensor_at(name, shape, dt, offset=at)


CONST = {}
_at = 0
for _n, _w in (("ident", P), ("ones", P), ("neg_ones", P), ("neg_suffix", P), ("causal", P), ("strict", P),
               ("neg_fill", P), ("sel", ML_H * P), ("reset", HG_H * P), ("reset_meta", HG_H * META),
               ("inv_count", 4 * META)):
    CONST[_n] = (_at, _at + _w)
    _at += _w
CONST_ALL = _at
CONST_W = CONST["sel"][0]
LEVELS = (2, 4, 8, 16, 32, 64, 128)


def shape_constants():
    c = np.zeros((P, CONST_ALL), np.float32)
    s, t = np.arange(P)[:, None], np.arange(P)[None, :]
    put = lambda name, v: c.__setitem__((slice(None), slice(*CONST[name])), v)
    put("ident", s == t)
    put("ones", 1.0)
    put("neg_ones", -1.0)
    put("neg_suffix", np.where(s >= t, -1.0, 0.0))
    put("causal", t >= s)
    put("strict", t > s)
    put("neg_fill", np.where(t > s, 0.0, -1e30))
    put("sel", np.arange(ML_H * P)[None, :] // P == s)
    put("reset", np.arange(HG_H * P)[None, :] % P != 0)
    put("reset_meta", np.arange(HG_H * META)[None, :] % META != 0)
    put("inv_count", np.concatenate([1.0 / np.minimum(np.arange(META) + 1, w) for w in WINDOWS])[None, :])
    m = np.zeros((P, len(LEVELS), P), np.int32)
    for n, b in enumerate(LEVELS):
        m[:, n, :] = (s // b == t // b) & (s % b < b // 2) & (t % b >= b // 2)
    return c, m.reshape(P, -1)


def build(nc, units, xT, memT, vecs_d, gates_w, gates_b, pool_w, conv_d, consts_d, masks_d, out):
    n_units = units.shape[0]
    assert n_units % RING == 0
    ctx = ExitStack()
    with ctx:
        pr = Program(nc, ctx, n_units)
        pe, act, dve, pool, sp = pr.pe, pr.act, pr.dve, pr.pool, pr.sp
        A, V, T, mms = pr.A, pr.V, pr.P, pr.mms
        m = Map(nc)
        sb = m.place
        sem = lambda name: ctx.enter_context(nc.semaphore(name))

        x = sb("x", [P, DT, N])
        y_wide = m.at
        u_hi = sb("u_hi", [P, DT, N], F32R)
        u_lo = sb("u_lo", [P, DT, N], F32R)
        y_ffn = sb("y_ffn", [P, DT, N], F32, over=y_wide)[:, :, META:]
        w_land = sb("w_land", [P, LAND, UT * P])
        w_hi = sb("w_hi", [P, RING, UT * P], F32R)
        w_lo = sb("w_lo", [P, RING, UT * P], F32R)
        rstd = sb("rstd", [P, N])
        rstd_y = sb("rstd_y", [P, N])
        sq = sb("sq", [P, 2, N])
        acc = sb("acc", [P, N])
        NVEC = len(VEC) * DT + 4 * len(HALF_VEC)
        vecs = sb("vecs", [P, NVEC])
        consts = sb("consts", [P, CONST_W])
        conv = sb("conv", [P, FT, CONV + 1])
        eps = sb("eps", [P, 1])
        uT = sb("uT", [P, 4, ML_H])
        zrow = sb("zrow", [P, 1])
        small = sb("small", [P, 4, 4])
        arena_at = m.at
        ARENA = 2 * FT * S + 4 * N
        arena = sb("arena", [P, ARENA])
        hid_hi = sb("hid_hi", [P, FT, S], F32R, over=arena_at)
        hid_lo = sb("hid_lo", [P, FT, S], F32R, over=arena_at + 4 * FT * S)
        tmp_at = 2 * FT * S
        ps = ctx.enter_context(nc.psum_tensor("ps", [P, 8, 512], F32))

        def area(at, *shape):
            size = int(np.prod(shape))
            assert at + size <= ARENA
            v = arena[:, at:at + size]
            if len(shape) == 2:
                return v.rearrange("p (a b) -> p a b", b=shape[1])
            if len(shape) == 3:
                return v.rearrange("p (a b c) -> p a b c", b=shape[1], c=shape[2])
            return v

        tmp = area(tmp_at, 4, N)
        const = lambda name: consts[:, slice(*CONST[name])]
        ident, ones = const("ident"), const("ones")
        col = lambda name, k: vecs[:, VEC[name] * DT + k:VEC[name] * DT + k + 1]
        def half_col(name, k):
            c = len(VEC) * DT + 4 * HALF_VEC[name] + k
            return vecs[:, c:c + 1]
        XS = slice(META, N)
        MS = slice(0, MEM)

        s_small, s_x, s_mem, s_out = sem("small_loaded"), sem("x_loaded"), sem("mem_loaded"), sem("out_stored")
        c_small, c_xl, c_meml = Counter(s_small), Counter(s_x), Counter(s_mem)
        units_r = units
        land_at = lambda j: w_land[:, j % LAND, :]
        sp.dma_start(x[:, :, :], xT.rearrange("(k p) n -> p k n", p=P)).then_inc(s_x, 16)
        sp.dma_start(consts[:, :], consts_d[:, 0:CONST_W]).then_inc(s_small, 16)
        sp.dma_start(vecs[:, :], vecs_d).then_inc(s_small, 16)
        sp.dma_start(conv[:, :, :], conv_d.rearrange("p (k n) -> p k n", k=FT)).then_inc(s_small, 16)
        loaded_first = Tok(c_small, 48)
        x_in = Tok(c_xl, 16)
        for j in range(LAND):
            sp.dma_start(land_at(j), units[j, :, :]).then_inc(pr.landed[j], 16)
        with sp.Fori(1, n_units // LAND) as g:
            for j in range(LAND):
                sp.wait_ge(pr.lo_done, g * LAND + (j + 1 - LAND))
                sp.dma_start(land_at(j), units[bass.ds(g * LAND + j, 1), :, :].rearrange("o p n -> (o p) n"))\
                  .then_inc(pr.landed[j], 16)

        def split_lo(g, j, first):
            pool.wait_ge(pr.hi_done, g * RING + (j + 1))
            if not first:
                pool.wait_ge(pr.unit_done, g * RING + (j + 1 - RING + DONE0))
            pool.tensor_tensor(w_lo[:, j, :], land_at(j), w_hi[:, j, :].bitcast(F32), ALU.subtract)\
                .then_inc(pr.lo_done, 1)

        for j in range(RING):
            split_lo(0, j, True)
        with pool.Fori(1, n_units // RING) as g:
            for j in range(RING):
                split_lo(g, j, False)

        def split_hi(u):
            if pr.dry or (pr.unit_i is None and u >= n_units):
                return
            j = u % RING
            gi = None if pr.unit_i is None else pr.unit_i
            assert pr.unit_step % RING == 0 or gi is None
            v = 16 * (u // LAND + 1)
            act.wait_ge(pr.landed[j % LAND], v if gi is None else gi * (16 * (pr.unit_step // LAND)) + v)
            if u >= RING or (gi is not None and u >= RING - 1):
                pr.unit_wait(act, pr.unit_done, u - RING + DONE0)
            act.activation(w_hi[:, j, :], land_at(j), ACT.Copy).then_inc(pr.hi_done, 1)

        for u in range(LEAD):
            split_hi(u)
        t_eps = V([], lambda e: e.memset(eps[:, :], EPS))

        c_unit = Counter(pr.unit_done)
        pe.sem_inc(pr.unit_done, DONE0)

        def linear(n_iter, outs, n_u, rhs, parts, evac, after, depth, layout=None):
            wait_all(pe, after)
            if layout is None:
                layout = [(parts, [o * len(parts) + b for b in range(len(parts))]) for o in range(depth)]

            def body(i, prev, keep):
                free = {}
                begun = -1
                for o, tiles in enumerate(outs):
                    parts_o, banks = layout[o % depth]
                    back = o - depth
                    t_free = free[back] if back >= 0 else prev(f"free{back + len(outs)}") if len(outs) >= depth else None
                    if not pr.dry:
                        if t_free is not None:
                            t_free.wait(pe)
                        for n, (uj, q, k) in enumerate(tiles):
                            u = pr.unit + uj
                            if uj > begun:
                                pr.unit_wait(pe, pr.lo_done, u)
                                begun = uj
                            hi = w_hi[:, u % RING, q * P:(q + 1) * P]
                            lo = w_lo[:, u % RING, q * P:(q + 1) * P]
                            for h, (w, which) in enumerate(((hi, 0), (hi, 1), (lo, 0))):
                                for (c0, c1), bank in zip(parts_o, banks):
                                    ins = pe.matmul(ps[:, bank, 0:c1 - c0], w, rhs(k, c0, c1)[which],
                                                    start=n == 0 and h == 0, stop=n == len(tiles) - 1 and h == 2)
                            more = any(t[0] == uj for t in tiles[n + 1:]) or any(t[0] == uj for ts in outs[o + 1:] for t in ts)
                            if not more:
                                ins.then_inc(pr.unit_done, 1)
                    last_u = tiles[-1][0]
                    for uj in sorted({t[0] for t in tiles}):
                        if not any(t[0] == uj for ts in outs[o + 1:] for t in ts):
                            split_hi(pr.unit + uj + LEAD)
                    ready = Tok(c_unit, pr.unit + last_u + 1 + DONE0, pr.unit_step, pr.unit_i)
                    free[o] = evac(i, o, banks, ready, prev, keep)
                    keep(f"free{o}", free[o])
                keep("evac", free[len(outs) - 1])
                pr.unit += n_u

            last = pr.unit + n_iter * n_u >= n_units
            if last:
                n_iter -= 1
            got = pr.loop(n_iter, body)
            if last:
                seen = {}
                body(n_iter, lambda name: got.get(name), lambda name, t: seen.__setitem__(name, t))
                got = seen
            return got

        square_outs = [[(j, q, q) for q in range(UT)] for j in range(RING)]

        def rsqrt_mean(ss_banks, parts, width, dst, after):
            for (c0, c1), b in zip(parts, ss_banks):
                t = A(after + [t_eps], lambda e: e.activation(dst[:, c0:c1], ps[:, b, 0:c1 - c0], ACT.Ln,
                                                    bias=eps[:, 0:1], scale=1.0 / width))
            a, z = parts[0][0], parts[-1][1]
            return A([t], lambda e: e.activation(dst[:, a:z], dst[:, a:z], ACT.Exp, scale=-0.5))

        ONE = [(META, N)]
        TWO = [(0, HALF), (HALF, N)]

        def prenorm(src, gain, parts, after, each=None):
            a, z = parts[0][0], parts[-1][1]
            t_sq, t_mm, t_lo = [], [], None
            for k in range(DT):
                t_x = each(k) if each else None
                first = after if k == 0 else []
                t_sq.append(A(first + [t_x, t_mm[k - 2] if k >= 2 else None],
                              lambda e: e.activation(sq[:, k % 2, a:z], src[:, k, a:z], ACT.Square)))
                t_hi = A([], lambda e: e.activation(u_hi[:, k, a:z], src[:, k, a:z], ACT.Copy, scale=col(gain, k)))
                t_lo = V([t_hi], lambda e: e.scalar_tensor_tensor(u_lo[:, k, a:z], src[:, k, a:z], col(gain, k),
                                                                 u_hi[:, k, a:z].bitcast(F32), ALU.mult, ALU.subtract))
                for b, (c0, c1) in enumerate(parts):
                    t = mms(first + [t_sq[k]], ps[:, 6 + b, 0:c1 - c0], [(ones, sq[:, k % 2, c0:c1])],
                            start=k == 0, stop=k == DT - 1)
                t_mm.append(t)
            t_r = rsqrt_mean([6, 7], parts, D, rstd, [t_mm[-1]])
            return [t_lo, t_r]

        def u_rhs(k, c0, c1):
            return u_hi[:, k, c0:c1], u_lo[:, k, c0:c1]

        def hid_rhs(k, c0, c1):
            return hid_hi[:, k, c0:c1], hid_lo[:, k, c0:c1]

        def y_evac(y, parts):
            a, z = parts[0][0], parts[-1][1]

            def evac(i, o, banks, ready, prev, keep):
                k = dslice(i, y_evac.per, o, 1)
                for (c0, c1), b in zip(parts, banks):
                    t = A([ready], lambda e: e.activation(y[:, k, c0 - a:c1 - a], ps[:, b:b + 1, 0:c1 - c0], ACT.Copy))
                added = y_evac.added[o - 2] if o >= 2 else prev(f"added{o - 2 + y_evac.per}")
                t2 = V([t, added], lambda e: e.tensor_tensor(sq[:, o % 2:o % 2 + 1, 0:z - a], y[:, k, :], y[:, k, :], ALU.mult))
                y_evac.added[o] = V([t2], lambda e: e.tensor_tensor(acc[:, 0:z - a], acc[:, 0:z - a], sq[:, o % 2, 0:z - a], ALU.add))
                keep(f"added{o}", y_evac.added[o])
                return t
            return evac

        def project_out(y, rhs, after, n_iter=2, outs=square_outs, n_u=RING, parts=ONE):
            t = V(after, lambda e: e.memset(acc[:, :], 0.0))
            y_evac.per, y_evac.added = len(outs), {}
            a = parts[0][0]
            cols = parts if rhs is not hid_rhs else [(0, S)]
            linear(n_iter, outs, n_u, rhs, cols, y_evac(y, cols), after + [t], 4)
            for b, (c0, c1) in enumerate(parts):
                t = mms([pr.now(pr.c_dve)], ps[:, 5 + b, 0:c1 - c0], [(ones, acc[:, c0 - a:c1 - a])])
            return [rsqrt_mean([5, 6], parts, D, rstd_y, [t])]

        def add_tile(y, gain, cols=XS):
            def each(k):
                t = V([], lambda e: e.scalar_tensor_tensor(y[:, k, :], y[:, k, :], col(gain, k), rstd_y[:, cols], ALU.mult, ALU.mult))
                return V([t], lambda e: e.tensor_tensor(x[:, k, cols], x[:, k, cols], y[:, k, :], ALU.add))
            return each

        def scaled_to(dst, per, part=ONE, scale=None):
            def evac(i, o, banks, ready, prev, keep):
                for (c0, c1), b in zip(part, banks):
                    w0 = c0 - part[0][0]
                    t = V([ready], lambda e: e.tensor_tensor(dst[:, dslice(i, per, o, 1), w0:w0 + c1 - c0],
                                                             ps[:, b:b + 1, 0:c1 - c0], rstd[:, c0:c1].rearrange("p (o n) -> p o n", o=1), ALU.mult))
                return t
            return evac

        def add_after(after, y, gain, cols=XS):
            add = add_tile(y, gain, cols)
            def each(k):
                for t in (after if k == 0 else []):
                    t.wait(dve)
                return add(k)
            return each

        def table(name):
            if not pr.dry:
                act.preload_act_table_set(name)

        def transpose_tiles(after, src, dst, n_tok_tiles, tiles, size=P, first=0):
            t_cp = [None, None]
            for b in range(n_tok_tiles):
                for half in range(-(-tiles // 4)):
                    bank = 6 + (b * -(-tiles // 4) + half) % 2
                    ks = range(4 * half, min(4 * half + 4, tiles))
                    for t in after:
                        t.wait(pe)
                    if t_cp[bank - 6] is not None:
                        t_cp[bank - 6].wait(pe)
                    for k in ks:
                        ins = pe.transpose(ps[0:size, bank, (k % 4) * P:(k % 4) * P + P],
                                           src[:, k, first + b * size:first + (b + 1) * size], ident)
                    t = pr.c_pe.add(ins)
                    after = []
                    w = len(ks) * P
                    t_cp[bank - 6] = (A if bank == 6 else V)([t], lambda e: (e.activation(dst[0:size, b, ks[0] * P:ks[0] * P + w], ps[0:size, bank, 0:w], ACT.Copy)
                                                           if bank == 6 else e.tensor_copy(dst[0:size, b, ks[0] * P:ks[0] * P + w], ps[0:size, bank, 0:w])))
            return [t for t in t_cp if t is not None]

        def mlstm():
            t_pre = prenorm(x, "g00", ONE, [x_in, loaded_first])
            qT, kT, vT, og = area(0, 4, S), area(2048, 4, S), area(4096, 8, S), area(8192, 8, S)
            v_tok = area(12288, 4, D)
            M_bc, floor_bc = area(16384, 4, S), area(18432, 4, S)
            pT = area(20480, 4, S)
            gw = area(20480, DT, 36)
            rows = tmp
            gb = area(20480 + DT * 36, 4)
            sel_all = area(20480 + DT * 36 + 4, ML_H * P)

            t0 = V([], lambda e: e.memset(gw, 0.0))
            if not pr.dry:
                t0.wait(act)
                act.dma_start(gw[:, :, 0:ML_H], gates_w.rearrange("(k p) n -> p k n", p=P)[:, :, 0:ML_H]).then_inc(s_small, 16)
                act.dma_start(gw[:, :, 32:36], gates_w.rearrange("(k p) n -> p k n", p=P)[:, :, ML_H:]).then_inc(s_small, 16)
                act.dma_start(sel_all, consts_d[:, slice(*CONST["sel"])]).then_inc(s_small, 16)
                act.dma_start(gb[0:ML_H, 0:1], gates_b[0:ML_H, :]).then_inc(s_small, 16)
                act.dma_start(gb[0:ML_H, 1:2], gates_b[ML_H:2 * ML_H, :]).then_inc(s_small, 16)
            gates_in = Tok(c_small, 48 + 80)

            linear(2, square_outs, RING, u_rhs, ONE, scaled_to(area(0, 8, S), 4), t_pre, 4)
            linear(2, square_outs, RING, u_rhs, ONE, scaled_to(vT, 4), [pr.now(pr.c_dve)], 4)
            to_og = scaled_to(og, 4)
            def og_evac(i, o, banks, ready, prev, keep):
                t = to_og(i, o, banks, ready, prev, keep)
                v = og[:, dslice(i, 4, o, 1), :]
                A([t], lambda e: e.activation(v, v, ACT.Sigmoid))
                return t
            linear(2, square_outs, RING, u_rhs, ONE, og_evac, [pr.now(pr.c_dve)], 4)
            pairs = [(gw[:, k, :], u[:, k, XS].bitcast(F32)) for k in range(DT) for u in (u_hi, u_lo)]
            t_g = mms([gates_in], ps[0:36, 4, :], pairs)
            t = V([t_g], lambda e: e.tensor_tensor(rows[0:4, 0, 0:S], ps[0:4, 4, :], rstd[0:4, XS], ALU.mult))
            t = V([t], lambda e: e.tensor_tensor(rows[32:36, 1, 0:S], ps[32:36, 4, :], rstd[32:36, XS], ALU.mult))
            t = A([t, gates_in], lambda e: e.activation(rows[0:4, 1, 0:S], rows[32:36, 1, 0:S], ACT.Copy))
            ig, lf = rows[0:4, 0, 0:S], rows[0:4, 1, 0:S]
            w1, w2 = rows[0:4, 2, 0:S], rows[0:4, 3, 0:S]
            for n, r in ((0, ig), (1, lf)):
                t = V([t], lambda e: e.tensor_scalar(r, r, gb[0:4, n:n + 1], 1.0 / GATE_CAP, ALU.add, ALU.mult))
                t = A([t], lambda e: e.activation(r, r, ACT.Tanh))
                t = V([t], lambda e: e.tensor_scalar(r, r, GATE_CAP, None, ALU.mult))
            t = A([t], lambda e: e.activation(w1, lf, ACT.Abs))
            t = A([t], lambda e: e.activation(w1, w1, ACT.Exp, scale=-1.0))
            t = A([t], lambda e: e.activation(w1, w1, ACT.Ln, bias=1.0))
            t = V([t], lambda e: e.scalar_tensor_tensor(lf, lf, 0.0, w1, ALU.min, ALU.subtract))
            t = V([t], lambda e: e.tensor_tensor_scan(w2, ones_row(4), lf, 0.0, ALU.mult, ALU.add))
            t = V([t], lambda e: e.tensor_tensor(ig, ig, w2, ALU.subtract))
            t = V([t], lambda e: e.tensor_tensor_scan(w1, ig, ig, 0.0, ALU.max, ALU.max))
            t_F = V([t], lambda e: e.tensor_tensor(w2, w2, w1, ALU.add))
            t_m = A([t_F], lambda e: e.activation(w2, w2, ACT.Exp, scale=-1.0))
            t_bc = None
            for h in range(ML_H):
                sel = sel_all[0:4, h * P:(h + 1) * P]
                t1 = mms([t_F, t_m], ps[:, 4, :], [(sel, w1)])
                t1 = V([t1], lambda e: e.tensor_copy(M_bc[:, h, :], ps[:, 4, :]))
                t2 = mms([t1, t_bc], ps[:, 5, :], [(sel, w2)])
                t_bc = A([t2, t1], lambda e: e.activation(floor_bc[:, h, :], ps[:, 5, :], ACT.Copy))
            for b in range(4):
                t2 = T([t_bc], lambda e: e.transpose(ps[:, 4, 4 * b:4 * b + 4], rows[0:4, 0, b * P:(b + 1) * P], ident[0:4, 0:4]))
            t_u = V([t2], lambda e: e.tensor_copy(uT[:, :, :], ps[:, 4, 0:16].rearrange("p (b h) -> p b h", h=4)))
            t_v = transpose_tiles([t_u], vT, v_tok, 4, DT)
            k_h, v_h, u_h = area(4096, S), area(4608, 4, ML_DV), area(5632, 4)
            hT = area(5700, 2, S)
            den, r_h = area(6724, S), area(7236, S)
            wexp = area(7748, S)[:, 0:444] if False else tmp[:, 0, 0:S]

            def head(h, prev, keep):
                one = lambda v: v.rearrange("p (o n) -> p o n", o=1)
                t_k = V([prev("pv")], lambda e: e.tensor_scalar(one(k_h), kT[:, dslice(h, 1, 0, 1), :], ML_DK ** -0.5, None, ALU.mult))
                t_vh = A([prev("pv")], lambda e: e.activation(v_h, v_tok[:, :, dslice(h, ML_DV, 0, ML_DV)], ACT.Copy))
                t_uh = V([], lambda e: e.tensor_copy(u_h, uT[:, :, dslice(h, 1, 0, 1)].rearrange("p b o -> p (b o)")))
                t_s, t_p = [], []
                for b in range(4):
                    w = S - b * P
                    sl = slice(b * P, S)
                    t_s.append(mms([t_k, prev("pv"), prev(f"p{b}")], ps[:, b, 0:w],
                                   [(k_h[:, b * P:(b + 1) * P], qT[:, dslice(h, 1, 0, 1), sl])]))
                    t = V([t_uh, t_p[-1] if t_p else None], lambda e: e.scalar_tensor_tensor(one(wexp[:, sl]), M_bc[:, dslice(h, 1, 0, 1), sl], u_h[:, b:b + 1],
                                                                       zeros_like(w), ALU.subtract, ALU.max))
                    t = A([t], lambda e: e.activation(wexp[:, sl], wexp[:, sl], ACT.Exp, scale=-1.0))
                    t = V([t, t_s[b], prev("pv")], lambda e: e.tensor_tensor(pT[:, b, sl], ps[:, b, 0:w], wexp[:, sl], ALU.mult))
                    keep(f"p{b}", t)
                    t_p.append(V([t], lambda e: e.tensor_tensor(pT[:, b, b * P:(b + 1) * P], pT[:, b, b * P:(b + 1) * P], const("causal"), ALU.mult)))
                def over_blocks(bank, lhs):
                    if pr.dry:
                        return
                    for b in range(4):
                        ins = pe.matmul(ps[:, bank, b * P:S], lhs(b), pT[:, b, b * P:S], start=b == 0, stop=b == 3, skip_group_check=True)
                    return ins
                t_n = None
                for t in (t_p[-1], t_vh, prev("h1")):
                    if t is not None and not pr.dry:
                        t.wait(pe)
                t_n0 = pr.c_pe.add(over_blocks(4, lambda b: v_h[:, b, 0:P]))
                t_n1 = pr.c_pe.add(over_blocks(5, lambda b: v_h[:, b, P:2 * P]))
                t_den = pr.c_pe.add(over_blocks(6, lambda b: ones))
                keep("pv", t_den)
                t = A([t_den, prev("h1")], lambda e: e.activation(den, ps[:, 6, :], ACT.Abs))
                t = V([t], lambda e: e.tensor_tensor(one(den), one(den), floor_bc[:, dslice(h, 1, 0, 1), :], ALU.max))
                t = V([t], lambda e: e.reciprocal(den, den))
                for j in range(2):
                    t = V([t], lambda e: e.tensor_tensor(hT[:, j, :], ps[:, 4 + j, :], den, ALU.mult))
                keep("h1", t)
                t_q = A([t, prev("ss")], lambda e: e.activation(sq[:, :, 0:S], hT, ACT.Square))
                t_ss = mms([t_q], ps[:, 7, :], [(ones, sq[:, 0, 0:S]), (ones, sq[:, 1, 0:S])])
                keep("ss", t_ss)
                t_r = rsqrt_mean([7], [(0, S)], ML_DV, r_h, [t_ss])
                for j in range(2):
                    kk = dslice(h, 2, j, 1)
                    gain = vecs[:, dslice(h, 2, VEC["ml_head"] * DT + j, 1)]
                    t = V([t_r], lambda e: e.tensor_scalar(hT[:, j, :], hT[:, j, :], gain, None, ALU.mult))
                    t = V([t], lambda e: e.tensor_tensor(hT[:, j, :], hT[:, j, :], r_h, ALU.mult))
                    t = V([t], lambda e: e.tensor_tensor(one(hT[:, j, :]), one(hT[:, j, :]), og[:, kk, :], ALU.mult))
                    t2 = A([t], lambda e: e.activation(u_hi[:, kk, XS], one(hT[:, j, :]), ACT.Copy))
                    t = V([t2], lambda e: e.tensor_tensor(u_lo[:, kk, XS], one(hT[:, j, :]), u_hi[:, kk, XS].bitcast(F32), ALU.subtract))
            for t in t_v + [t_u]:
                for e in (act, dve, pe):
                    t.wait(e)
            pr.loop(ML_H, head)
            y = area(0, 8, S)
            return y, project_out(y, u_rhs, pr.all_done())

        V([], lambda e: e.memset(zrow[:, :], 0.0))
        zeros_like = lambda w: zrow[:, 0:1].broadcast_to([P, w])
        ones_row = lambda n: const("ones")[0:n, 0:1].broadcast_to([n, S])

        def finish(src):
            ts = pr.all_done()
            for t in ts:
                t.wait(sp)
            sp.dma_start(out.rearrange("(k p) n -> p k n", p=P), src).then_inc(s_out, 16)
            sp.wait_ge(s_out, 16)

        y, t_y = mlstm()

        def attend_memory(layer, y_in, t_y):
            mem_in, kv = area(8192, DT, MEM), area(10240, 16, MEM)
            v_tok, qT = area(14336, 2, D), area(16384, 8, S)
            Pn, pT = area(20480, 4, MEM), area(21504, 2, S)
            q_h, v_h = area(8192, 2, S), area(9216, 2, XA_D)
            for t in pr.all_done():
                t.wait(act)
            act.dma_start(mem_in, memT.rearrange("(k p) n -> p k n", p=P)).then_inc(s_mem, 16)
            t_mem = Tok(c_meml, 16 * (layer + 1))
            after = prenorm(mem_in, "mem", [(0, MEM)], pr.all_done() + [t_mem])
            linear(4, square_outs, RING, u_rhs, [(0, MEM)], scaled_to(kv, 4, [(0, MEM)]), after, 4)
            after = prenorm(x, f"g{layer}2", ONE, pr.all_done(), each=add_after(t_y + pr.all_done(), y_in, f"g{layer}1"))
            linear(2, square_outs, RING, u_rhs, ONE, scaled_to(qT, 4), after, 4)
            kT = kv[:, 0:DT, :]
            transpose_tiles(pr.all_done(), kv[:, DT:, :], v_tok, 2, DT)
            for t in pr.all_done():
                for e in (pe, act, dve):
                    t.wait(e)
            scale = XA_D ** -0.5
            mx, sm = tmp[:, 0, 0:4], tmp[:, 1, 0:4]

            def head(h, prev, keep):
                t_q = V([prev("scores")], lambda e: e.tensor_copy(q_h, qT[:, dslice(h, 2, 0, 2), :]))
                t_v = A([prev("pv")], lambda e: e.activation(v_h, v_tok[:, :, dslice(h, XA_D, 0, XA_D)], ACT.Copy))
                for b in range(4):
                    t_s = mms([t_q, prev("exp")], ps[:, b // 2, (b % 2) * MEM:(b % 2 + 1) * MEM],
                              [(q_h[:, j, b * P:(b + 1) * P], kT[:, dslice(h, 2, j, 1), :].rearrange("p o n -> p (o n)")) for j in range(2)])
                keep("scores", t_s)
                sc = lambda b: ps[:, b // 2, (b % 2) * MEM:(b % 2 + 1) * MEM]
                t = V([t_s, prev("exp")], lambda e: e.tensor_reduce(mx, ps[:, 0:2, :].rearrange("p c (b n) -> p (c b) n", n=MEM), AX.X, ALU.max))
                t = V([t], lambda e: e.tensor_scalar(mx, mx, -scale, None, ALU.mult))
                for b in range(4):
                    t_e = A([t, prev("pT")], lambda e: e.activation(Pn[:, b, :], sc(b), ACT.Exp, bias=mx[:, b:b + 1], scale=scale, accum_out=sm[:, b:b + 1]))
                keep("exp", t_e)
                t = V([t_e], lambda e: e.reciprocal(sm, sm))
                for b in range(4):
                    t_n = V([t], lambda e: e.tensor_scalar(Pn[:, b, :], Pn[:, b, :], sm[:, b:b + 1], None, ALU.mult))
                for j in range(2):
                    if not pr.dry:
                        t_n.wait(pe)
                        if prev("pT"):
                            prev("pT").wait(pe)
                        for b in range(4):
                            ins = pe.transpose(ps[:, 2 + j, b * P:(b + 1) * P], Pn[:, b, j * P:(j + 1) * P], ident)
                        ins_ = ins
                    else:
                        ins_ = None
                    t_tr = pr.c_pe.add(ins_)
                    if j == 0:
                        t_c0 = V([t_tr, prev("pv")], lambda e: e.tensor_copy(pT[:, 0, :], ps[:, 2, :]))
                    else:
                        t_c1 = A([t_tr, prev("pv")], lambda e: e.activation(pT[:, 1, :], ps[:, 3, :], ACT.Copy))
                keep("pT", t_tr)
                for j in range(2):
                    t_o = mms([t_c0, t_c1, t_v, prev(f"out{j}")], ps[:, 4 + j, :], [(v_h[:, b, j * P:(j + 1) * P], pT[:, b, :]) for b in range(2)])
                    k = dslice(h, 2, j, 1)
                    t_h = A([t_o], lambda e: e.activation(u_hi[:, k, XS], ps[:, 4 + j:5 + j, :], ACT.Copy))
                    t = V([t_h], lambda e: e.tensor_tensor(u_lo[:, k, XS], ps[:, 4 + j:5 + j, :], u_hi[:, k, XS].bitcast(F32), ALU.subtract))
                    keep(f"out{j}", t)
                keep("pv", t_o)
                keep("copied", t_c1)
            pr.loop(XA_H, head)
            y = area(0, 8, S)
            return y, project_out(y, u_rhs, pr.all_done())

        FFN_OUTS = [[(o * DOWN_UNITS + k // UT, k % UT, k) for k in range(FT)] for o in range(4)]

        def store_split(t, v, k):
            t2 = A([t], lambda e: e.activation(hid_hi[:, k, :], v, ACT.Copy))
            return V([t2], lambda e: e.tensor_tensor(hid_lo[:, k, :], v, hid_hi[:, k, :].bitcast(F32), ALU.subtract))

        def ffn(layer, y_in, t_y):
            after = prenorm(x, f"g{layer}4", ONE, pr.all_done(), each=add_after(t_y + pr.all_done(), y_in, f"g{layer}3"))
            rs = rstd[:, XS]

            def evac(i, o, banks, ready, prev, keep):
                f = o // 2
                g, w = tmp[:, 2 * f, 0:S], tmp[:, 2 * f + 1, 0:S]
                bank = ps[:, banks[0], :]
                if o % 2 == 0:
                    t = V([ready, prev(f"h{f}")], lambda e: e.tensor_tensor(g, bank, rs, ALU.mult))
                    evac.silu = A([t], lambda e: e.activation(g, g, ACT.Silu))
                    return t
                t = V([ready, prev(f"hi{f}")], lambda e: e.tensor_tensor(w, bank, rs, ALU.mult))
                t2 = V([evac.silu, t], lambda e: e.tensor_tensor(w, w, g, ALU.mult))
                keep(f"h{f}", t2)
                k = dslice(i, 2, f, 1)
                one = w.rearrange("p (o n) -> p o n", o=1)
                keep(f"hi{f}", store_split(t2, one, k))
                return t
            linear(FT // 2, square_outs, RING, u_rhs, ONE, evac, after, 4)
            return y_ffn, project_out(y_ffn, hid_rhs, pr.all_done(), 2, FFN_OUTS, 4 * DOWN_UNITS)

        y, t_y = attend_memory(0, y, t_y)
        y, t_y = ffn(0, y, t_y)

        AT = (0, 512, 1024, 896)
        SPAN = 1280

        def stick_breaking(y_in, t_y):
            after = prenorm(x, "g10", ONE, pr.all_done(), each=add_after(t_y + pr.all_done(), y_in, "g05"))
            qT, kT, vT = area(0, 8, S), area(4096, 8, S), area(8192, 8, S)
            v_tok = area(12288, 4, D)
            sp_, aT = area(16384, 2, SPAN), area(18944, 2, SPAN)
            q_p, k_p, v_p = area(8192, S), area(8704, S), area(9216, 4, P)
            linear(6, square_outs, RING, u_rhs, ONE, scaled_to(area(0, 24, S), 4), after, 4)
            transpose_tiles(pr.all_done(), vT, v_tok, 4, DT)
            for t in pr.all_done():
                for e in (pe, act, dve):
                    t.wait(e)
            table("natural_log_exp_and_others")
            one = lambda v: v.rearrange("p (o n) -> p o n", o=1)
            flat = ps[:, :, :].rearrange("p b n -> p (b n)")

            def pair(i, prev, keep):
                t_q = V([prev("z1")], lambda e: e.tensor_scalar(one(q_p), qT[:, dslice(i, 1, 0, 1), :], SB_D ** -0.5, None, ALU.mult))
                t_k = V([], lambda e: e.tensor_copy(one(k_p), kT[:, dslice(i, 1, 0, 1), :]))
                t_v = A([prev("av1")], lambda e: e.activation(v_p, v_tok[:, :, dslice(i, P, 0, P)], ACT.Copy))
                t_z, t_ab, t_sp, t_c, t_a = {}, {}, {}, {}, {}
                for h in range(2):
                    z0 = 3 * 512 * h
                    R = slice(64 * h, 64 * h + 64)
                    if not pr.dry:
                        wait_all(pe, [t_q, t_k, prev(f"a{h}")])
                        for b in range(4):
                            ins = pe.matmul(flat[:, z0 + AT[b]:z0 + AT[b] + S - b * P], k_p[R, b * P:(b + 1) * P], q_p[R, b * P:S],
                                            start=b != 3, stop=False, skip_group_check=True)
                    t_z[h] = pr.c_pe.add(None if pr.dry else ins)
                    keep(f"z{h}", t_z[h])
                    z = flat[:, z0:z0 + SPAN]
                    sp_h = sp_[:, h, :]
                    t = A([t_z[h], prev(f"c{h}")], lambda e: e.activation(sp_h, z, ACT.Abs))
                    t = A([t], lambda e: e.activation(sp_h, sp_h, ACT.Exp, scale=-1.0))
                    t = A([t], lambda e: e.activation(sp_h, sp_h, ACT.Ln, bias=1.0))
                    t = V([t], lambda e: e.scalar_tensor_tensor(sp_h, z, 0.0, sp_h, ALU.max, ALU.add))
                    for b in range(4):
                        d = sp_h[:, AT[b]:AT[b] + P]
                        t_sp[h] = V([t], lambda e: e.tensor_tensor(d, d, const("strict"), ALU.mult))
                for h in range(2):
                    z0 = 3 * 512 * h
                    if not pr.dry:
                        wait_all(pe, [t_sp[h]])
                        for b in range(4):
                            for j in range(3, b, -1):
                                pe.matmul(flat[:, z0 + AT[b] + (j - b) * P:z0 + AT[b] + S - b * P], const("neg_ones"),
                                          sp_[:, h, AT[j]:AT[j] + S - j * P], start=False, stop=False, skip_group_check=True)
                            pe.matmul(flat[:, z0 + AT[b]:z0 + AT[b] + S - b * P], const("neg_suffix"),
                                      sp_[:, h, AT[b]:AT[b] + S - b * P], start=False, stop=False, skip_group_check=True)
                            ins = pe.matmul(flat[:, z0 + AT[b]:z0 + AT[b] + P], ident, const("neg_fill"),
                                            start=False, stop=True, skip_group_check=True)
                    t_c[h] = pr.c_pe.add(None if pr.dry else ins)
                    keep(f"c{h}", t_c[h])
                    t_a[h] = A([t_c[h], prev(f"av{h}")], lambda e: e.activation(aT[:, h, :], flat[:, z0:z0 + SPAN], ACT.Exp))
                    keep(f"a{h}", t_a[h])
                for h in range(2):
                    if not pr.dry:
                        wait_all(pe, [t_a[h], t_v, prev("out")])
                        for b in range(4):
                            ins = pe.matmul(ps[64 * h:64 * h + 64, 6, b * P:S], v_p[:, b, 64 * h:64 * h + 64],
                                            aT[:, h, AT[b]:AT[b] + S - b * P], start=b == 0, stop=b == 3, skip_group_check=True)
                    t_av = pr.c_pe.add(None if pr.dry else ins)
                    keep(f"av{h}", t_av)
                k = dslice(i, 1, 0, 1)
                t = A([t_av], lambda e: e.activation(u_hi[:, k, XS], ps[:, 6:7, :], ACT.Copy))
                t = V([t], lambda e: e.tensor_tensor(u_lo[:, k, XS], ps[:, 6:7, :], u_hi[:, k, XS].bitcast(F32), ALU.subtract))
                keep("out", t)
            pr.loop(SB_H // 2, pair)
            y = area(0, 8, S)
            return y, project_out(y, u_rhs, pr.all_done())

        y, t_y = stick_breaking(y, t_y)
        y, t_y = attend_memory(1, y, t_y)
        y, t_y = ffn(1, y, t_y)

        z_hi = sb("z_hi", [P, DT, N], F32R, over=arena_at)
        z_lo = sb("z_lo", [P, DT, N], F32R, over=arena_at + 4 * DT * N)
        PAIRS = [(P_, b_) for P_, b_ in ((TWO, [0, 1]), (TWO, [2, 3]), (TWO, [4, 5]), (TWO, [6, 7]))]
        HN = HG_H * N

        def mix(y_in, t_y):
            table("natural_log_exp_and_others")
            after = prenorm(x, "mix_pre", TWO, pr.all_done(), each=add_after(t_y + pr.all_done(), y_in, "g15"))
            proj = area(0, 20, N)
            q, f, iT, g, vp = (proj[:, 4 * n:4 * n + 4, :] for n in range(5))
            flat = lambda n: area(n * HN, HN)
            kT, aT = area(5 * HN, 4, N), area(6 * HN, 4, N)
            work = 7 * HN
            masks = area(work, len(LEVELS), P).bitcast(I32)
            reset, reset_m = area(work + 896, HG_H * P), area(work + 1408, HG_H * META)
            inv = area(work + 1472, 4, META)
            pool_w_sb = area(work + 1536, 4, P)
            at = work + 2048
            bufs = {}
            for name in ("q_s", "k_s", "l_s", "b", "e0", "e1", "ac0", "ac1", "sc", "state", "i_tok", "k_tok", "o_s"):
                bufs[name] = area(at, HG_H * P)
                at += HG_H * P
            t_all = pr.all_done()
            wait_all(act, t_all)
            for dst, src in ((area(work, 896), masks_d), (area(work + 896, 640), consts_d[:, CONST["reset"][0]:CONST_ALL]),
                             (area(work + 1536, 512), pool_w)):
                act.dma_start(dst.bitcast(I32) if src is masks_d else dst, src).then_inc(s_small, 16)
            loaded = Tok(c_small, 48 + 80 + 48)
            linear(5, square_outs, RING, u_rhs, TWO, scaled_to(proj, 4, TWO), after, 4)
            t_all = pr.all_done()

            low = vecs[:, len(VEC) * DT + 4 * HALF_VEC["lower"]:len(VEC) * DT + 4 * HALF_VEC["lower"] + 4]
            lb, lb1, gam = tmp_small(0), tmp_small(1), tmp_small(2)
            t = V(t_all, lambda e: e.tensor_tensor(gam, low, low, ALU.subtract))
            t = A([t], lambda e: e.activation(gam, gam, ACT.Exp))
            t = V([t], lambda e: e.reciprocal(lb, gam))
            t = V([t], lambda e: e.tensor_tensor(gam, gam, lb, ALU.mult))
            t = V([t], lambda e: e.tensor_tensor(lb, gam, gam, ALU.subtract))
            t = V([t], lambda e: e.tensor_scalar(lb, lb, 0.0, 1.0, ALU.max, ALU.min))
            t_lb = V([t], lambda e: e.tensor_scalar(lb1, lb, -1.0, 1.0, ALU.mult, ALU.add))

            table("sigmoid_and_others")
            t_k = A(t_all, lambda e: e.activation(flat(5), flat(1), ACT.Sigmoid, scale=-1.0))
            t_f = A([t_k], lambda e: e.activation(flat(1), flat(1), ACT.Sigmoid))
            A([], lambda e: e.activation(flat(3), flat(3), ACT.Sigmoid))
            for h in range(HG_H):
                V([t_k, t_lb], lambda e: e.tensor_scalar(kT[:, h, :], kT[:, h, :], lb1[:, h:h + 1], None, ALU.mult))
                t = V([t_f, t_lb], lambda e: e.tensor_scalar(f[:, h, :], f[:, h, :], lb1[:, h:h + 1], lb[:, h:h + 1], ALU.mult, ALU.add))
            low_f = area(6 * HN, HN)
            t = V([t], lambda e: e.tensor_scalar(low_f, flat(1), 1e-30, 2.0 ** 60, ALU.max, ALU.mult))
            t = V([t], lambda e: e.tensor_scalar(low_f, low_f, 1.0, None, ALU.min))
            t = V([t], lambda e: e.tensor_scalar(flat(1), flat(1), 2.0 ** -60, None, ALU.max))
            table("natural_log_exp_and_others")
            t = A([t], lambda e: e.activation(low_f, low_f, ACT.Ln))
            t = A([t], lambda e: e.activation(flat(1), flat(1), ACT.Ln))
            t_l = V([t], lambda e: e.tensor_tensor(flat(1), flat(1), low_f, ALU.add))

            wait_all(dve, [loaded])
            for gi, width in enumerate(WINDOWS):
                src, d, n = vp[:, gi, :], 1, 0
                while d < width:
                    dst = sq[:, n % 2, :]
                    t = V([t_l], lambda e: e.tensor_copy(dst[:, 0:d], src[:, 0:d]))
                    t = V([t], lambda e: e.tensor_tensor(dst[:, d:N], src[:, d:N], src[:, 0:N - d], ALU.add))
                    t_l, src, d, n = t, dst, 2 * d, n + 1
                t = V([t], lambda e: e.tensor_tensor(src[:, 0:META], src[:, 0:META], inv[:, gi, :], ALU.mult))
                t = V([t], lambda e: e.tensor_scalar(src[:, META:N], src[:, META:N], 1.0 / width, None, ALU.mult))
                t = V([t], lambda e: e.tensor_tensor(src, src, vp[:, gi, :], ALU.subtract))
                for b, (c0, c1) in enumerate(TWO):
                    t_m = mms([t, loaded], ps[:, b, 0:HALF], [(pool_w_sb[:, gi, :], src[:, c0:c1])])
                for b, (c0, c1) in enumerate(TWO):
                    t = V([t_m], lambda e: e.tensor_scalar(vp[:, gi, c0:c1], ps[:, b, 0:HALF], half_col("pool_scale", gi), None, ALU.mult))
                t_l = t

            def tile(T, cols, first, prev, keep):
                w = HG_H * T
                r2 = lambda v: v[:, 0:w]
                r3 = lambda v: v[:, 0:w].rearrange("p (h t) -> p h t", h=HG_H)
                q_s, k_s, l_s, b = (bufs[n] for n in ("q_s", "k_s", "l_s", "b"))
                state, i_tok, k_tok, o_s, sc = (bufs[n] for n in ("state", "i_tok", "k_tok", "o_s", "sc"))
                ee, ac = [bufs["e0"], bufs["e1"]], [bufs["ac0"], bufs["ac1"]]
                t_q = V([prev("end")], lambda e: e.tensor_copy(r3(q_s), q[:, :, cols]))
                t_kk = V([], lambda e: e.tensor_copy(r3(k_s), kT[:, :, cols]))
                t_i = A([prev("end")], lambda e: e.activation(r3(o_s), iT[:, :, cols], ACT.Copy))
                t = V([], lambda e: e.tensor_copy(r3(l_s), f[:, :, cols]))
                t_b = V([t], lambda e: e.tensor_tensor_scan(r2(b), (reset if T == P else reset_m)[:, 0:w], r2(l_s), 0.0, ALU.mult, ALU.add))
                wait_all(pe, [] if pr.dry else [t_kk, prev("end"), prev("end_a")])
                def heads(bank, lhs, rhs, M):
                    if pr.dry:
                        return pr.c_pe.add(None)
                    for h in range(HG_H):
                        ins = pe.matmul(ps[0:M, bank, h * T:(h + 1) * T], lhs(h), rhs(h), start=True, stop=True)
                    return pr.c_pe.add(ins)
                hd = lambda v, h: v[:, h * T:(h + 1) * T]
                t_d = heads(2, lambda h: hd(k_s, h), lambda h: hd(q_s, h), T)
                bc = lambda v: v.rearrange("p (o t) -> p o t", o=1).broadcast_to([T, HG_H, T])
                sc3 = sc[0:T, 0:w].rearrange("p (h t) -> p h t", h=HG_H)
                t_sc = V([t_d], lambda e: e.tensor_tensor(sc3, ps[0:T, 2, 0:w].rearrange("p (h t) -> p h t", h=HG_H), bc(ident[0:T, 0:T]), ALU.mult))
                def turned(bank, src, dst, after, on):
                    if not pr.dry:
                        wait_all(pe, after)
                        for h in range(HG_H):
                            ins = pe.transpose(ps[0:T, bank, h * P:(h + 1) * P], hd(src, h), ident)
                    t = pr.c_pe.add(None if pr.dry else ins)
                    return A([t], lambda e: e.activation(dst[0:T, :], ps[0:T, bank, :], ACT.Copy))
                t_it = turned(3, o_s, i_tok, [t_i], A)
                t_ac, t_mask = [], []
                def masked(n):
                    return V([], lambda e: e.copy_predicated(sc3, bc(masks[0:T, n, 0:T]), ps[0:T, n % 2, 0:w].rearrange("p (h t) -> p h t", h=HG_H)))
                for n, B in enumerate(l_ for l_ in LEVELS if l_ <= T):
                    nb, hb = w // B, B // 2
                    blk = lambda v: v[:, 0:w].rearrange("p (n b) -> p n b", b=B)
                    e_, a_ = ee[n % 2], ac[n % 2]
                    t = V([t_b, t_ac[n - 2] if n >= 2 else None], lambda e: e.tensor_tensor(blk(e_), blk(b), blk(b)[:, :, hb - 1:hb].broadcast_to([P, nb, B]), ALU.subtract))
                    A([t], lambda e: e.activation(blk(e_)[:, :, 0:hb], blk(e_)[:, :, 0:hb], ACT.Exp, scale=-1.0))
                    t = A([], lambda e: e.activation(blk(e_)[:, :, hb:B], blk(e_)[:, :, hb:B], ACT.Exp))
                    V([t, t_mask[n - 2] if n >= 2 else None], lambda e: e.tensor_tensor(blk(a_)[:, :, 0:hb], blk(k_s)[:, :, 0:hb], blk(e_)[:, :, 0:hb], ALU.mult))
                    t = V([t_m, t_sc] if n else [], lambda e: e.tensor_tensor(blk(a_)[:, :, hb:B], blk(q_s)[:, :, hb:B], blk(e_)[:, :, hb:B], ALU.mult))
                    t_ac.append(t)
                    if n:
                        t_sc = masked(n - 1)
                        t_mask.append(t_sc)
                    if not pr.dry:
                        wait_all(pe, [t, t_mask[n - 2] if n >= 2 else None])
                    t_m = heads(n % 2, lambda h: hd(a_, h), lambda h: hd(a_, h), T)
                last = r3(b)[:, :, T - 1:T]
                t = V([t_ac[-1], t_m, t_sc], lambda e: e.tensor_tensor(r3(ee[0]), last.broadcast_to([P, HG_H, T]), r3(b), ALU.subtract))
                t_sc = masked(n)
                A([t], lambda e: e.activation(r2(ee[0]), r2(ee[0]), ACT.Exp))
                A([], lambda e: e.activation(small_e, last.rearrange("p h o -> p (h o)"), ACT.Exp))
                t = A([], lambda e: e.activation(r2(ee[1]), r2(b), ACT.Exp))
                V([t, t_sc], lambda e: e.tensor_tensor(r2(ac[0]), r2(k_s), r2(ee[0]), ALU.mult))
                t = V([], lambda e: e.tensor_tensor(r2(ac[1]), r2(q_s), r2(ee[1]), ALU.mult))
                t_kt = turned(4, ac[0], k_tok, [t], A)
                if not pr.dry:
                    wait_all(pe, [t_sc, t_it, t_kt, t])
                    for h in range(HG_H):
                        pe.matmul(ps[:, 5, h * T:(h + 1) * T], i_tok[0:T, h * P:(h + 1) * P], sc[0:T, h * T:(h + 1) * T], start=True, stop=first)
                        if not first:
                            ins = pe.matmul(ps[:, 5, h * T:(h + 1) * T], state[:, h * P:(h + 1) * P], hd(ac[1], h), start=False, stop=True)
                    for h in range(HG_H):
                        ins = pe.matmul(ps[:, 6, h * P:(h + 1) * P], k_tok[0:T, h * P:(h + 1) * P], i_tok[0:T, h * P:(h + 1) * P], start=True, stop=True)
                t_o = pr.c_pe.add(None if pr.dry else ins)
                for h in range(HG_H):
                    hs = slice(h * P, (h + 1) * P)
                    if first:
                        t_st = V([t_o], lambda e: e.tensor_copy(state[:, hs], ps[:, 6, hs]))
                    else:
                        t_st = V([t_o], lambda e: e.scalar_tensor_tensor(state[:, hs], state[:, hs], small_e[:, h:h + 1], ps[:, 6, hs], ALU.mult, ALU.add))
                t = A([t_o], lambda e: e.activation(r2(o_s), ps[:, 5, 0:w], ACT.Copy))
                t = A([t], lambda e: e.activation(sq[:, 0, 0:w], r2(o_s), ACT.Square))
                t = mms([t], ps[:, 7, 0:w], [(ones, sq[:, 0, 0:w])])
                t = rsqrt_mean([7], [(0, w)], P, sq[:, 1, :], [t])
                t = V([t], lambda e: e.tensor_tensor(r2(o_s), r2(o_s), sq[:, 1, 0:w], ALU.mult))
                for h in range(HG_H):
                    t2 = V([t], lambda e: e.tensor_scalar(hd(o_s, h), hd(o_s, h), half_col("hg_out", h), None, ALU.mult))
                t = V([t2], lambda e: e.tensor_tensor(aT[:, :, cols], r3(o_s), g[:, :, cols], ALU.mult))
                keep("end", t)
                keep("end_a", pr.now(pr.c_act))

            ts = pr.all_done()
            for e in (pe, act, dve):
                wait_all(e, ts)
            tile(META, slice(0, META), True, lambda n: None, lambda n, t: None)
            ts = pr.all_done()
            for e in (pe, act, dve):
                wait_all(e, ts)
            pr.loop(S // P, lambda i, prev, keep: tile(P, dslice(i, P, META, P), False, prev, keep))

            table("sigmoid_and_others")
            sg = area(7 * HN, 16, N)
            to_sg = scaled_to(sg, 4, TWO)
            def sg_evac(i, o, banks, ready, prev, keep):
                t = to_sg(i, o, banks, ready, prev, keep)
                v = sg[:, dslice(i, 4, o, 1), :]
                A([t], lambda e: e.activation(v, v, ACT.Sigmoid))
                return t
            linear(4, square_outs, RING, u_rhs, TWO, sg_evac, pr.all_done(), 4)
            for k in range(DT):
                src = aT[:, k, :] if k < 4 else vp[:, k - 4, :]
                t = A(pr.all_done() if k == 0 else [], lambda e: e.activation(u_hi[:, k, :], src, ACT.Copy))
                V([t], lambda e: e.tensor_tensor(u_lo[:, k, :], src, u_hi[:, k, :].bitcast(F32), ALU.subtract))

            def z_evac(i, o, banks, ready, prev, keep):
                m, br = o // 2, o % 2
                s_ = sg[:, dslice(i, 8, o, 1), :]
                zt = sq[:, br:br + 1, :]
                for (c0, c1), b in zip(TWO, banks):
                    t = V([ready, prev("z7") if o < 2 else z_evac.z.get(o - 1 - br)], lambda e: e.tensor_tensor(zt[:, :, c0:c1], ps[:, b:b + 1, 0:HALF], s_[:, :, c0:c1], ALU.mult))
                if br:
                    k = dslice(i, 4, m, 1)
                    t2 = V([t], lambda e: e.tensor_tensor(zt, zt, sq[:, 0:1, :], ALU.add))
                    t2 = A([t2], lambda e: e.activation(z_hi[:, k, :], zt, ACT.Copy))
                    t2 = V([t2], lambda e: e.tensor_tensor(z_lo[:, k, :], zt, z_hi[:, k, :].bitcast(F32), ALU.subtract))
                    z_evac.z[o] = t2
                    keep(f"z{o}", t2)
                return t
            z_evac.z = {}
            outs = [[(o // 2, 4 * (o % 2) + k, 4 * (o % 2) + k) for k in range(4)] for o in range(2 * RING)]
            linear(2, outs, RING, u_rhs, TWO, z_evac, pr.all_done(), 4)
            y = area(2 * DT * N, DT, N)
            z_rhs = lambda k, c0, c1: (z_hi[:, k, c0:c1], z_lo[:, k, c0:c1])
            return y, project_out(y, z_rhs, pr.all_done(), parts=TWO)

        tmp_small = lambda n: small[:, n, :]
        small_e = small[:, 3, :]

        G0 = META - 4
        GW = N - G0
        CONV_LAYOUT = [([(G0, G0 + GW // 2), (G0 + GW // 2, N)], [0, 1]), (ONE, [2]),
                       ([(G0, G0 + GW // 2), (G0 + GW // 2, N)], [3, 4]), (ONE, [5])]

        def conv_ffn(y_in, t_y):
            table("natural_log_exp_and_others")
            after = prenorm(x, "ffn_pre", TWO, pr.all_done(), each=add_after(t_y + pr.all_done(), y_in, "mix_post", slice(0, N)))
            table("gelu_apprx_tanh_and_others")

            def evac(i, o, banks, ready, prev, keep):
                f_ = o // 2
                gt, w = tmp[:, 2 * f_, 0:GW], tmp[:, 2 * f_ + 1, 0:S]
                if o % 2 == 0:
                    for (c0, c1), b in zip(CONV_LAYOUT[0][0], banks):
                        t = V([ready, prev(f"done{f_}")], lambda e: e.tensor_tensor(gt[:, c0 - G0:c1 - G0], ps[:, b, 0:c1 - c0], rstd[:, c0:c1], ALU.mult))
                    one = lambda v: v.rearrange("p (o n) -> p o n", o=1)
                    tap = lambda j: conv[:, dslice(i, 2, f_, 1), j:j + 1].rearrange("p o n -> p (o n)")
                    c = sq[:, f_, 0:S]
                    lag = lambda j: gt[:, META - G0 - j:META - G0 - j + S]
                    t2 = V([t], lambda e: e.tensor_scalar(c, lag(0), tap(2), tap(3), ALU.mult, ALU.add))
                    t2 = V([t2], lambda e: e.scalar_tensor_tensor(c, lag(1), tap(1), c, ALU.mult, ALU.add))
                    t2 = V([t2], lambda e: e.scalar_tensor_tensor(c, lag(2), tap(0), c, ALU.mult, ALU.add))
                    evac.gelu = A([t2], lambda e: e.activation(c, c, ACT.Gelu_apprx_tanh))
                    return t
                c = sq[:, f_, 0:S]
                t = V([ready, prev(f"done{f_}")], lambda e: e.tensor_tensor(w, ps[:, banks[0], :], rstd[:, XS], ALU.mult))
                t2 = V([evac.gelu, t], lambda e: e.tensor_tensor(w, w, c, ALU.mult))
                k = dslice(i, 2, f_, 1)
                keep(f"done{f_}", store_split(t2, w.rearrange("p (o n) -> p o n", o=1), k))
                return t
            linear(FT // 2, square_outs, RING, u_rhs, ONE, evac, after, 4, CONV_LAYOUT)
            return y_ffn, project_out(y_ffn, hid_rhs, pr.all_done(), 2, FFN_OUTS, 4 * DOWN_UNITS)

        y, t_y = mix(y, t_y)
        y, t_y = conv_ffn(y, t_y)
        add = add_after(t_y, y, "ffn_post")
        for k in range(DT):
            add(k)
        finish(x[:, :, XS])


def tiles_of(w, tiles):
    k, m = w.shape[0] // P, w.shape[1] // P
    t = np.asarray(w).reshape(k, P, m, P).transpose(0, 2, 1, 3)
    return [t[a, b] for a, b in tiles]


def pack(*tile_lists):
    flat = [t for ts in tile_lists for t in ts]
    blank = np.zeros((P, P), np.float32)
    flat = [blank if t is None else t for t in flat]
    a = np.stack(flat).reshape(-1, UT, P, P)
    return a.transpose(0, 2, 1, 3).reshape(-1, P, UT * P)


def by_output(w, cols=None):
    k, m = w.shape[0] // P, w.shape[1] // P
    return tiles_of(w, [(a, b) for b in (cols or range(m)) for a in range(k)])


def down_tiles(w):
    out = []
    for b in range(w.shape[1] // P):
        out += tiles_of(w, [(a, b) for a in range(FT)]) + [None] * (DOWN_UNITS * UT - FT)
    return out


def pairs_of(a, b):
    out = []
    for c in range(a.shape[1] // P):
        out += by_output(a, [c]) + by_output(b, [c])
    return out


def kernel(**inputs):
    import concourse.bacc as bacc
    from concourse.bass_utils import run_bass_kernel_spmd
    a = {k: np.asarray(v) for k, v in inputs.items()}
    stream = []
    w = a["ml_w_in"][0]
    stream += [by_output(w[:, 0:3072])]
    gates_w = w[:, 3072:3080]
    stream += [by_output(a["ml_w_out"][0])]
    for layer in range(2):
        if layer == 1:
            stream += [by_output(a["sb_w_qkv"][0]), by_output(a["sb_w_out"][0])]
        stream += [by_output(a["xa_w_kv"][layer]), by_output(a["xa_w_q"][layer]), by_output(a["xa_w_o"][layer])]
        gu = a["ffn_w_gate_up"][layer]
        stream += [pairs_of(gu[:, :FF], gu[:, FF:]), down_tiles(a["ffn_w_down"][layer])]
    w2 = a["w_in_2"][0]
    stream += [by_output(w2[:, 0:2560]), pairs_of(w2[:, 2560:3584], w2[:, 3584:4608])]
    stream += [pairs_of(a["w_branch_hgrn_2"][0], a["w_branch_pool_2"][0]), by_output(a["w_out_2"][0])]
    stream += [pairs_of(a["ffn_w_gate_2"][0], a["ffn_w_up_2"][0]), down_tiles(a["ffn_w_down_2"][0])]
    units = pack(*stream)
    xT = np.concatenate([a["meta_tokens_2"].T, a["x"][0].T], axis=1)
    col = lambda v: v.reshape(-1, P).T
    full = [a["norm_gains"][l, n] for l in range(2) for n in range(6)]
    full += [a["mem_norm_gain"], a["ml_head_gain"][0], a["mix_norm_pre_2"][0], a["mix_norm_post_2"][0],
             a["ffn_norm_pre_2"][0], a["ffn_norm_post_2"][0]]
    half = [a["hgrn_out_norm_2"][0], a["pool_scale_2"][0], a["hgrn_lower_bounds_2"][0]]
    vecs = np.concatenate([col(v) for v in full + half], axis=1)
    conv = np.stack([col(a["ffn_conv_w_2"][0, j]) for j in range(CONV)] + [col(a["ffn_conv_b_2"][0])], axis=2)
    consts, masks = shape_constants()
    arrays = {"units": units, "xT": xT, "memT": a["mem"][0].T, "vecs": vecs, "gates_w": gates_w,
              "gates_b": a["ml_b_gate"][0].reshape(8, 1), "pool_w": a["pool_proj_2"][0].transpose(1, 0, 2).reshape(P, -1),
              "conv": conv.reshape(P, -1), "consts": consts, "masks": masks}
    arrays = {k: np.ascontiguousarray(v) for k, v in arrays.items()}
    nc = bacc.Bacc("TRN2", target_bir_lowering=False, num_devices=1)
    args = [nc.dram_tensor(f"in_{k}", v.shape, mybir.dt.from_np(v.dtype), kind="ExternalInput").ap() for k, v in arrays.items()]
    o = nc.dram_tensor("outT", (D, S), F32, kind="ExternalOutput").ap()
    build(nc, *args, o)
    r = run_bass_kernel_spmd(nc, [{f"in_{k}": v for k, v in arrays.items()}], core_ids=[0])
    return np.ascontiguousarray(r.results[0]["outT"].T)[None]
```

```python
from contextlib import ExitStack, contextmanager

import numpy as np

import concourse.bass as bass
from concourse import mybir
from concourse.alu_op_type import AluOpType as ALU

F32 = mybir.dt.float32
F32R = mybir.dt.float32r
I32 = mybir.dt.int32
ACT = mybir.ActivationFunctionType
AX = mybir.AxisListType

P = 128
D = 1024
DT = D // P
S = 512
META = 16
N = S + META
HALF = N // 2
MEM = 256
FF = 2816
FT = FF // P
EPS = 1e-6

ML_H, ML_DK, ML_DV = 4, 128, 256
GATE_CAP = 15.0
SB_H, SB_D = 16, 64
XA_H, XA_D = 4, 256
HG_H = 4
CONV = 3
WINDOWS = (2, 4, 8, 16)

UT = 8
RING = 4
LAND = 2
LEAD = 3
DONE0 = 1
DOWN_UNITS = -(-FT // UT)

VEC = {}
for _l in range(2):
    for _n in range(6):
        VEC[f"g{_l}{_n}"] = len(VEC)
for _n in ("mem", "ml_head", "mix_pre", "mix_post", "ffn_pre", "ffn_post"):
    VEC[_n] = len(VEC)
HALF_VEC = {"hg_out": 0, "pool_scale": 1, "lower": 2}


class Tok:

    def __init__(self, counter, value, step=0, i=None):
        self.counter, self.value, self.step, self.i = counter, value, step, i

    def wait(self, eng):
        v = self.value if self.i is None or not self.step else self.i * self.step + self.value
        eng.wait_ge(self.counter.sem, v)


def wait_all(eng, toks):
    top = {}
    for t in toks:
        if t is not None:
            key = (id(t.counter), t.i is None)
            if key not in top or top[key].value < t.value:
                top[key] = t
    for t in top.values():
        t.wait(eng)


class Counter:

    def __init__(self, sem):
        self.sem, self.n, self.step, self.i = sem, 0, 0, None

    def add(self, ins):
        if ins is not None:
            ins.then_inc(self.sem, 1)
        self.n += 1
        return Tok(self, self.n, self.step, self.i)


class Program:
    def __init__(self, nc, ctx, n_units):
        self.nc, self.ctx = nc, ctx
        self.pe, self.act, self.dve, self.pool, self.sp = nc.tensor, nc.scalar, nc.vector, nc.gpsimd, nc.sync
        sem = lambda name: ctx.enter_context(nc.semaphore(name))
        self.c_pe, self.c_act = Counter(sem("pe_done")), Counter(sem("act_done"))
        self.c_dve, self.c_pool = Counter(sem("dve_done")), Counter(sem("pool_done"))
        self.counters = [self.c_pe, self.c_act, self.c_dve, self.c_pool]
        self.landed = [sem(f"unit_landed{j}") for j in range(LAND)]
        self.hi_done, self.lo_done = sem("unit_hi_done"), sem("unit_lo_done")
        self.unit_done = sem("unit_multiplied")
        self.dry = False
        self.n_units, self.unit = n_units, 0

    def op(self, eng, counter, after, make):
        if self.dry:
            return counter.add(None)
        wait_all(eng, after)
        return counter.add(make(eng))

    def P(self, after, make):
        return self.op(self.pe, self.c_pe, after, make)

    def A(self, after, make):
        return self.op(self.act, self.c_act, after, make)

    def V(self, after, make):
        return self.op(self.dve, self.c_dve, after, make)

    def G(self, after, make):
        return self.op(self.pool, self.c_pool, after, make)

    def mms(self, after, out, pairs, start=True, stop=True):
        if self.dry:
            return self.c_pe.add(None)
        wait_all(self.pe, after)
        for n, (a, b) in enumerate(pairs):
            ins = self.pe.matmul(out, a, b, start=start and n == 0, stop=stop and n == len(pairs) - 1,
                                 skip_group_check=not (start and stop))
        return self.c_pe.add(ins)

    def loop(self, n, body, engines=None):
        counts = [c.n for c in self.counters]
        kept = {}
        self.dry, unit = True, self.unit
        body(0, lambda name: None, lambda name, t: kept.__setitem__(name, (t.counter, t.value)))
        self.dry = False
        steps = [c.n - n0 for c, n0 in zip(self.counters, counts)]
        units = self.unit - unit
        self.unit = unit
        step_of = dict(zip([id(c) for c in self.counters], steps))
        for c, n0, st in zip(self.counters, counts, steps):
            c.n, c.step = n0, st
        with self.nc.Fori(0, n) as i:
            for c in self.counters:
                c.i = i
            self.unit_i, self.unit_step = i, units
            prev = lambda name: Tok(kept[name][0], kept[name][1] - step_of[id(kept[name][0])],
                                    step_of[id(kept[name][0])], i)
            body(i, prev, lambda name, t: None)
        for c, n0, st in zip(self.counters, counts, steps):
            assert c.n == n0 + st
            c.n, c.step, c.i = n0 + st * n, 0, None
        self.unit, self.unit_i, self.unit_step = unit + units * n, None, 0
        return {k: Tok(c, v + step_of[id(c)] * (n - 1)) for k, (c, v) in kept.items()}

    def now(self, counter):
        return Tok(counter, counter.n)

    def all_done(self):
        return [self.now(c) for c in self.counters]

    unit_i, unit_step = None, 0

    def unit_wait(self, eng, sem, u, each=1):
        v = (u + 1) * each
        if self.unit_i is not None:
            v = self.unit_i * (self.unit_step * each) + v
        eng.wait_ge(sem, v)


def dslice(i, step, j, size):
    if isinstance(i, int):
        return slice(i * step + j, i * step + j + size)
    return bass.ds(i * step + j, size)


class Map:

    def __init__(self, nc):
        self.nc = nc
        self.at = -(-nc.sbuf_base // 64) * 64

    def place(self, name, shape, dt=F32, over=None):
        size = 4 * int(np.prod(shape[1:]))
        at = self.at if over is None else over
        if over is None:
            self.at += -(-size // 64) * 64
            assert self.at <= self.nc.sbuf_usable_end, (name, self.at)
        return self.nc.alloc_sbuf_tensor_at(name, shape, dt, offset=at)


CONST = {}
_at = 0
for _n, _w in (("ident", P), ("ones", P), ("neg_ones", P), ("neg_suffix", P), ("causal", P), ("strict", P),
               ("neg_fill", P), ("sel", ML_H * P), ("reset", HG_H * P), ("reset_meta", HG_H * META),
               ("inv_count", 4 * META)):
    CONST[_n] = (_at, _at + _w)
    _at += _w
CONST_ALL = _at
CONST_W = CONST["sel"][0]
LEVELS = (2, 4, 8, 16, 32, 64, 128)


def shape_constants():
    c = np.zeros((P, CONST_ALL), np.float32)
    s, t = np.arange(P)[:, None], np.arange(P)[None, :]
    put = lambda name, v: c.__setitem__((slice(None), slice(*CONST[name])), v)
    put("ident", s == t)
    put("ones", 1.0)
    put("neg_ones", -1.0)
    put("neg_suffix", np.where(s >= t, -1.0, 0.0))
    put("causal", t >= s)
    put("strict", t > s)
    put("neg_fill", np.where(t > s, 0.0, -1e30))
    put("sel", np.arange(ML_H * P)[None, :] // P == s)
    put("reset", np.arange(HG_H * P)[None, :] % P != 0)
    put("reset_meta", np.arange(HG_H * META)[None, :] % META != 0)
    put("inv_count", np.concatenate([1.0 / np.minimum(np.arange(META) + 1, w) for w in WINDOWS])[None, :])
    m = np.zeros((P, len(LEVELS), P), np.int32)
    for n, b in enumerate(LEVELS):
        m[:, n, :] = (s // b == t // b) & (s % b < b // 2) & (t % b >= b // 2)
    return c, m.reshape(P, -1)


def build(nc, units, xT, memT, vecs_d, gates_w, gates_b, pool_w, conv_d, consts_d, masks_d, out):
    n_units = units.shape[0]
    assert n_units % RING == 0
    ctx = ExitStack()
    with ctx:
        pr = Program(nc, ctx, n_units)
        pe, act, dve, pool, sp = pr.pe, pr.act, pr.dve, pr.pool, pr.sp
        A, V, T, mms = pr.A, pr.V, pr.P, pr.mms
        m = Map(nc)
        sb = m.place
        sem = lambda name: ctx.enter_context(nc.semaphore(name))

        x = sb("x", [P, DT, N])
        y_wide = m.at
        u_hi = sb("u_hi", [P, DT, N], F32R)
        u_lo = sb("u_lo", [P, DT, N], F32R)
        y_ffn = sb("y_ffn", [P, DT, N], F32, over=y_wide)[:, :, META:]
        w_land = sb("w_land", [P, LAND, UT * P])
        w_hi = sb("w_hi", [P, RING, UT * P], F32R)
        w_lo = sb("w_lo", [P, RING, UT * P], F32R)
        rstd = sb("rstd", [P, N])
        rstd_y = sb("rstd_y", [P, N])
        sq = sb("sq", [P, 2, N])
        acc_at = m.at
        acc = sb("acc", [P, N])
        NVEC = len(VEC) * DT + 4 * len(HALF_VEC)
        vecs = sb("vecs", [P, NVEC])
        consts = sb("consts", [P, CONST_W])
        conv = sb("conv", [P, FT, CONV + 1])
        eps = sb("eps", [P, 1])
        uT = sb("uT", [P, 4, ML_H])
        zrow = sb("zrow", [P, 1])
        rT = sb("rT", [P, 4])
        small = sb("small", [P, 4, 4])
        arena_at = m.at
        ARENA = 2 * FT * S + 4 * N
        arena = sb("arena", [P, ARENA])
        hid_hi = sb("hid_hi", [P, FT, S], F32R, over=arena_at)
        hid_lo = sb("hid_lo", [P, FT, S], F32R, over=arena_at + 4 * FT * S)
        tmp_at = 2 * FT * S
        ps = ctx.enter_context(nc.psum_tensor("ps", [P, 8, 512], F32))

        def area(at, *shape):
            size = int(np.prod(shape))
            assert at + size <= ARENA
            v = arena[:, at:at + size]
            if len(shape) == 2:
                return v.rearrange("p (a b) -> p a b", b=shape[1])
            if len(shape) == 3:
                return v.rearrange("p (a b c) -> p a b c", b=shape[1], c=shape[2])
            return v

        def halves(name, at, *shape):
            assert at + int(np.prod(shape)) <= ARENA
            v = sb(name, [P, *shape], F32R, over=arena_at + 4 * at)
            return v[(slice(None),) * (1 + len(shape))]

        tmp = area(tmp_at, 4, N)
        const = lambda name: consts[:, slice(*CONST[name])]
        ident, ones = const("ident"), const("ones")
        col = lambda name, k: vecs[:, VEC[name] * DT + k:VEC[name] * DT + k + 1]
        def half_col(name, k):
            c = len(VEC) * DT + 4 * HALF_VEC[name] + k
            return vecs[:, c:c + 1]
        XS = slice(META, N)
        MS = slice(0, MEM)

        s_small, s_x, s_mem, s_out = sem("small_loaded"), sem("x_loaded"), sem("mem_loaded"), sem("out_stored")
        c_small, c_xl, c_meml = Counter(s_small), Counter(s_x), Counter(s_mem)
        units_r = units
        land_at = lambda j: w_land[:, j % LAND, :]
        sp.dma_start(x[:, :, :], xT.rearrange("(k p) n -> p k n", p=P)).then_inc(s_x, 16)
        sp.dma_start(consts[:, :], consts_d[:, 0:CONST_W]).then_inc(s_small, 16)
        sp.dma_start(vecs[:, :], vecs_d).then_inc(s_small, 16)
        sp.dma_start(conv[:, :, :], conv_d.rearrange("p (k n) -> p k n", k=FT)).then_inc(s_small, 16)
        loaded_first = Tok(c_small, 48)
        x_in = Tok(c_xl, 16)
        for j in range(LAND):
            sp.dma_start(land_at(j), units[j, :, :]).then_inc(pr.landed[j], 16)
        with sp.Fori(1, n_units // LAND) as g:
            for j in range(LAND):
                sp.wait_ge(pr.lo_done, g * LAND + (j + 1 - LAND))
                sp.dma_start(land_at(j), units[bass.ds(g * LAND + j, 1), :, :].rearrange("o p n -> (o p) n"))\
                  .then_inc(pr.landed[j], 16)

        def split(u):
            if pr.dry or (pr.unit_i is None and u >= n_units):
                return
            j, looped = u % RING, pr.unit_i is not None
            v = 16 * (u // LAND + 1)
            act.wait_ge(pr.landed[j % LAND], pr.unit_i * (16 * (pr.unit_step // LAND)) + v if looped else v)
            if u >= RING or looped:
                pr.unit_wait(act, pr.unit_done, u - RING + DONE0)
                pr.unit_wait(pool, pr.unit_done, u - RING + DONE0)
            act.activation(w_hi[:, j, :], land_at(j), ACT.Copy).then_inc(pr.hi_done, 1)
            pr.unit_wait(pool, pr.hi_done, u)
            pool.tensor_tensor(w_lo[:, j, :], land_at(j), w_hi[:, j, :].bitcast(F32), ALU.subtract)\
                .then_inc(pr.lo_done, 1)

        for u in range(LEAD):
            split(u)
        t_eps = V([], lambda e: e.memset(eps[:, :], EPS))

        c_unit = Counter(pr.unit_done)
        pe.sem_inc(pr.unit_done, DONE0)

        def linear(n_iter, outs, n_u, rhs, parts, evac, after, depth, layout=None, head=None, before=None, between=()):
            between = list(between)
            wait_all(pe, after)
            if layout is None:
                layout = [(parts, [o * len(parts) + b for b in range(len(parts))]) for o in range(depth)]

            def tile_products(outs_, o, n, wait_unit):
                tiles = outs_[o]
                uj, q, k = tiles[n]
                u = pr.unit + uj
                parts_o, banks = layout[o % depth]
                if wait_unit:
                    pr.unit_wait(pe, pr.lo_done, u)
                hi = w_hi[:, u % RING, q * P:(q + 1) * P]
                lo = w_lo[:, u % RING, q * P:(q + 1) * P]
                for h, (w, which) in enumerate(((hi, 0), (hi, 1), (lo, 0))):
                    for (c0, c1), bank in zip(parts_o, banks):
                        ins = pe.matmul(ps[:, bank, 0:c1 - c0], w, rhs(k, c0, c1)[which],
                                        start=n == 0 and h == 0, stop=n == len(tiles) - 1 and h == 2)
                if not (any(t[0] == uj for t in tiles[n + 1:]) or any(t[0] == uj for ts in outs_[o + 1:] for t in ts)):
                    ins.then_inc(pr.unit_done, 1)

            def body(i, prev, keep, abreast=0):
                free = {}
                begun = -1
                if abreast:
                    ready, _, finish = head
                    for n in range(UT):
                        wait_all(pe, [ready[n]])
                        if n < UT - 2:
                            for o in range(abreast):
                                tile_products(outs, o, n, n == 0)
                    for o in range(abreast):
                        for n in range(UT - 2, UT):
                            tile_products(outs, o, n, False)
                    begun = abreast - 1
                    t_fin = finish() if finish else None
                    wait_all(dve, [t_fin])
                for o, tiles in enumerate(outs):
                    parts_o, banks = layout[o % depth]
                    back = o - depth
                    t_free = free[back] if back >= 0 else prev(f"free{back + len(outs)}")
                    if abreast and back < 0 and max(banks) >= 6:
                        t_free = t_fin
                    if not pr.dry and o >= abreast:
                        wait_all(pe, [t_free])
                        for n, (uj, q, k) in enumerate(tiles):
                            tile_products(outs, o, n, uj > begun)
                            begun = max(begun, uj)
                    last_u = tiles[-1][0]
                    for uj in sorted({t[0] for t in tiles}):
                        if not any(t[0] == uj for ts in outs[o + 1:] for t in ts) and uj + LEAD >= abreast:
                            split(pr.unit + uj + LEAD)
                    ready_o = Tok(c_unit, pr.unit + last_u + 1 + DONE0, pr.unit_step, pr.unit_i)
                    free[o] = evac(i, o, banks, ready_o, prev, keep)
                    keep(f"free{o}", free[o])
                    if between:
                        between.pop(0)()
                pr.unit += n_u

            n0, got = 0, dict(before or {})
            while n0 < n_iter and (n0 == 0 and (head or before) or between):
                body(n0, got.get, lambda name, t: got.__setitem__(name, t), head[1] if head and n0 == 0 else 0)
                n0 += 1
            last = pr.unit + (n_iter - n0) * n_u >= n_units
            n1 = n_iter - 1 if last else n_iter
            if n1 > n0:
                got = pr.loop(n1 - n0, lambda i, prev, keep: body(i + n0, prev, keep))
            if last:
                seen = {}
                body(n_iter - 1, lambda name: got.get(name), lambda name, t: seen.__setitem__(name, t))
                got = seen
            return got

        def linear_by_token(u_, n_blocks, evac, after, between=()):
            wait_all(pe, after)
            between, drained = list(between), []
            for g in range(2):
                for j in range(RING):
                    u = pr.unit + j
                    pr.unit_wait(pe, pr.lo_done, u)
                    for kk in range(2):
                        k, cols = 2 * j + kk, slice(kk * 4 * P, (kk + 1) * 4 * P)
                        for b in range(n_blocks):
                            u_h, u_l = u_(k, b)
                            for n, (a_, w_) in enumerate(((u_h, w_hi), (u_l, w_hi), (u_h, w_lo))):
                                ins = pe.matmul(ps[:, 4 * g + b, :], a_, w_[:, u % RING, cols],
                                                start=k == 0 and n == 0, stop=k == DT - 1 and n == 2)
                    ins.then_inc(pr.unit_done, 1)
                    split(u + LEAD)
                    if between:
                        between.pop(0)()
                ready = Tok(c_unit, pr.unit + RING + DONE0)
                free = [evac(g, b, 4 * g + b, ready) for b in range(n_blocks)]
                drained.append(free)
                pr.unit += RING
            return drained

        def rstd_columns(bank, r, n_blocks, after):
            for b in range(n_blocks):
                t = T(after, lambda e: e.transpose(ps[:, bank, b * P:(b + 1) * P], r[:, b * P:(b + 1) * P], ident))
            return V([t], lambda e: e.tensor_copy(rT[:, 0:n_blocks], ps[:, bank, 0:n_blocks * P]
                                                  .rearrange("p (b n) -> p b n", n=P)[:, :, 0:1].rearrange("p b n -> p (b n)")))

        def tokens_out(v_tok):
            def evac(g, b, bank, ready):
                dst = v_tok[:, b, g * 4 * P:(g + 1) * 4 * P]
                if b % 2:
                    return A([ready], lambda e: e.activation(dst, ps[:, bank, :], ACT.Copy, scale=rT[:, b:b + 1]))
                else:
                    return V([ready], lambda e: e.tensor_scalar(dst, ps[:, bank, :], rT[:, b:b + 1], None, ALU.mult))
            return evac

        square_outs = [[(j, q, q) for q in range(UT)] for j in range(RING)]

        def rsqrt_mean(ss_banks, parts, width, dst, after):
            for (c0, c1), b in zip(parts, ss_banks):
                t = A(after + [t_eps], lambda e: e.activation(dst[:, c0:c1], ps[:, b, 0:c1 - c0], ACT.Ln,
                                                    bias=eps[:, 0:1], scale=1.0 / width))
            a, z = parts[0][0], parts[-1][1]
            return A([t], lambda e: e.activation(dst[:, a:z], dst[:, a:z], ACT.Exp, scale=-0.5))

        ONE = [(META, N)]
        TWO = [(0, HALF), (HALF, N)]

        def prenorm(src, gain, parts, after, each=None, dst=None, r_dst=None, sum_=None, abreast=RING, bank=6):
            d_hi, d_lo = dst or (u_hi, u_lo)
            r_dst, sum_ = rstd if r_dst is None else r_dst, acc if sum_ is None else sum_
            a, z = parts[0][0], parts[-1][1]
            t_sum, t_lo = [], []
            for u in range(LEAD, abreast):
                split(pr.unit + u)
            for k in range(DT):
                t_x = each(k) if each else None
                first = after if k == 0 else []
                s_ = sum_[:, a:z] if k == 0 else sq[:, k % 2, a:z]
                t_hi = A(first + [t_x], lambda e: e.activation(d_hi[:, k, a:z], src[:, k, a:z], ACT.Copy, scale=col(gain, k)))
                t_sq = A([t_sum[k - 2] if k >= 2 else None], lambda e: e.activation(s_, src[:, k, a:z], ACT.Square))
                t_lo.append(V(first + [t_hi], lambda e: e.scalar_tensor_tensor(d_lo[:, k, a:z], src[:, k, a:z], col(gain, k),
                                                                       d_hi[:, k, a:z].bitcast(F32), ALU.mult, ALU.subtract)))
                t_sum.append(pr.G([t_sq, t_sum[-1]], lambda e: e.tensor_tensor(sum_[:, a:z], sum_[:, a:z], s_, ALU.add)) if k else t_sq)

            def finish():
                for b, (c0, c1) in enumerate(parts):
                    t = mms([t_sum[-1]], ps[:, bank + b, 0:c1 - c0], [(ones, sum_[:, c0:c1])])
                return rsqrt_mean([bank + b for b in range(len(parts))], parts, D, r_dst, [t])
            return t_lo, abreast, finish

        def u_rhs(k, c0, c1):
            return u_hi[:, k, c0:c1], u_lo[:, k, c0:c1]

        def hid_rhs(k, c0, c1):
            return hid_hi[:, k, c0:c1], hid_lo[:, k, c0:c1]

        def y_evac(y, parts):
            a, z = parts[0][0], parts[-1][1]

            def evac(i, o, banks, ready, prev, keep):
                k = dslice(i, y_evac.per, o, 1)
                for (c0, c1), b in zip(parts, banks):
                    t = A([ready], lambda e: e.activation(y[:, k, c0 - a:c1 - a], ps[:, b:b + 1, 0:c1 - c0], ACT.Copy))
                added = y_evac.added[o - 2] if o >= 2 else prev(f"added{o - 2 + y_evac.per}")
                t2 = V([t, added], lambda e: e.tensor_tensor(sq[:, o % 2:o % 2 + 1, 0:z - a], y[:, k, :], y[:, k, :], ALU.mult))
                y_evac.added[o] = V([t2], lambda e: e.tensor_tensor(acc[:, 0:z - a], acc[:, 0:z - a], sq[:, o % 2, 0:z - a], ALU.add))
                keep(f"added{o}", y_evac.added[o])
                return t
            return evac

        def project_out(y, rhs, after, n_iter=2, outs=square_outs, n_u=RING, parts=ONE):
            t = V(after, lambda e: e.memset(acc[:, :], 0.0))
            y_evac.per, y_evac.added = len(outs), {}
            a = parts[0][0]
            cols = parts if rhs is not hid_rhs else [(0, S)]
            linear(n_iter, outs, n_u, rhs, cols, y_evac(y, cols), after + [t], 4)
            for b, (c0, c1) in enumerate(parts):
                t = mms([pr.now(pr.c_dve)], ps[:, 5 + b, 0:c1 - c0], [(ones, acc[:, c0 - a:c1 - a])])
            return [rsqrt_mean([5, 6], parts, D, rstd_y, [t])]

        def add_tile(y, gain, cols=XS):
            def each(k):
                t = V([], lambda e: e.scalar_tensor_tensor(y[:, k, :], y[:, k, :], col(gain, k), rstd_y[:, cols], ALU.mult, ALU.mult))
                return V([t], lambda e: e.tensor_tensor(x[:, k, cols], x[:, k, cols], y[:, k, :], ALU.add))
            return each

        def scaled_to(dst, per, part=ONE, scale=None):
            def evac(i, o, banks, ready, prev, keep):
                for (c0, c1), b in zip(part, banks):
                    w0 = c0 - part[0][0]
                    v, r_ = dst[:, dslice(i, per, o, 1), w0:w0 + c1 - c0], rstd[:, c0:c1].rearrange("p (o n) -> p o n", o=1)
                    p_ = ps[:, b:b + 1, 0:c1 - c0]
                    if scale is None:
                        t = V([ready], lambda e: e.tensor_tensor(v, p_, r_, ALU.mult))
                    else:
                        t = V([ready], lambda e: e.scalar_tensor_tensor(v, p_, scale, r_, ALU.mult, ALU.mult))
                return t
            return evac

        def add_after(after, y, gain, cols=XS):
            add = add_tile(y, gain, cols)
            def each(k):
                for t in (after if k == 0 else []):
                    t.wait(dve)
                return add(k)
            return each

        def table(name):
            if not pr.dry:
                act.preload_act_table_set(name)

        def transpose_tiles(after, src, dst, n_tok_tiles, tiles, size=P, first=0):
            t_cp = [None, None]
            for b in range(n_tok_tiles):
                for half in range(-(-tiles // 4)):
                    bank = 6 + (b * -(-tiles // 4) + half) % 2
                    ks = range(4 * half, min(4 * half + 4, tiles))
                    for t in after:
                        t.wait(pe)
                    if t_cp[bank - 6] is not None:
                        t_cp[bank - 6].wait(pe)
                    for k in ks:
                        ins = pe.transpose(ps[0:size, bank, (k % 4) * P:(k % 4) * P + P],
                                           src[:, k, first + b * size:first + (b + 1) * size], ident)
                    t = pr.c_pe.add(ins)
                    after = []
                    w = len(ks) * P
                    t_cp[bank - 6] = (A if bank == 6 else V)([t], lambda e: (e.activation(dst[0:size, b, ks[0] * P:ks[0] * P + w], ps[0:size, bank, 0:w], ACT.Copy)
                                                           if bank == 6 else e.tensor_copy(dst[0:size, b, ks[0] * P:ks[0] * P + w], ps[0:size, bank, 0:w])))
            return [t for t in t_cp if t is not None]

        AT = (0, 512, 1024, 896)
        SPAN = 1280

        def mlstm():
            t_pre = prenorm(x, "g00", ONE, [x_in, loaded_first])
            qT, kT, vT, og = area(0, 4, S), area(2048, 4, S), area(4096, 8, S), area(8192, 8, S)
            v_tok = area(12288, 4, D)
            M_bc, floor_bc = area(16384, 4, S), area(18432, 4, S)
            gw = area(20480, DT, 36)
            rows = tmp
            gb = area(20480 + DT * 36, 4)
            sel_all = area(20480 + DT * 36 + 4, ML_H * P)
            gw_hi, gw_lo = (halves(f"gw{n}", 21504 + n * DT * 36, DT, 36) for n in range(2))

            t0 = V([], lambda e: e.memset(gw, 0.0))
            if not pr.dry:
                t0.wait(act)
                act.dma_start(gw[:, :, 0:ML_H], gates_w.rearrange("(k p) n -> p k n", p=P)[:, :, 0:ML_H]).then_inc(s_small, 16)
                act.dma_start(gw[:, :, 32:36], gates_w.rearrange("(k p) n -> p k n", p=P)[:, :, ML_H:]).then_inc(s_small, 16)
                act.dma_start(sel_all, consts_d[:, slice(*CONST["sel"])]).then_inc(s_small, 16)
                act.dma_start(gb[0:ML_H, 0:1], gates_b[0:ML_H, :]).then_inc(s_small, 16)
                act.dma_start(gb[0:ML_H, 1:2], gates_b[ML_H:2 * ML_H, :]).then_inc(s_small, 16)
            gates_in = Tok(c_small, 48 + 80)

            t1 = A([gates_in], lambda e: e.activation(gw_hi, gw, ACT.Copy))
            t_gw = V([t1, gates_in], lambda e: e.tensor_tensor(gw_lo, gw, gw_hi.bitcast(F32), ALU.subtract))
            got = linear(1, square_outs, RING, u_rhs, ONE, scaled_to(qT, 4), [], 4, head=t_pre)
            got = linear(1, square_outs, RING, u_rhs, ONE, scaled_to(kT, 4, scale=ML_DK ** -0.5), [], 4, before=got)
            t_g = mms([t_gw], ps[0:36, 4, :], [(g_[:, k, :], u_[:, k, XS]) for k in range(DT)
                                               for g_, u_ in ((gw_hi, u_hi), (gw_hi, u_lo), (gw_lo, u_hi))])
            t_rT = rstd_columns(5, rstd[:, XS], 4, [])

            ig, lf = rows[0:4, 0, 0:S], rows[0:4, 1, 0:S]
            w1, w2 = rows[0:4, 2, 0:S], rows[0:4, 3, 0:S]
            st = {"t": t_g}
            def step(eng, make, waits=()):
                def do():
                    st["t"] = eng([st["t"], *waits], make)
                return do
            gate_steps = [
                step(V, lambda e: e.tensor_tensor(ig, ps[0:4, 4, :], rstd[0:4, XS], ALU.mult)),
                step(V, lambda e: e.tensor_tensor(rows[32:36, 1, 0:S], ps[32:36, 4, :], rstd[32:36, XS], ALU.mult)),
                step(A, lambda e: e.activation(lf, rows[32:36, 1, 0:S], ACT.Copy))]
            for n, row in ((0, ig), (1, lf)):
                gate_steps += [
                    step(V, lambda e, row=row, n=n: e.tensor_scalar(row, row, gb[0:4, n:n + 1], 1.0 / GATE_CAP, ALU.add, ALU.mult), [gates_in]),
                    step(A, lambda e, row=row: e.activation(row, row, ACT.Tanh)),
                    step(V, lambda e, row=row: e.tensor_scalar(row, row, GATE_CAP, None, ALU.mult))]
            scan_steps = [
                step(A, lambda e: e.activation(w1, lf, ACT.Abs)),
                step(A, lambda e: e.activation(w1, w1, ACT.Exp, scale=-1.0)),
                step(A, lambda e: e.activation(w1, w1, ACT.Ln, bias=1.0)),
                step(V, lambda e: e.scalar_tensor_tensor(lf, lf, 0.0, w1, ALU.min, ALU.subtract)),
                step(V, lambda e: e.tensor_tensor_scan(w2, ones_row(4), lf, 0.0, ALU.mult, ALU.add)),
                step(V, lambda e: e.tensor_tensor(ig, ig, w2, ALU.subtract)),
                step(V, lambda e: e.tensor_tensor_scan(w1, ig, ig, 0.0, ALU.max, ALU.max)),
                step(V, lambda e: e.tensor_tensor(w2, w2, w1, ALU.add)),
                step(A, lambda e: e.activation(w2, w2, ACT.Exp, scale=-1.0))]

            def together(steps):
                return lambda: [do() for do in steps]
            table("sigmoid_and_others")
            to_og = scaled_to(og, 4)
            def og_evac(i, o, banks, ready, prev, keep):
                t = to_og(i, o, banks, ready, prev, keep)
                v = og[:, dslice(i, 4, o, 1), :]
                A([t], lambda e: e.activation(v, v, ACT.Sigmoid))
                return t
            pairs = [together(gate_steps[n:n + 2]) for n in range(0, len(gate_steps), 2)]
            pairs += [lambda: None] * (8 - len(pairs))
            linear(2, square_outs, RING, u_rhs, ONE, og_evac, [], 4, before=got, between=pairs)
            table("natural_log_exp_and_others")
            u_tok = lambda k, b: (u_hi[:, k, META + b * P:META + (b + 1) * P], u_lo[:, k, META + b * P:META + (b + 1) * P])
            drained = linear_by_token(u_tok, 4, tokens_out(v_tok), [pr.now(pr.c_dve)], [together(scan_steps[n:n + 2]) for n in range(0, len(scan_steps), 2)])
            t_F = st["t"]
            t_row = drained[0]
            for h in range(ML_H):
                sel = sel_all[0:4, h * P:(h + 1) * P]
                b = 2 * (h % 2)
                t1 = mms([t_F, t_row[b]], ps[:, b, :], [(sel, w1)])
                t_row[b] = V([t1], lambda e: e.tensor_copy(M_bc[:, h, :], ps[:, b, :]))
                t2 = mms([t_row[b + 1]], ps[:, b + 1, :], [(sel, w2)])
                t_row[b + 1] = A([t2], lambda e: e.activation(floor_bc[:, h, :], ps[:, b + 1, :], ACT.Copy))
            for b in range(4):
                t2 = T([t_row[0]], lambda e: e.transpose(ps[:, 0, 4 * b:4 * b + 4], rows[0:4, 0, b * P:(b + 1) * P], ident[0:4, 0:4]))
            t_u = V([t2], lambda e: e.tensor_copy(uT[:, :, :], ps[:, 0, 0:16].rearrange("p (b h) -> p b h", h=4)))

            weights, k_h, u_h = area(4096, 2, SPAN), area(6656, 2, S), area(7680, 2, 4)
            v_h, hT = area(20480, 8, ML_DV), area(22528, 4, S)
            den = [acc[:, 0:S], rstd_y[:, 0:S]]
            flat = ps[:, :, :].rearrange("p b n -> p (b n)")
            one = lambda v: v.rearrange("p (o n) -> p o n", o=1)

            def two_heads(i, prev, keep):
                t_k, t_v, t_w, t_s, t_n, t_q, t_r = {}, {}, {}, {}, {}, {}, {}
                B0 = lambda j: 3 * j
                for j in range(2):
                    at = lambda v: v[:, dslice(i, 2, j, 1), :]
                    t_k[j] = A([prev(f"n{j}")], lambda e: e.activation(one(k_h[:, j, :]), at(kT), ACT.Copy))
                    t_u = V([prev(f"n{j}")], lambda e: e.tensor_copy(u_h[:, j, :], uT[:, :, dslice(i, 2, j, 1)].rearrange("p b o -> p (b o)")))
                    for b in range(4):
                        t_w[j] = V([t_u, prev(f"n{j}")], lambda e: e.scalar_tensor_tensor(one(weights[:, j, AT[b]:AT[b] + S - b * P]), at(M_bc)[:, :, b * P:S],
                                                                   u_h[:, j, b:b + 1], zeros_like(S - b * P), ALU.subtract, ALU.max))
                    if not pr.dry:
                        wait_all(pe, [t_k[j], prev(f"h{j}")])
                        for b in range(4):
                            a0 = 512 * B0(j) + AT[b]
                            ins = pe.matmul(flat[:, a0:a0 + S - b * P], k_h[:, j, b * P:(b + 1) * P], at(qT)[:, :, b * P:S].rearrange("p o n -> p (o n)"),
                                            start=b != 3, stop=b != 1, skip_group_check=True)
                    t_s[j] = pr.c_pe.add(None if pr.dry else ins)
                for j in range(2):
                    w = weights[:, j, :]
                    t_w[j] = A([t_w[j]], lambda e: e.activation(w, w, ACT.Exp, scale=-1.0))
                    t_v[j] = A([prev(f"n{j}")], lambda e: e.activation(v_h[:, 4 * j:4 * j + 4, :], v_tok[:, :, dslice(i, 2 * ML_DV, j * ML_DV, ML_DV)], ACT.Copy))
                for j in range(2):
                    w, b0 = weights[:, j, :], 512 * B0(j)
                    t = V([t_w[j], t_s[j]], lambda e: e.tensor_tensor(w, flat[:, b0:b0 + SPAN], w, ALU.mult))
                    for b in range(4):
                        d = weights[:, j, AT[b]:AT[b] + P]
                        t_w[j] = V([t], lambda e: e.tensor_tensor(d, d, const("causal"), ALU.mult))
                    for n, lhs in enumerate((lambda b: ones, lambda b: v_h[:, 4 * j + b, 0:P], lambda b: v_h[:, 4 * j + b, P:2 * P])):
                        if not pr.dry:
                            wait_all(pe, [t_w[j], t_v[j]])
                            for b in range(4):
                                ins = pe.matmul(ps[:, B0(j) + n, b * P:S], lhs(b), weights[:, j, AT[b]:AT[b] + S - b * P],
                                                start=b == 0, stop=b == 3, skip_group_check=True)
                        t_n[j, n] = pr.c_pe.add(None if pr.dry else ins)
                    keep(f"n{j}", t_n[j, 2])
                for j in range(2):
                    at = lambda v: v[:, dslice(i, 2, j, 1), :]
                    h_, b0 = hT[:, 2 * j:2 * j + 2, :], B0(j)
                    t = A([t_n[j, 0], prev(f"den{j}")], lambda e: e.activation(den[j], ps[:, b0, :], ACT.Abs))
                    t = V([t], lambda e: e.tensor_tensor(one(den[j]), one(den[j]), at(floor_bc), ALU.max))
                    t = V([t], lambda e: e.reciprocal(den[j], den[j]))
                    t_h = V([t, t_n[j, 2], prev(f"den{j}")], lambda e: e.tensor_tensor(h_, ps[:, b0 + 1:b0 + 3, :], one(den[j]).broadcast_to([P, 2, S]), ALU.mult))
                    keep(f"h{j}", t_h)
                    t_sq = A([t_h, t_q.get(0) or prev("ss")], lambda e: e.activation(sq[:, :, 0:S], h_, ACT.Square))
                    t_q[j] = mms([t_sq], ps[:, 6 + j, :], [(ones, sq[:, 0, 0:S]), (ones, sq[:, 1, 0:S])])
                    keep("ss", t_q[j])
                    t_r[j] = rsqrt_mean([6 + j], [(0, S)], ML_DV, den[j], [t_q[j]])
                    t_h = pr.G([t_sq], lambda e: e.tensor_tensor(h_, h_, og[:, dslice(i, 4, 2 * j, 2), :], ALU.mult))
                    t_w[j] = t_h
                for j in range(2):
                    h_ = hT[:, 2 * j:2 * j + 2, :]
                    t = V([t_r[j], t_w[j]], lambda e: e.tensor_tensor(h_, h_, one(den[j]).broadcast_to([P, 2, S]), ALU.mult))
                    for n in range(2):
                        kk, hn = dslice(i, 4, 2 * j + n, 1), one(hT[:, 2 * j + n, :])
                        gain = vecs[:, dslice(i, 4, VEC["ml_head"] * DT + 2 * j + n, 1)]
                        t = V([t], lambda e: e.tensor_scalar(hn, hn, gain, None, ALU.mult))
                        t2 = A([t], lambda e: e.activation(u_hi[:, kk, XS], hn, ACT.Copy))
                        t3 = V([t2], lambda e: e.tensor_tensor(u_lo[:, kk, XS], hn, u_hi[:, kk, XS].bitcast(F32), ALU.subtract))
                    keep(f"den{j}", t3)
            all_wait()
            pr.loop(ML_H // 2, two_heads)
            y = area(0, 8, S)
            return y, project_out(y, u_rhs, pr.all_done())

        V([], lambda e: e.memset(zrow[:, :], 0.0))
        def all_wait():
            ts = pr.all_done()
            for e in (pe, act, dve, pool):
                wait_all(e, ts)

        zeros_like = lambda w: zrow[:, 0:1].broadcast_to([P, w])
        ones_row = lambda n: const("ones")[0:n, 0:1].broadcast_to([n, S])

        def finish(src):
            ts = pr.all_done()
            for t in ts:
                t.wait(sp)
            sp.dma_start(out.rearrange("(k p) n -> p k n", p=P), src).then_inc(s_out, 16)
            sp.wait_ge(s_out, 16)

        y, t_y = mlstm()

        def attend_memory(layer, y_in, t_y):
            mem_in, kv = area(8192, DT, MEM), area(10240, 16, MEM)
            v_tok, qT = area(14336, 2, D), area(16384, 8, S)
            Pn, pT = area(20480, 4, MEM), area(21504, 2, S)
            q_h, v_h = area(8192, 2, S), area(9216, 2, XA_D)
            for t in pr.all_done():
                t.wait(act)
            act.dma_start(mem_in, memT.rearrange("(k p) n -> p k n", p=P)).then_inc(s_mem, 16)
            t_mem = Tok(c_meml, 16 * (layer + 1))
            head_in = prenorm(mem_in, "mem", [(0, MEM)], pr.all_done() + [t_mem])
            linear(4, square_outs, RING, u_rhs, [(0, MEM)], scaled_to(kv, 4, [(0, MEM)]), [], 4, head=head_in)
            head_in = prenorm(x, f"g{layer}2", ONE, pr.all_done(), each=add_after(t_y + pr.all_done(), y_in, f"g{layer}1"))
            linear(2, square_outs, RING, u_rhs, ONE, scaled_to(qT, 4), [], 4, head=head_in)
            kT = kv[:, 0:DT, :]
            transpose_tiles(pr.all_done(), kv[:, DT:, :], v_tok, 2, DT)
            for t in pr.all_done():
                for e in (pe, act, dve):
                    t.wait(e)
            scale = XA_D ** -0.5
            mx, sm = tmp[:, 0, 0:4], tmp[:, 1, 0:4]

            def head(h, prev, keep):
                t_q = V([prev("scores")], lambda e: e.tensor_copy(q_h, qT[:, dslice(h, 2, 0, 2), :]))
                t_v = A([prev("pv")], lambda e: e.activation(v_h, v_tok[:, :, dslice(h, XA_D, 0, XA_D)], ACT.Copy))
                for b in range(4):
                    t_s = mms([t_q, prev("exp")], ps[:, b // 2, (b % 2) * MEM:(b % 2 + 1) * MEM],
                              [(q_h[:, j, b * P:(b + 1) * P], kT[:, dslice(h, 2, j, 1), :].rearrange("p o n -> p (o n)")) for j in range(2)])
                keep("scores", t_s)
                sc = lambda b: ps[:, b // 2, (b % 2) * MEM:(b % 2 + 1) * MEM]
                t = V([t_s, prev("exp")], lambda e: e.tensor_reduce(mx, ps[:, 0:2, :].rearrange("p c (b n) -> p (c b) n", n=MEM), AX.X, ALU.max))
                t = V([t], lambda e: e.tensor_scalar(mx, mx, -scale, None, ALU.mult))
                for b in range(4):
                    t_e = A([t, prev("pT")], lambda e: e.activation(Pn[:, b, :], sc(b), ACT.Exp, bias=mx[:, b:b + 1], scale=scale, accum_out=sm[:, b:b + 1]))
                keep("exp", t_e)
                t = V([t_e], lambda e: e.reciprocal(sm, sm))
                for b in range(4):
                    t_n = V([t], lambda e: e.tensor_scalar(Pn[:, b, :], Pn[:, b, :], sm[:, b:b + 1], None, ALU.mult))
                for j in range(2):
                    if not pr.dry:
                        t_n.wait(pe)
                        if prev("pT"):
                            prev("pT").wait(pe)
                        for b in range(4):
                            ins = pe.transpose(ps[:, 2 + j, b * P:(b + 1) * P], Pn[:, b, j * P:(j + 1) * P], ident)
                        ins_ = ins
                    else:
                        ins_ = None
                    t_tr = pr.c_pe.add(ins_)
                    if j == 0:
                        t_c0 = V([t_tr, prev("pv")], lambda e: e.tensor_copy(pT[:, 0, :], ps[:, 2, :]))
                    else:
                        t_c1 = A([t_tr, prev("pv")], lambda e: e.activation(pT[:, 1, :], ps[:, 3, :], ACT.Copy))
                keep("pT", t_tr)
                for j in range(2):
                    t_o = mms([t_c0, t_c1, t_v, prev(f"out{j}")], ps[:, 4 + j, :], [(v_h[:, b, j * P:(j + 1) * P], pT[:, b, :]) for b in range(2)])
                    k = dslice(h, 2, j, 1)
                    t_h = A([t_o], lambda e: e.activation(u_hi[:, k, XS], ps[:, 4 + j:5 + j, :], ACT.Copy))
                    t = V([t_h], lambda e: e.tensor_tensor(u_lo[:, k, XS], ps[:, 4 + j:5 + j, :], u_hi[:, k, XS].bitcast(F32), ALU.subtract))
                    keep(f"out{j}", t)
                keep("pv", t_o)
                keep("copied", t_c1)
            pr.loop(XA_H, head)
            y = area(0, 8, S)
            return y, project_out(y, u_rhs, pr.all_done())

        FFN_OUTS = [[(o * DOWN_UNITS + k // UT, k % UT, k) for k in range(FT)] for o in range(4)]

        def store_split(t, v, k):
            t2 = A([t], lambda e: e.activation(hid_hi[:, k, :], v, ACT.Copy))
            return V([t2], lambda e: e.tensor_tensor(hid_lo[:, k, :], v, hid_hi[:, k, :].bitcast(F32), ALU.subtract))

        def ffn(layer, y_in, t_y):
            head_in = prenorm(x, f"g{layer}4", ONE, pr.all_done(), each=add_after(t_y + pr.all_done(), y_in, f"g{layer}3"))
            rs = rstd[:, XS]

            def evac(i, o, banks, ready, prev, keep):
                f = o // 2
                g, w = tmp[:, 2 * f, 0:S], tmp[:, 2 * f + 1, 0:S]
                bank = ps[:, banks[0], :]
                if o % 2 == 0:
                    t = V([ready, prev(f"h{f}")], lambda e: e.tensor_tensor(g, bank, rs, ALU.mult))
                    evac.silu = A([t], lambda e: e.activation(g, g, ACT.Silu))
                    return t
                t = V([ready, prev(f"hi{f}")], lambda e: e.tensor_tensor(w, bank, rs, ALU.mult))
                t2 = V([evac.silu, t], lambda e: e.tensor_tensor(w, w, g, ALU.mult))
                keep(f"h{f}", t2)
                k = dslice(i, 2, f, 1)
                one = w.rearrange("p (o n) -> p o n", o=1)
                keep(f"hi{f}", store_split(t2, one, k))
                return t
            linear(FT // 2, square_outs, RING, u_rhs, ONE, evac, [], 4, head=head_in)
            return y_ffn, project_out(y_ffn, hid_rhs, pr.all_done(), 2, FFN_OUTS, 4 * DOWN_UNITS)

        y, t_y = attend_memory(0, y, t_y)
        y, t_y = ffn(0, y, t_y)


        def stick_breaking(y_in, t_y):
            head_in = prenorm(x, "g10", ONE, pr.all_done(), each=add_after(t_y + pr.all_done(), y_in, "g05"))
            qT, kT, vT = area(0, 8, S), area(4096, 8, S), area(8192, 8, S)
            v_tok = area(12288, 4, D)
            sp_, aT = area(16384, 2, SPAN), area(18944, 2, SPAN)
            sp_hi, sp_lo = halves("sp_hi", 8192, 2, SPAN), halves("sp_lo", 16384, 2, SPAN)
            q_p, k_p, v_p = area(10752, S), area(11264, S), area(21504, 4, P)
            sums_c = sb("sums_c", [P, 4 * P], F32R, over=acc_at)
            linear(2, square_outs, RING, u_rhs, ONE, scaled_to(qT, 4, scale=SB_D ** -0.5), [], 4, head=head_in)
            linear(4, square_outs, RING, u_rhs, ONE, scaled_to(area(4096, 16, S), 4), [], 4)
            table("natural_log_exp_and_others")
            transpose_tiles(pr.all_done(), vT, v_tok, 4, DT)
            t_all = pr.all_done()
            for n, name in enumerate(("neg_ones", "neg_suffix", "ident", "neg_fill")):
                A(t_all, lambda e: e.activation(sums_c[:, n * P:(n + 1) * P], const(name), ACT.Copy))
            neg_ones, neg_suffix, ident_r, neg_fill = (sums_c[:, n * P:(n + 1) * P] for n in range(4))
            all_wait()
            one = lambda v: v.rearrange("p (o n) -> p o n", o=1)
            flat = ps[:, :, :].rearrange("p b n -> p (b n)")
            scores = lambda h: flat[:, 3 * 512 * h:3 * 512 * h + SPAN]
            block = lambda h, b, skip=0: flat[:, 3 * 512 * h + AT[b] + skip:3 * 512 * h + AT[b] + S - b * P]

            def operands(i, t):
                pr.G([t("z1")], lambda e: e.tensor_copy(one(q_p), qT[:, dslice(i, 1, 0, 1), :]))
                t["qk"] = pr.G([], lambda e: e.tensor_copy(one(k_p), kT[:, dslice(i, 1, 0, 1), :]))

            def v_operand(i, t):
                t["v"] = pr.G([t("av1")], lambda e: e.tensor_copy(v_p, v_tok[:, :, dslice(i, P, 0, P)]))

            def scores_of(h, t):
                R = slice(64 * h, 64 * h + 64)
                if not pr.dry:
                    wait_all(pe, [t("qk"), t(f"a_0{h}")])
                    for b in range(4):
                        if b == 1:
                            wait_all(pe, [t(f"a{h}")])
                        ins = pe.matmul(block(h, b), k_p[R, b * P:(b + 1) * P], q_p[R, b * P:S],
                                        start=b != 3, stop=False, skip_group_check=True)
                t[f"z{h}"] = pr.c_pe.add(None if pr.dry else ins)

            def softplus(h, t):
                v = sp_[:, h, :]
                t1 = A([t(f"z{h}"), t(f"c{h}")], lambda e: e.activation(v, scores(h), ACT.Abs))
                t1 = A([t1], lambda e: e.activation(v, v, ACT.Exp, scale=-1.0))
                t1 = A([t1], lambda e: e.activation(v, v, ACT.Ln, bias=1.0))
                t1 = V([t1], lambda e: e.scalar_tensor_tensor(v, scores(h), 0.0, v, ALU.max, ALU.add))
                for b in range(4):
                    d = v[:, AT[b]:AT[b] + P]
                    t[f"sp{h}"] = V([t1], lambda e: e.tensor_tensor(d, d, const("strict"), ALU.mult))

            def softplus_halves(h, t):
                t1 = A([t(f"sp{h}")], lambda e: e.activation(sp_hi[:, h, :], sp_[:, h, :], ACT.Copy))
                t[f"lo{h}"] = V([t1], lambda e: e.tensor_tensor(sp_lo[:, h, :], sp_[:, h, :], sp_hi[:, h, :].bitcast(F32), ALU.subtract))

            def sums(h, t):
                if not pr.dry:
                    wait_all(pe, [t(f"lo{h}")])
                    for b in range(4):
                        for part in (sp_hi, sp_lo):
                            for j in range(3, b, -1):
                                pe.matmul(block(h, b, (j - b) * P), neg_ones, part[:, h, AT[j]:AT[j] + S - j * P],
                                          start=False, stop=False, skip_group_check=True)
                            pe.matmul(block(h, b), neg_suffix, part[:, h, AT[b]:AT[b] + S - b * P],
                                      start=False, stop=False, skip_group_check=True)
                        ins = pe.matmul(block(h, b)[:, 0:P], ident_r, neg_fill, start=False, stop=True, skip_group_check=True)
                t[f"c{h}"] = pr.c_pe.add(None if pr.dry else ins)

            def weights(h, t):
                t[f"a_0{h}"] = A([t(f"c{h}"), t(f"av{h}")], lambda e: e.activation(aT[:, h, 0:512], scores(h)[:, 0:512], ACT.Exp))
                t[f"a{h}"] = A([], lambda e: e.activation(aT[:, h, 512:SPAN], scores(h)[:, 512:SPAN], ACT.Exp))

            def times_v(h, t, blocks=(0, 1, 2, 3)):
                if not pr.dry:
                    wait_all(pe, [t(f"a{h}"), t("v"), t("out")])
                    for b in blocks:
                        ins = pe.matmul(ps[64 * h:64 * h + 64, 6, b * P:S], v_p[:, b, 64 * h:64 * h + 64],
                                        aT[:, h, AT[b]:AT[b] + S - b * P], start=b == 0, stop=b == 3, skip_group_check=True)
                t[f"av{h}"] = pr.c_pe.add(None if pr.dry else ins)

            def output(i, t):
                k = dslice(i, 1, 0, 1)
                t1 = A([t("av1")], lambda e: e.activation(u_hi[:, k, XS], ps[:, 6:7, :], ACT.Copy))
                t["out"] = V([t1], lambda e: e.tensor_tensor(u_lo[:, k, XS], ps[:, 6:7, :], u_hi[:, k, XS].bitcast(F32), ALU.subtract))

            class Last(dict):
                def __init__(self, prev):
                    self.prev = prev
                def __call__(self, name):
                    return self[name] if name in self else self.prev(name)

            def pair(i, t, more):
                v_operand(i, t)
                scores_of(0, t)
                softplus(0, t)
                times_v(0, t, (0, 1))
                sums(1, t)
                times_v(0, t, (2, 3))
                weights(1, t)
                softplus_halves(0, t)
                scores_of(1, t)
                if more:
                    operands(i + 2, t)
                softplus(1, t)
                times_v(1, t, (0, 1))
                sums(0, t)
                times_v(1, t, (2, 3))
                weights(0, t)
                softplus_halves(1, t)
                output(i, t)

            def looped_pair(i, prev, keep):
                t = Last(prev)
                pair(i, t, True)
                for name in t:
                    keep(name, t[name])

            first = Last(lambda name: None)
            operands(0, first)
            for h in range(2):
                scores_of(h, first)
            operands(1, first)
            for h in range(2):
                softplus(h, first)
                softplus_halves(h, first)
            sums(0, first)
            weights(0, first)
            all_wait()
            got = pr.loop(SB_H // 2 - 2, looped_pair)
            last, i = Last(got.get), SB_H // 2 - 1
            pair(i - 1, last, False)
            v_operand(i, last)
            sums(1, last)
            times_v(0, last)
            weights(1, last)
            times_v(1, last)
            output(i, last)
            y = area(0, 8, S)
            return y, project_out(y, u_rhs, pr.all_done())

        y, t_y = stick_breaking(y, t_y)
        y, t_y = attend_memory(1, y, t_y)
        y, t_y = ffn(1, y, t_y)

        z_hi, z_lo = halves("z_hi", 0, DT, N), halves("z_lo", DT * N, DT, N)
        PAIRS = [(P_, b_) for P_, b_ in ((TWO, [0, 1]), (TWO, [2, 3]), (TWO, [4, 5]), (TWO, [6, 7]))]
        HN = HG_H * N

        def mix(y_in, t_y):
            table("natural_log_exp_and_others")
            head_in = prenorm(x, "mix_pre", TWO, pr.all_done(), each=add_after(t_y + pr.all_done(), y_in, "g15"), abreast=3)
            proj = area(0, 20, N)
            q, f, iT, g, vp = (proj[:, 4 * n:4 * n + 4, :] for n in range(5))
            flat = lambda n: area(n * HN, HN)
            kT, aT = area(5 * HN, 4, N), area(6 * HN, 4, N)
            work = 7 * HN
            masks = area(work, len(LEVELS), P).bitcast(I32)
            reset, reset_m = area(work + 896, HG_H * P), area(work + 1408, HG_H * META)
            inv = area(work + 1472, 4, META)
            pool_w_sb = area(work + 1536, 4, P)
            at = work + 2048
            bufs = {}
            for name in ("q_s", "k_s", "l_s", "b", "e0", "e1", "ac0", "ac1", "sc", "state", "i_tok", "k_tok", "o_s"):
                bufs[name] = area(at, HG_H * P)
                at += HG_H * P
            t_all = pr.all_done()
            wait_all(act, t_all)
            for dst, src in ((area(work, 896), masks_d), (area(work + 896, 640), consts_d[:, CONST["reset"][0]:CONST_ALL]),
                             (area(work + 1536, 512), pool_w)):
                act.dma_start(dst.bitcast(I32) if src is masks_d else dst, src).then_inc(s_small, 16)
            loaded = Tok(c_small, 48 + 80 + 48)
            linear(5, square_outs, RING, u_rhs, TWO, scaled_to(proj, 4, TWO), [], 4, head=head_in)
            t_all = pr.all_done()

            low = vecs[:, len(VEC) * DT + 4 * HALF_VEC["lower"]:len(VEC) * DT + 4 * HALF_VEC["lower"] + 4]
            lb, lb1, gam = tmp_small(0), tmp_small(1), tmp_small(2)
            t = V(t_all, lambda e: e.tensor_tensor(gam, low, low, ALU.subtract))
            t = A([t], lambda e: e.activation(gam, gam, ACT.Exp))
            t = V([t], lambda e: e.reciprocal(lb, gam))
            t = V([t], lambda e: e.tensor_tensor(gam, gam, lb, ALU.mult))
            t = V([t], lambda e: e.tensor_tensor(lb, gam, gam, ALU.subtract))
            t = V([t], lambda e: e.tensor_scalar(lb, lb, 0.0, 1.0, ALU.max, ALU.min))
            t_lb = V([t], lambda e: e.tensor_scalar(lb1, lb, -1.0, 1.0, ALU.mult, ALU.add))

            table("sigmoid_and_others")
            t_k = A(t_all, lambda e: e.activation(flat(5), flat(1), ACT.Sigmoid, scale=-1.0))
            t_f = A([t_k], lambda e: e.activation(flat(1), flat(1), ACT.Sigmoid))
            A([], lambda e: e.activation(flat(3), flat(3), ACT.Sigmoid))
            for h in range(HG_H):
                V([t_k, t_lb], lambda e: e.tensor_scalar(kT[:, h, :], kT[:, h, :], lb1[:, h:h + 1], None, ALU.mult))
                t = V([t_f, t_lb], lambda e: e.tensor_scalar(f[:, h, :], f[:, h, :], lb1[:, h:h + 1], lb[:, h:h + 1], ALU.mult, ALU.add))
            low_f = area(6 * HN, HN)
            t = V([t], lambda e: e.tensor_scalar(low_f, flat(1), 1e-30, 2.0 ** 60, ALU.max, ALU.mult))
            t = V([t], lambda e: e.tensor_scalar(low_f, low_f, 1.0, None, ALU.min))
            t = V([t], lambda e: e.tensor_scalar(flat(1), flat(1), 2.0 ** -60, None, ALU.max))
            table("natural_log_exp_and_others")
            t = A([t], lambda e: e.activation(low_f, low_f, ACT.Ln))
            t = A([t], lambda e: e.activation(flat(1), flat(1), ACT.Ln))
            t_l = V([t], lambda e: e.tensor_tensor(flat(1), flat(1), low_f, ALU.add))

            wait_all(dve, [loaded])
            for gi, width in enumerate(WINDOWS):
                src, d, n = vp[:, gi, :], 1, 0
                while d < width:
                    dst = sq[:, n % 2, :]
                    t = V([t_l], lambda e: e.tensor_copy(dst[:, 0:d], src[:, 0:d]))
                    t = V([t], lambda e: e.tensor_tensor(dst[:, d:N], src[:, d:N], src[:, 0:N - d], ALU.add))
                    t_l, src, d, n = t, dst, 2 * d, n + 1
                t = V([t], lambda e: e.tensor_tensor(src[:, 0:META], src[:, 0:META], inv[:, gi, :], ALU.mult))
                t = V([t], lambda e: e.tensor_scalar(src[:, META:N], src[:, META:N], 1.0 / width, None, ALU.mult))
                t = V([t], lambda e: e.tensor_tensor(src, src, vp[:, gi, :], ALU.subtract))
                for b, (c0, c1) in enumerate(TWO):
                    t_m = mms([t, loaded], ps[:, b, 0:HALF], [(pool_w_sb[:, gi, :], src[:, c0:c1])])
                for b, (c0, c1) in enumerate(TWO):
                    t = V([t_m], lambda e: e.tensor_scalar(vp[:, gi, c0:c1], ps[:, b, 0:HALF], half_col("pool_scale", gi), None, ALU.mult))
                t_l = t

            def tile(T, cols, first, prev, keep):
                w = HG_H * T
                r2 = lambda v: v[:, 0:w]
                r3 = lambda v: v[:, 0:w].rearrange("p (h t) -> p h t", h=HG_H)
                q_s, k_s, l_s, b = (bufs[n] for n in ("q_s", "k_s", "l_s", "b"))
                state, i_tok, k_tok, o_s, sc = (bufs[n] for n in ("state", "i_tok", "k_tok", "o_s", "sc"))
                ee, ac = [bufs["e0"], bufs["e1"]], [bufs["ac0"], bufs["ac1"]]
                t_q = V([prev("end")], lambda e: e.tensor_copy(r3(q_s), q[:, :, cols]))
                t_kk = V([], lambda e: e.tensor_copy(r3(k_s), kT[:, :, cols]))
                t_i = A([prev("end")], lambda e: e.activation(r3(o_s), iT[:, :, cols], ACT.Copy))
                t = V([], lambda e: e.tensor_copy(r3(l_s), f[:, :, cols]))
                t_b = V([t], lambda e: e.tensor_tensor_scan(r2(b), (reset if T == P else reset_m)[:, 0:w], r2(l_s), 0.0, ALU.mult, ALU.add))
                wait_all(pe, [] if pr.dry else [t_kk, prev("end"), prev("end_a")])
                def heads(bank, lhs, rhs, M):
                    if pr.dry:
                        return pr.c_pe.add(None)
                    for h in range(HG_H):
                        ins = pe.matmul(ps[0:M, bank, h * T:(h + 1) * T], lhs(h), rhs(h), start=True, stop=True)
                    return pr.c_pe.add(ins)
                hd = lambda v, h: v[:, h * T:(h + 1) * T]
                t_d = heads(2, lambda h: hd(k_s, h), lambda h: hd(q_s, h), T)
                bc = lambda v: v.rearrange("p (o t) -> p o t", o=1).broadcast_to([T, HG_H, T])
                sc3 = sc[0:T, 0:w].rearrange("p (h t) -> p h t", h=HG_H)
                t_sc = V([t_d], lambda e: e.tensor_tensor(sc3, ps[0:T, 2, 0:w].rearrange("p (h t) -> p h t", h=HG_H), bc(ident[0:T, 0:T]), ALU.mult))
                def turned(bank, src, dst, after, on):
                    if not pr.dry:
                        wait_all(pe, after)
                        for h in range(HG_H):
                            ins = pe.transpose(ps[0:T, bank, h * P:(h + 1) * P], hd(src, h), ident)
                    t = pr.c_pe.add(None if pr.dry else ins)
                    return A([t], lambda e: e.activation(dst[0:T, :], ps[0:T, bank, :], ACT.Copy))
                t_it = turned(3, o_s, i_tok, [t_i], A)
                t_ac, t_mask = [], []
                def masked(n):
                    return V([], lambda e: e.copy_predicated(sc3, bc(masks[0:T, n, 0:T]), ps[0:T, n % 2, 0:w].rearrange("p (h t) -> p h t", h=HG_H)))
                for n, B in enumerate(l_ for l_ in LEVELS if l_ <= T):
                    nb, hb = w // B, B // 2
                    blk = lambda v: v[:, 0:w].rearrange("p (n b) -> p n b", b=B)
                    e_, a_ = ee[n % 2], ac[n % 2]
                    t = V([t_b, t_ac[n - 2] if n >= 2 else None], lambda e: e.tensor_tensor(blk(e_), blk(b), blk(b)[:, :, hb - 1:hb].broadcast_to([P, nb, B]), ALU.subtract))
                    A([t], lambda e: e.activation(blk(e_)[:, :, 0:hb], blk(e_)[:, :, 0:hb], ACT.Exp, scale=-1.0))
                    t = A([], lambda e: e.activation(blk(e_)[:, :, hb:B], blk(e_)[:, :, hb:B], ACT.Exp))
                    V([t, t_mask[n - 2] if n >= 2 else None], lambda e: e.tensor_tensor(blk(a_)[:, :, 0:hb], blk(k_s)[:, :, 0:hb], blk(e_)[:, :, 0:hb], ALU.mult))
                    t = V([t_m, t_sc] if n else [], lambda e: e.tensor_tensor(blk(a_)[:, :, hb:B], blk(q_s)[:, :, hb:B], blk(e_)[:, :, hb:B], ALU.mult))
                    t_ac.append(t)
                    if n:
                        t_sc = masked(n - 1)
                        t_mask.append(t_sc)
                    if not pr.dry:
                        wait_all(pe, [t, t_mask[n - 2] if n >= 2 else None])
                    t_m = heads(n % 2, lambda h: hd(a_, h), lambda h: hd(a_, h), T)
                last = r3(b)[:, :, T - 1:T]
                t = V([t_ac[-1], t_m, t_sc], lambda e: e.tensor_tensor(r3(ee[0]), last.broadcast_to([P, HG_H, T]), r3(b), ALU.subtract))
                t_sc = masked(n)
                A([t], lambda e: e.activation(r2(ee[0]), r2(ee[0]), ACT.Exp))
                A([], lambda e: e.activation(small_e, last.rearrange("p h o -> p (h o)"), ACT.Exp))
                t = A([], lambda e: e.activation(r2(ee[1]), r2(b), ACT.Exp))
                V([t, t_sc], lambda e: e.tensor_tensor(r2(ac[0]), r2(k_s), r2(ee[0]), ALU.mult))
                t = V([], lambda e: e.tensor_tensor(r2(ac[1]), r2(q_s), r2(ee[1]), ALU.mult))
                t_kt = turned(4, ac[0], k_tok, [t], A)
                if not pr.dry:
                    wait_all(pe, [t_sc, t_it, t_kt, t])
                    for h in range(HG_H):
                        pe.matmul(ps[:, 5, h * T:(h + 1) * T], i_tok[0:T, h * P:(h + 1) * P], sc[0:T, h * T:(h + 1) * T], start=True, stop=first)
                        if not first:
                            ins = pe.matmul(ps[:, 5, h * T:(h + 1) * T], state[:, h * P:(h + 1) * P], hd(ac[1], h), start=False, stop=True)
                    for h in range(HG_H):
                        ins = pe.matmul(ps[:, 6, h * P:(h + 1) * P], k_tok[0:T, h * P:(h + 1) * P], i_tok[0:T, h * P:(h + 1) * P], start=True, stop=True)
                t_o = pr.c_pe.add(None if pr.dry else ins)
                for h in range(HG_H):
                    hs = slice(h * P, (h + 1) * P)
                    if first:
                        t_st = V([t_o], lambda e: e.tensor_copy(state[:, hs], ps[:, 6, hs]))
                    else:
                        t_st = V([t_o], lambda e: e.scalar_tensor_tensor(state[:, hs], state[:, hs], small_e[:, h:h + 1], ps[:, 6, hs], ALU.mult, ALU.add))
                t = A([t_o], lambda e: e.activation(r2(o_s), ps[:, 5, 0:w], ACT.Copy))
                t = A([t], lambda e: e.activation(sq[:, 0, 0:w], r2(o_s), ACT.Square))
                t = mms([t], ps[:, 7, 0:w], [(ones, sq[:, 0, 0:w])])
                t = rsqrt_mean([7], [(0, w)], P, sq[:, 1, :], [t])
                t = V([t], lambda e: e.tensor_tensor(r2(o_s), r2(o_s), sq[:, 1, 0:w], ALU.mult))
                for h in range(HG_H):
                    t2 = V([t], lambda e: e.tensor_scalar(hd(o_s, h), hd(o_s, h), half_col("hg_out", h), None, ALU.mult))
                t = V([t2], lambda e: e.tensor_tensor(aT[:, :, cols], r3(o_s), g[:, :, cols], ALU.mult))
                keep("end", t)
                keep("end_a", pr.now(pr.c_act))

            ts = pr.all_done()
            for e in (pe, act, dve):
                wait_all(e, ts)
            tile(META, slice(0, META), True, lambda n: None, lambda n, t: None)
            ts = pr.all_done()
            for e in (pe, act, dve):
                wait_all(e, ts)
            pr.loop(S // P, lambda i, prev, keep: tile(P, dslice(i, P, META, P), False, prev, keep))

            table("sigmoid_and_others")
            sg = area(7 * HN, 16, N)
            to_sg = scaled_to(sg, 4, TWO)
            def sg_evac(i, o, banks, ready, prev, keep):
                t = to_sg(i, o, banks, ready, prev, keep)
                v = sg[:, dslice(i, 4, o, 1), :]
                A([t], lambda e: e.activation(v, v, ACT.Sigmoid))
                return t
            linear(4, square_outs, RING, u_rhs, TWO, sg_evac, pr.all_done(), 4)
            for k in range(DT):
                src = aT[:, k, :] if k < 4 else vp[:, k - 4, :]
                t = A(pr.all_done() if k == 0 else [], lambda e: e.activation(u_hi[:, k, :], src, ACT.Copy))
                V([t], lambda e: e.tensor_tensor(u_lo[:, k, :], src, u_hi[:, k, :].bitcast(F32), ALU.subtract))

            def z_evac(i, o, banks, ready, prev, keep):
                m, br = o // 2, o % 2
                s_ = sg[:, dslice(i, 8, o, 1), :]
                zt = sq[:, br:br + 1, :]
                for (c0, c1), b in zip(TWO, banks):
                    t = V([ready, prev("z7") if o < 2 else z_evac.z.get(o - 1 - br)], lambda e: e.tensor_tensor(zt[:, :, c0:c1], ps[:, b:b + 1, 0:HALF], s_[:, :, c0:c1], ALU.mult))
                if br:
                    k = dslice(i, 4, m, 1)
                    t2 = V([t], lambda e: e.tensor_tensor(zt, zt, sq[:, 0:1, :], ALU.add))
                    t2 = A([t2], lambda e: e.activation(z_hi[:, k, :], zt, ACT.Copy))
                    t2 = V([t2], lambda e: e.tensor_tensor(z_lo[:, k, :], zt, z_hi[:, k, :].bitcast(F32), ALU.subtract))
                    z_evac.z[o] = t2
                    keep(f"z{o}", t2)
                return t
            z_evac.z = {}
            outs = [[(o // 2, 4 * (o % 2) + k, 4 * (o % 2) + k) for k in range(4)] for o in range(2 * RING)]
            linear(2, outs, RING, u_rhs, TWO, z_evac, pr.all_done(), 4)
            y = area(2 * DT * N, DT, N)
            z_rhs = lambda k, c0, c1: (z_hi[:, k, c0:c1], z_lo[:, k, c0:c1])
            return y, project_out(y, z_rhs, pr.all_done(), parts=TWO)

        tmp_small = lambda n: small[:, n, :]
        small_e = small[:, 3, :]

        G0 = META - 4
        GW = N - G0
        CONV_LAYOUT = [([(G0, G0 + GW // 2), (G0 + GW // 2, N)], [0, 1]), (ONE, [2]),
                       ([(G0, G0 + GW // 2), (G0 + GW // 2, N)], [3, 4]), (ONE, [5])]

        def conv_ffn(y_in, t_y):
            table("natural_log_exp_and_others")
            head_in = prenorm(x, "ffn_pre", TWO, pr.all_done(), each=add_after(t_y + pr.all_done(), y_in, "mix_post", slice(0, N)))
            table("gelu_apprx_tanh_and_others")

            def evac(i, o, banks, ready, prev, keep):
                f_ = o // 2
                gt, w = tmp[:, 2 * f_, 0:GW], tmp[:, 2 * f_ + 1, 0:S]
                if o % 2 == 0:
                    for (c0, c1), b in zip(CONV_LAYOUT[0][0], banks):
                        t = V([ready, prev(f"done{f_}")], lambda e: e.tensor_tensor(gt[:, c0 - G0:c1 - G0], ps[:, b, 0:c1 - c0], rstd[:, c0:c1], ALU.mult))
                    one = lambda v: v.rearrange("p (o n) -> p o n", o=1)
                    tap = lambda j: conv[:, dslice(i, 2, f_, 1), j:j + 1].rearrange("p o n -> p (o n)")
                    c = sq[:, f_, 0:S]
                    lag = lambda j: gt[:, META - G0 - j:META - G0 - j + S]
                    t2 = V([t], lambda e: e.tensor_scalar(c, lag(0), tap(2), tap(3), ALU.mult, ALU.add))
                    t2 = V([t2], lambda e: e.scalar_tensor_tensor(c, lag(1), tap(1), c, ALU.mult, ALU.add))
                    t2 = V([t2], lambda e: e.scalar_tensor_tensor(c, lag(2), tap(0), c, ALU.mult, ALU.add))
                    evac.gelu = A([t2], lambda e: e.activation(c, c, ACT.Gelu_apprx_tanh))
                    return t
                c = sq[:, f_, 0:S]
                t = V([ready, prev(f"done{f_}")], lambda e: e.tensor_tensor(w, ps[:, banks[0], :], rstd[:, XS], ALU.mult))
                t2 = V([evac.gelu, t], lambda e: e.tensor_tensor(w, w, c, ALU.mult))
                k = dslice(i, 2, f_, 1)
                keep(f"done{f_}", store_split(t2, w.rearrange("p (o n) -> p o n", o=1), k))
                return t
            linear(FT // 2, square_outs, RING, u_rhs, ONE, evac, [], 4, CONV_LAYOUT, head=head_in)
            return y_ffn, project_out(y_ffn, hid_rhs, pr.all_done(), 2, FFN_OUTS, 4 * DOWN_UNITS)

        y, t_y = mix(y, t_y)
        y, t_y = conv_ffn(y, t_y)
        add = add_after(t_y, y, "ffn_post")
        for k in range(DT):
            add(k)
        finish(x[:, :, XS])


def tiles_of(w, tiles):
    k, m = w.shape[0] // P, w.shape[1] // P
    t = np.asarray(w).reshape(k, P, m, P).transpose(0, 2, 1, 3)
    return [t[a, b] for a, b in tiles]


def pack(*tile_lists):
    flat = [t for ts in tile_lists for t in ts]
    blank = np.zeros((P, P), np.float32)
    flat = [blank if t is None else t for t in flat]
    a = np.stack(flat).reshape(-1, UT, P, P)
    return a.transpose(0, 2, 1, 3).reshape(-1, P, UT * P)


def by_output(w, cols=None):
    k, m = w.shape[0] // P, w.shape[1] // P
    return tiles_of(w, [(a, b) for b in (cols or range(m)) for a in range(k)])


def by_token(w):
    return tiles_of(w, [(a, 4 * g + b) for g in range(2) for a in range(DT) for b in range(4)])


def down_tiles(w):
    out = []
    for b in range(w.shape[1] // P):
        out += tiles_of(w, [(a, b) for a in range(FT)]) + [None] * (DOWN_UNITS * UT - FT)
    return out


def pairs_of(a, b):
    out = []
    for c in range(a.shape[1] // P):
        out += by_output(a, [c]) + by_output(b, [c])
    return out


def kernel(**inputs):
    import concourse.bacc as bacc
    from concourse.bass_utils import run_bass_kernel_spmd
    a = {k: np.asarray(v) for k, v in inputs.items()}
    stream = []
    w = a["ml_w_in"][0]
    stream += [by_output(w[:, 0:1024]), by_output(w[:, 2048:3072]), by_token(w[:, 1024:2048])]
    gates_w = w[:, 3072:3080]
    stream += [by_output(a["ml_w_out"][0])]
    for layer in range(2):
        if layer == 1:
            stream += [by_output(a["sb_w_qkv"][0]), by_output(a["sb_w_out"][0])]
        stream += [by_output(a["xa_w_kv"][layer]), by_output(a["xa_w_q"][layer]), by_output(a["xa_w_o"][layer])]
        gu = a["ffn_w_gate_up"][layer]
        stream += [pairs_of(gu[:, :FF], gu[:, FF:]), down_tiles(a["ffn_w_down"][layer])]
    w2 = a["w_in_2"][0]
    stream += [by_output(w2[:, 0:2560]), pairs_of(w2[:, 2560:3584], w2[:, 3584:4608])]
    stream += [pairs_of(a["w_branch_hgrn_2"][0], a["w_branch_pool_2"][0]), by_output(a["w_out_2"][0])]
    stream += [pairs_of(a["ffn_w_gate_2"][0], a["ffn_w_up_2"][0]), down_tiles(a["ffn_w_down_2"][0])]
    units = pack(*stream)
    xT = np.concatenate([a["meta_tokens_2"].T, a["x"][0].T], axis=1)
    col = lambda v: v.reshape(-1, P).T
    full = [a["norm_gains"][l, n] for l in range(2) for n in range(6)]
    full += [a["mem_norm_gain"], a["ml_head_gain"][0], a["mix_norm_pre_2"][0], a["mix_norm_post_2"][0],
             a["ffn_norm_pre_2"][0], a["ffn_norm_post_2"][0]]
    half = [a["hgrn_out_norm_2"][0], a["pool_scale_2"][0], a["hgrn_lower_bounds_2"][0]]
    vecs = np.concatenate([col(v) for v in full + half], axis=1)
    conv = np.stack([col(a["ffn_conv_w_2"][0, j]) for j in range(CONV)] + [col(a["ffn_conv_b_2"][0])], axis=2)
    consts, masks = shape_constants()
    arrays = {"units": units, "xT": xT, "memT": a["mem"][0].T, "vecs": vecs, "gates_w": gates_w,
              "gates_b": a["ml_b_gate"][0].reshape(8, 1), "pool_w": a["pool_proj_2"][0].transpose(1, 0, 2).reshape(P, -1),
              "conv": conv.reshape(P, -1), "consts": consts, "masks": masks}
    arrays = {k: np.ascontiguousarray(v) for k, v in arrays.items()}
    nc = bacc.Bacc("TRN2", target_bir_lowering=False, num_devices=1)
    args = [nc.dram_tensor(f"in_{k}", v.shape, mybir.dt.from_np(v.dtype), kind="ExternalInput").ap() for k, v in arrays.items()]
    o = nc.dram_tensor("outT", (D, S), F32, kind="ExternalOutput").ap()
    build(nc, *args, o)
    r = run_bass_kernel_spmd(nc, [{f"in_{k}": v for k, v in arrays.items()}], core_ids=[0])
    return np.ascontiguousarray(r.results[0]["outT"].T)[None]
```

```python
from contextlib import ExitStack

import numpy as np

import concourse.bass as bass
from concourse import mybir
from concourse.alu_op_type import AluOpType as ALU

F32 = mybir.dt.float32
F32R = mybir.dt.float32r
I32 = mybir.dt.int32
ACT = mybir.ActivationFunctionType
AX = mybir.AxisListType

P = 128
D = 1024
DT = D // P
S = 512
META = 16
N = S + META
HALF = N // 2
MEM = 256
FF = 2816
FT = FF // P
EPS = 1e-6

ML_H, ML_DK, ML_DV = 4, 128, 256
GATE_CAP = 15.0
SB_H, SB_D = 16, 64
XA_H, XA_D = 4, 256
HG_H = 4
CONV = 3
WINDOWS = (2, 4, 8, 16)

UT = 8
RING = 4
LAND = 2
LEAD = 3
DONE0 = 1
DOWN_UNITS = -(-FT // UT)

VEC = {}
for _l in range(2):
    for _n in range(6):
        VEC[f"g{_l}{_n}"] = len(VEC)
for _n in ("mem", "ml_head", "mix_pre", "mix_post", "ffn_pre", "ffn_post"):
    VEC[_n] = len(VEC)
HALF_VEC = {"hg_out": 0, "pool_scale": 1, "lower": 2}


class Tok:

    def __init__(self, counter, value, step=0, i=None):
        self.counter, self.value, self.step, self.i = counter, value, step, i

    def wait(self, eng):
        v = self.value if self.i is None or not self.step else self.i * self.step + self.value
        eng.wait_ge(self.counter.sem, v)


def wait_all(eng, toks):
    top = {}
    for t in toks:
        if t is not None:
            key = (id(t.counter), t.i is None)
            if key not in top or top[key].value < t.value:
                top[key] = t
    for t in top.values():
        t.wait(eng)


class Counter:

    def __init__(self, sem):
        self.sem, self.n, self.step, self.i = sem, 0, 0, None

    def add(self, ins):
        if ins is not None:
            ins.then_inc(self.sem, 1)
        self.n += 1
        return Tok(self, self.n, self.step, self.i)


class Program:
    def __init__(self, nc, ctx, n_units):
        self.nc, self.ctx = nc, ctx
        self.pe, self.act, self.dve, self.pool, self.sp = nc.tensor, nc.scalar, nc.vector, nc.gpsimd, nc.sync
        sem = lambda name: ctx.enter_context(nc.semaphore(name))
        self.c_pe, self.c_act = Counter(sem("pe_done")), Counter(sem("act_done"))
        self.c_dve, self.c_pool = Counter(sem("dve_done")), Counter(sem("pool_done"))
        self.counters = [self.c_pe, self.c_act, self.c_dve, self.c_pool]
        self.landed = [sem(f"unit_landed{j}") for j in range(LAND)]
        self.hi_done, self.lo_done = sem("unit_hi_done"), sem("unit_lo_done")
        self.unit_done = sem("unit_multiplied")
        self.dry = False
        self.n_units, self.unit = n_units, 0

    def op(self, eng, counter, after, make):
        if self.dry:
            return counter.add(None)
        wait_all(eng, after)
        return counter.add(make(eng))

    def P(self, after, make):
        return self.op(self.pe, self.c_pe, after, make)

    def A(self, after, make):
        return self.op(self.act, self.c_act, after, make)

    def V(self, after, make):
        return self.op(self.dve, self.c_dve, after, make)

    def G(self, after, make):
        return self.op(self.pool, self.c_pool, after, make)

    def mms(self, after, out, pairs, start=True, stop=True):
        if self.dry:
            return self.c_pe.add(None)
        wait_all(self.pe, after)
        for n, (a, b) in enumerate(pairs):
            ins = self.pe.matmul(out, a, b, start=start and n == 0, stop=stop and n == len(pairs) - 1,
                                 skip_group_check=not (start and stop))
        return self.c_pe.add(ins)

    def loop(self, n, body):
        counts = [c.n for c in self.counters]
        kept = {}
        self.dry, unit = True, self.unit
        body(0, lambda name: None, lambda name, t: kept.__setitem__(name, (t.counter, t.value)))
        self.dry = False
        steps = [c.n - n0 for c, n0 in zip(self.counters, counts)]
        units = self.unit - unit
        self.unit = unit
        step_of = dict(zip([id(c) for c in self.counters], steps))
        for c, n0, st in zip(self.counters, counts, steps):
            c.n, c.step = n0, st
        with self.nc.Fori(0, n) as i:
            for c in self.counters:
                c.i = i
            self.unit_i, self.unit_step = i, units
            prev = lambda name: Tok(kept[name][0], kept[name][1] - step_of[id(kept[name][0])],
                                    step_of[id(kept[name][0])], i)
            body(i, prev, lambda name, t: None)
        for c, n0, st in zip(self.counters, counts, steps):
            assert c.n == n0 + st
            c.n, c.step, c.i = n0 + st * n, 0, None
        self.unit, self.unit_i, self.unit_step = unit + units * n, None, 0
        ends = {k: Tok(c, v + step_of[id(c)] * (n - 1)) for k, (c, v) in kept.items()}
        ends.update({k + " before": Tok(c, v + step_of[id(c)] * (n - 2)) for k, (c, v) in kept.items()})
        return ends

    def now(self, counter):
        return Tok(counter, counter.n)

    def all_done(self):
        return [self.now(c) for c in self.counters]

    unit_i, unit_step = None, 0

    def unit_wait(self, eng, sem, u, each=1):
        v = (u + 1) * each
        if self.unit_i is not None:
            v = self.unit_i * (self.unit_step * each) + v
        eng.wait_ge(sem, v)


def dslice(i, step, j, size):
    if isinstance(i, int):
        return slice(i * step + j, i * step + j + size)
    return bass.ds(i * step + j, size)


class Map:

    def __init__(self, nc):
        self.nc = nc
        self.at = -(-nc.sbuf_base // 64) * 64

    def place(self, name, shape, dt=F32, over=None):
        size = 4 * int(np.prod(shape[1:]))
        at = self.at if over is None else over
        if over is None:
            self.at += -(-size // 64) * 64
            assert self.at <= self.nc.sbuf_usable_end, (name, self.at)
        return self.nc.alloc_sbuf_tensor_at(name, shape, dt, offset=at)


CONST = {}
_at = 0
for _n, _w in (("ident", P), ("ones", P), ("neg_ones", P), ("neg_suffix", P), ("causal", P), ("strict", P),
               ("neg_fill", P), ("sel", ML_H * P), ("reset", N),
               ("inv_count", 4 * META)):
    CONST[_n] = (_at, _at + _w)
    _at += _w
CONST_ALL = _at
CONST_W = CONST["sel"][0]
LEVELS = (2, 4, 8, 16, 32, 64, 128)


def shape_constants():
    c = np.zeros((P, CONST_ALL), np.float32)
    s, t = np.arange(P)[:, None], np.arange(P)[None, :]
    put = lambda name, v: c.__setitem__((slice(None), slice(*CONST[name])), v)
    put("ident", s == t)
    put("ones", 1.0)
    put("neg_ones", -1.0)
    put("neg_suffix", np.where(s >= t, -1.0, 0.0))
    put("causal", t >= s)
    put("strict", t > s)
    put("neg_fill", np.where(t > s, 0.0, -1e30))
    put("sel", np.arange(ML_H * P)[None, :] // P == s)
    put("reset", (np.arange(N)[None, :] - META) % P != 0)
    put("inv_count", np.concatenate([1.0 / np.minimum(np.arange(META) + 1, w) for w in WINDOWS])[None, :])
    m = np.zeros((P, len(LEVELS), P), np.int32)
    for n, b in enumerate(LEVELS):
        m[:, n, :] = (s // b == t // b) & (s % b < b // 2) & (t % b >= b // 2)
    return c, m.reshape(P, -1)


def build(nc, units, xT, memT, vecs_d, gates_w, gates_b, pool_w, conv_d, consts_d, masks_d, out):
    n_units = units.shape[0]
    assert n_units % RING == 0
    ctx = ExitStack()
    with ctx:
        pr = Program(nc, ctx, n_units)
        pe, act, dve, pool, sp = pr.pe, pr.act, pr.dve, pr.pool, pr.sp
        A, V, T, mms = pr.A, pr.V, pr.P, pr.mms
        m = Map(nc)
        sb = m.place
        sem = lambda name: ctx.enter_context(nc.semaphore(name))

        x = sb("x", [P, DT, N])
        y_wide = m.at
        u_hi = sb("u_hi", [P, DT, N], F32R)
        u_lo = sb("u_lo", [P, DT, N], F32R)
        y_ffn = sb("y_ffn", [P, DT, N], F32, over=y_wide)[:, :, META:]
        w_land = sb("w_land", [P, LAND, UT * P])
        w_hi = sb("w_hi", [P, RING, UT * P], F32R)
        w_lo = sb("w_lo", [P, RING, UT * P], F32R)
        rstd = sb("rstd", [P, N])
        rstd_y = sb("rstd_y", [P, N])
        sq = sb("sq", [P, 2, N])
        acc_at = m.at
        acc = sb("acc", [P, N])
        NVEC = len(VEC) * DT + 4 * len(HALF_VEC)
        vecs = sb("vecs", [P, NVEC])
        consts = sb("consts", [P, CONST_W])
        conv = sb("conv", [P, FT, CONV + 1])
        eps = sb("eps", [P, 1])
        uT = sb("uT", [P, 4, ML_H])
        zrow = sb("zrow", [P, 1])
        rT = sb("rT", [P, 4])
        small = sb("small", [P, 4, 4])
        arena_at = m.at
        ARENA = 2 * FT * S + 4 * N
        arena = sb("arena", [P, ARENA])
        hid_hi = sb("hid_hi", [P, FT, S], F32R, over=arena_at)
        hid_lo = sb("hid_lo", [P, FT, S], F32R, over=arena_at + 4 * FT * S)
        tmp_at = 2 * FT * S
        ps = ctx.enter_context(nc.psum_tensor("ps", [P, 8, 512], F32))

        def area(at, *shape):
            size = int(np.prod(shape))
            assert at + size <= ARENA
            v = arena[:, at:at + size]
            if len(shape) == 2:
                return v.rearrange("p (a b) -> p a b", b=shape[1])
            if len(shape) == 3:
                return v.rearrange("p (a b c) -> p a b c", b=shape[1], c=shape[2])
            return v

        def halves(name, at, *shape):
            assert at + int(np.prod(shape)) <= ARENA
            v = sb(name, [P, *shape], F32R, over=arena_at + 4 * at)
            return v[(slice(None),) * (1 + len(shape))]

        tmp = area(tmp_at, 4, N)
        const = lambda name: consts[:, slice(*CONST[name])]
        ident, ones = const("ident"), const("ones")
        col = lambda name, k: vecs[:, VEC[name] * DT + k:VEC[name] * DT + k + 1]
        def half_col(name, k):
            c = len(VEC) * DT + 4 * HALF_VEC[name] + k
            return vecs[:, c:c + 1]
        XS = slice(META, N)
        MS = slice(0, MEM)

        s_small, s_mem, s_out = sem("small_loaded"), sem("mem_loaded"), sem("out_stored")
        c_small, c_meml = Counter(s_small), Counter(s_mem)
        land_at = lambda j: w_land[:, j % LAND, :]
        x_pairs = [Counter(sem(f"x_loaded{n}")) for n in range(DT // 2)]
        def load_x(n):
            sp.dma_start(x[:, 2 * n:2 * n + 2, :], xT.rearrange("(k p) n -> p k n", p=P)[:, 2 * n:2 * n + 2, :]).then_inc(x_pairs[n].sem, 16)
        x_in = lambda k: Tok(x_pairs[k // 2], 16)
        s_vecs = sem("vecs_loaded")
        sp.dma_start(vecs[:, :], vecs_d).then_inc(s_vecs, 16)
        for j in range(LAND):
            sp.dma_start(land_at(j), units[j, :, :]).then_inc(pr.landed[j], 16)
            load_x(j)
        for n in range(LAND, DT // 2):
            load_x(n)
        sp.dma_start(consts[:, :], consts_d[:, 0:CONST_W]).then_inc(s_small, 16)
        sp.dma_start(conv[:, :, :], conv_d.rearrange("p (k n) -> p k n", k=FT)).then_inc(s_small, 16)
        vecs_in, consts_in = Tok(Counter(s_vecs), 16), Tok(c_small, 32)
        with sp.Fori(1, n_units // LAND) as g:
            for j in range(LAND):
                sp.wait_ge(pr.lo_done, g * LAND + (j + 1 - LAND))
                sp.dma_start(land_at(j), units[bass.ds(g * LAND + j, 1), :, :].rearrange("o p n -> (o p) n"))\
                  .then_inc(pr.landed[j], 16)

        def split(u):
            if pr.dry or (pr.unit_i is None and u >= n_units):
                return
            j, looped = u % RING, pr.unit_i is not None
            v = 16 * (u // LAND + 1)
            act.wait_ge(pr.landed[j % LAND], pr.unit_i * (16 * (pr.unit_step // LAND)) + v if looped else v)
            if u >= RING or looped:
                pr.unit_wait(act, pr.unit_done, u - RING + DONE0)
                pr.unit_wait(pool, pr.unit_done, u - RING + DONE0)
            act.activation(w_hi[:, j, :], land_at(j), ACT.Copy).then_inc(pr.hi_done, 1)
            pr.unit_wait(pool, pr.hi_done, u)
            pool.tensor_tensor(w_lo[:, j, :], land_at(j), w_hi[:, j, :].bitcast(F32), ALU.subtract)\
                .then_inc(pr.lo_done, 1)

        for u in range(LAND):
            split(u)
        t_eps = V([], lambda e: e.memset(eps[:, :], EPS))

        c_unit = Counter(pr.unit_done)
        pe.sem_inc(pr.unit_done, DONE0)

        def linear(n_iter, outs, n_u, rhs, parts, evac, after, depth, layout=None, head=None, before=None, between=(), arrive=None):
            between = list(between)
            wait_all(pe, after)
            if layout is None:
                layout = [(parts, [o * len(parts) + b for b in range(len(parts))]) for o in range(depth)]

            def last_user(o):
                mine = layout[o % depth][1]
                return next(b for b in range(o - 1, o - 1 - len(outs), -1) if set(mine) & set(layout[b % len(outs) % depth][1]))

            def tile_products(outs_, o, n, wait_unit):
                tiles = outs_[o]
                uj, q, k = tiles[n]
                u = pr.unit + uj
                parts_o, banks = layout[o % depth]
                if wait_unit:
                    pr.unit_wait(pe, pr.lo_done, u)
                hi = w_hi[:, u % RING, q * P:(q + 1) * P]
                lo = w_lo[:, u % RING, q * P:(q + 1) * P]
                for h, (w, which) in enumerate(((hi, 0), (hi, 1), (lo, 0))):
                    for (c0, c1), bank in zip(parts_o, banks):
                        ins = pe.matmul(ps[:, bank, 0:c1 - c0], w, rhs(k, c0, c1)[which],
                                        start=n == 0 and h == 0, stop=n == len(tiles) - 1 and h == 2)
                if not (any(t[0] == uj for t in tiles[n + 1:]) or any(t[0] == uj for ts in outs_[o + 1:] for t in ts)):
                    ins.then_inc(pr.unit_done, 1)

            arrive = dict(arrive or {})

            def body(i, prev, keep, abreast=0):
                free = {}
                begun, split_to = -1, 0
                if abreast:
                    ready, _, finish = head
                    for n in range(UT):
                        wait_all(pe, [ready[n]])
                        if n < UT - 2:
                            for o in range(abreast):
                                tile_products(outs, o, n, n == 0)
                    for o in range(abreast):
                        for n in range(UT - 2, UT):
                            tile_products(outs, o, n, False)
                    begun = abreast - 1
                    split_to = RING + min(abreast, LEAD)
                    for u in range(RING, split_to):
                        split(pr.unit + u)
                    t_fin = finish()
                    wait_all(dve, [t_fin])
                for o, tiles in enumerate(outs):
                    parts_o, banks = layout[o % depth]
                    back = last_user(o)
                    t_free = free[back] if back >= 0 else prev(f"free{back + len(outs)}")
                    if abreast and back < 0 and max(banks) >= 6:
                        t_free = t_fin
                    if not pr.dry and o >= abreast:
                        wait_all(pe, [t_free])
                        for n, (uj, q, k) in enumerate(tiles):
                            if n in arrive:
                                wait_all(pe, [arrive.pop(n)])
                            tile_products(outs, o, n, uj > begun)
                            begun = max(begun, uj)
                    last_u = tiles[-1][0]
                    for uj in sorted({t[0] for t in tiles}):
                        if not any(t[0] == uj for ts in outs[o + 1:] for t in ts) and uj + LEAD >= split_to:
                            split(pr.unit + uj + LEAD)
                    ready_o = Tok(c_unit, pr.unit + last_u + 1 + DONE0, pr.unit_step, pr.unit_i)
                    free[o] = evac(i, o, banks, ready_o, prev, keep)
                    keep(f"free{o}", free[o])
                    if between:
                        between.pop(0)()
                pr.unit += n_u

            n0, got = 0, dict(before or {})
            while n0 < n_iter and (n0 == 0 and (head or before) or between):
                body(n0, got.get, lambda name, t: got.__setitem__(name, t), head[1] if head and n0 == 0 else 0)
                n0 += 1
            last = n0 < n_iter and pr.unit + (n_iter - n0) * n_u >= n_units
            n1 = n_iter - 1 if last else n_iter
            if n1 > n0:
                got = pr.loop(n1 - n0, lambda i, prev, keep: body(i + n0, prev, keep))
            if last:
                seen = {}
                body(n_iter - 1, lambda name: got.get(name), lambda name, t: seen.__setitem__(name, t))
                got = seen
            return got

        def linear_by_token(u_, n_blocks, evac, after, between=()):
            wait_all(pe, after)
            between, drained = list(between), []
            for g in range(2):
                for j in range(RING):
                    u = pr.unit + j
                    pr.unit_wait(pe, pr.lo_done, u)
                    for kk in range(2):
                        k, cols = 2 * j + kk, slice(kk * 4 * P, (kk + 1) * 4 * P)
                        for b in range(n_blocks):
                            u_h, u_l = u_(k, b)
                            for n, (a_, w_) in enumerate(((u_h, w_hi), (u_l, w_hi), (u_h, w_lo))):
                                ins = pe.matmul(ps[:, 4 * g + b, :], a_, w_[:, u % RING, cols],
                                                start=k == 0 and n == 0, stop=k == DT - 1 and n == 2)
                    ins.then_inc(pr.unit_done, 1)
                    split(u + LEAD)
                    if between:
                        between.pop(0)()
                ready = Tok(c_unit, pr.unit + RING + DONE0)
                free = [evac(g, b, 4 * g + b, ready) for b in range(n_blocks)]
                drained.append(free)
                pr.unit += RING
            return drained

        def rstd_columns(bank, r, n_blocks, after):
            for b in range(n_blocks):
                t = T(after, lambda e: e.transpose(ps[:, bank, b * P:(b + 1) * P], r[:, b * P:(b + 1) * P], ident))
            return V([t], lambda e: e.tensor_copy(rT[:, 0:n_blocks], ps[:, bank, 0:n_blocks * P]
                                                  .rearrange("p (b n) -> p b n", n=P)[:, :, 0:1].rearrange("p b n -> p (b n)")))

        def tokens_out(v_tok):
            def evac(g, b, bank, ready):
                dst = v_tok[:, b, g * 4 * P:(g + 1) * 4 * P]
                if b % 2:
                    return A([ready], lambda e: e.activation(dst, ps[:, bank, :], ACT.Copy, scale=rT[:, b:b + 1]))
                else:
                    return V([ready], lambda e: e.tensor_scalar(dst, ps[:, bank, :], rT[:, b:b + 1], None, ALU.mult))
            return evac

        square_outs = [[(j, q, q) for q in range(UT)] for j in range(RING)]

        def rsqrt_mean(ss_banks, parts, width, dst, after):
            for (c0, c1), b in zip(parts, ss_banks):
                t = A(after + [t_eps], lambda e: e.activation(dst[:, c0:c1], ps[:, b, 0:c1 - c0], ACT.Ln,
                                                    bias=eps[:, 0:1], scale=1.0 / width))
            a, z = parts[0][0], parts[-1][1]
            return A([t], lambda e: e.activation(dst[:, a:z], dst[:, a:z], ACT.Exp, scale=-0.5))

        ONE = [(META, N)]
        TWO = [(0, HALF), (HALF, N)]

        def norm_steps(src, gain, a, z, after, dst, sum_, squares, each=None, adder=None):
            d_hi, d_lo = dst
            t_sum, t_lo, t_his = [], [], []

            def low(k):
                t_lo.append(V((after if k == 0 else []) + [t_his[k]], lambda e: e.scalar_tensor_tensor(
                    d_lo[:, k, a:z], src[:, k, a:z], col(gain, k), d_hi[:, k, a:z].bitcast(F32), ALU.mult, ALU.subtract)))

            def step(k):
                t_x = each(k) if each else None
                first = after if k == 0 else []
                s_ = sum_[:, a:z] if k == 0 else squares[:, k % 2, a:z]
                t_hi = A(first + [t_x], lambda e: e.activation(d_hi[:, k, a:z], src[:, k, a:z], ACT.Copy, scale=col(gain, k)))
                t_sq = A([t_sum[k - 2] if k >= 2 else None], lambda e: e.activation(s_, src[:, k, a:z], ACT.Square))
                t_his.append(t_hi)
                for n in [k - 1] * (k > 0) + [k] * (k == DT - 1):
                    low(n)
                t_sum.append((adder or pr.G)([t_sq, t_sum[-1]], lambda e: e.tensor_tensor(sum_[:, a:z], sum_[:, a:z], s_, ALU.add)) if k else t_sq)
            return step, t_lo, t_sum

        def mean_square(parts, sum_, t_sum, bank, r_dst):
            for b, (c0, c1) in enumerate(parts):
                t = mms([t_sum], ps[:, bank + b, 0:c1 - c0], [(ones, sum_[:, c0:c1])])
            return rsqrt_mean([bank + b for b in range(len(parts))], parts, D, r_dst, [t])

        def prenorm(src, gain, parts, after, each=None, abreast=3, first=LEAD):
            if first == LEAD:
                split(pr.unit + LEAD)
            step, t_lo, t_sum = norm_steps(src, gain, parts[0][0], parts[-1][1], after, (u_hi, u_lo), acc, sq, each)
            for k in range(DT):
                step(k)
            for u in range(first, RING if first < LEAD else 0):
                split(pr.unit + u)
            return t_lo, abreast, lambda: mean_square(parts, acc, t_sum[-1], 6, rstd)

        def u_rhs(k, c0, c1):
            return u_hi[:, k, c0:c1], u_lo[:, k, c0:c1]

        def u_tok(k, b):
            cols = slice(META + b * P, META + (b + 1) * P)
            return u_hi[:, k, cols], u_lo[:, k, cols]

        def hid_rhs(k, c0, c1):
            return hid_hi[:, k, c0:c1], hid_lo[:, k, c0:c1]

        def y_evac(y, parts):
            a, z = parts[0][0], parts[-1][1]

            def evac(i, o, banks, ready, prev, keep):
                k = dslice(i, y_evac.per, o, 1)
                for (c0, c1), b in zip(parts, banks):
                    t = A([ready], lambda e: e.activation(y[:, k, c0 - a:c1 - a], ps[:, b:b + 1, 0:c1 - c0], ACT.Copy))
                added = y_evac.added[o - 2] if o >= 2 else prev(f"added{o - 2 + y_evac.per}")
                t2 = V([t, added], lambda e: e.tensor_tensor(sq[:, o % 2:o % 2 + 1, 0:z - a], y[:, k, :], y[:, k, :], ALU.mult))
                sums = acc[:, y_evac.first:y_evac.first + z - a]
                y_evac.added[o] = V([t2], lambda e: e.tensor_tensor(sums, sums, sq[:, o % 2, 0:z - a], ALU.add))
                keep(f"added{o}", y_evac.added[o])
                return t
            return evac

        def project_out(y, rhs, after, n_iter=2, outs=square_outs, n_u=RING, parts=ONE, between=(), late=False, arrive=None, before=None):
            t = V(pr.all_done(), lambda e: e.memset(acc[:, :], 0.0))
            y_evac.per, y_evac.added = len(outs), {}
            y_evac.first = parts[0][0]
            cols = parts if rhs is not hid_rhs else [(0, S)]
            linear(n_iter, outs, n_u, rhs, cols, y_evac(y, cols), after, 4, between=between, arrive=arrive,
                   before={**(before or {}), f"added{len(outs) - 2}": t, f"added{len(outs) - 1}": t})
            t_sum, t_y = pr.now(pr.c_dve), []
            def finish_y():
                t_y.append(mean_square(parts, acc, t_sum, 5, rstd_y))
            if late:
                return t_y, finish_y
            finish_y()
            return t_y

        def add_tile(y, gain, cols=XS):
            def each(k):
                t = V([], lambda e: e.scalar_tensor_tensor(y[:, k, :], y[:, k, :], col(gain, k), rstd_y[:, cols], ALU.mult, ALU.mult))
                return V([t], lambda e: e.tensor_tensor(x[:, k, cols], x[:, k, cols], y[:, k, :], ALU.add))
            return each

        def scaled_to(dst, per, part=ONE, scale=None):
            def evac(i, o, banks, ready, prev, keep):
                for (c0, c1), b in zip(part, banks):
                    w0 = c0 - part[0][0]
                    v, r_ = dst[:, dslice(i, per, o, 1), w0:w0 + c1 - c0], rstd[:, c0:c1].rearrange("p (o n) -> p o n", o=1)
                    p_ = ps[:, b:b + 1, 0:c1 - c0]
                    if scale is None:
                        t = V([ready], lambda e: e.tensor_tensor(v, p_, r_, ALU.mult))
                    else:
                        t = V([ready], lambda e: e.scalar_tensor_tensor(v, p_, scale, r_, ALU.mult, ALU.mult))
                return t
            return evac

        def add_after(after, y, gain, cols=XS):
            add = add_tile(y, gain, cols)
            def each(k):
                for t in (after if k == 0 else []):
                    t.wait(dve)
                return add(k)
            return each

        def table(name):
            if not pr.dry:
                act.preload_act_table_set(name)

        AT = (0, 512, 1024, 896)
        SPAN = 1280

        def mlstm():
            def x_there(k):
                for e in (act, dve):
                    wait_all(e, [x_in(k)] + [consts_in] * (k == DT - 1))
            t_pre = prenorm(x, "g00", ONE, [vecs_in], each=x_there, abreast=2, first=LAND)
            qT, kT, vT, og = area(0, 4, S), area(2048, 4, S), area(4096, 8, S), area(8192, 8, S)
            v_tok = area(12288, 4, D)
            M_bc, floor_bc = area(16384, 4, S), area(18432, 4, S)
            gw = area(20480, DT, 36)
            rows = tmp
            gb = area(20480 + DT * 36, 4)
            sel_all = area(20480 + DT * 36 + 4, ML_H * P)
            gw_hi, gw_lo = (halves(f"gw{n}", 21504 + n * DT * 36, DT, 36) for n in range(2))

            t0 = V([], lambda e: e.memset(gw, 0.0))
            if not pr.dry:
                t0.wait(act)
                act.dma_start(gw[:, :, 0:ML_H], gates_w.rearrange("(k p) n -> p k n", p=P)[:, :, 0:ML_H]).then_inc(s_small, 16)
                act.dma_start(gw[:, :, 32:36], gates_w.rearrange("(k p) n -> p k n", p=P)[:, :, ML_H:]).then_inc(s_small, 16)
                act.dma_start(sel_all, consts_d[:, slice(*CONST["sel"])]).then_inc(s_small, 16)
                act.dma_start(gb[0:ML_H, 0:1], gates_b[0:ML_H, :]).then_inc(s_small, 16)
                act.dma_start(gb[0:ML_H, 1:2], gates_b[ML_H:2 * ML_H, :]).then_inc(s_small, 16)
            gates_in = Tok(c_small, 32 + 80)

            t1 = A([gates_in], lambda e: e.activation(gw_hi, gw, ACT.Copy))
            t_gw = V([t1, gates_in], lambda e: e.tensor_tensor(gw_lo, gw, gw_hi.bitcast(F32), ALU.subtract))
            got = linear(1, square_outs, RING, u_rhs, ONE, scaled_to(qT, 4), [], 4, head=t_pre)
            got = linear(1, square_outs, RING, u_rhs, ONE, scaled_to(kT, 4, scale=ML_DK ** -0.5), [], 4, before=got)
            t_g = mms([t_gw], ps[0:36, 4, :], [(g_[:, k, :], u_[:, k, XS]) for k in range(DT)
                                               for g_, u_ in ((gw_hi, u_hi), (gw_hi, u_lo), (gw_lo, u_hi))])
            t_rT = rstd_columns(5, rstd[:, XS], 4, [])

            ig, lf = rows[0:4, 0, 0:S], rows[0:4, 1, 0:S]
            w1, w2 = rows[0:4, 2, 0:S], rows[0:4, 3, 0:S]
            st = {"t": t_g}
            def step(eng, make, waits=()):
                def do():
                    st["t"] = eng([st["t"], *waits], make)
                return do
            gate_steps = [
                step(V, lambda e: e.tensor_tensor(ig, ps[0:4, 4, :], rstd[0:4, XS], ALU.mult)),
                step(V, lambda e: e.tensor_tensor(rows[32:36, 1, 0:S], ps[32:36, 4, :], rstd[32:36, XS], ALU.mult)),
                step(A, lambda e: e.activation(lf, rows[32:36, 1, 0:S], ACT.Copy))]
            for n, row in ((0, ig), (1, lf)):
                gate_steps += [
                    step(V, lambda e, row=row, n=n: e.tensor_scalar(row, row, gb[0:4, n:n + 1], 1.0 / GATE_CAP, ALU.add, ALU.mult), [gates_in]),
                    step(A, lambda e, row=row: e.activation(row, row, ACT.Tanh)),
                    step(V, lambda e, row=row: e.tensor_scalar(row, row, GATE_CAP, None, ALU.mult))]
            scan_steps = [
                step(A, lambda e: e.activation(w1, lf, ACT.Abs)),
                step(A, lambda e: e.activation(w1, w1, ACT.Exp, scale=-1.0)),
                step(A, lambda e: e.activation(w1, w1, ACT.Ln, bias=1.0)),
                step(V, lambda e: e.scalar_tensor_tensor(lf, lf, 0.0, w1, ALU.min, ALU.subtract)),
                step(V, lambda e: e.tensor_tensor_scan(w2, ones_row(4), lf, 0.0, ALU.mult, ALU.add)),
                step(V, lambda e: e.tensor_tensor(ig, ig, w2, ALU.subtract)),
                step(V, lambda e: e.tensor_tensor_scan(w1, ig, ig, 0.0, ALU.max, ALU.max)),
                step(V, lambda e: e.tensor_tensor(w2, w2, w1, ALU.add)),
                step(A, lambda e: e.activation(w2, w2, ACT.Exp, scale=-1.0))]

            def together(steps):
                return lambda: [do() for do in steps]
            table("sigmoid_and_others")
            to_og = scaled_to(og, 4)
            def og_evac(i, o, banks, ready, prev, keep):
                t = to_og(i, o, banks, ready, prev, keep)
                v = og[:, dslice(i, 4, o, 1), :]
                A([t], lambda e: e.activation(v, v, ACT.Sigmoid))
                return t
            pairs = [together(gate_steps[n:n + 2]) for n in range(0, len(gate_steps), 2)]
            pairs += [lambda: None] * (8 - len(pairs))
            linear(2, square_outs, RING, u_rhs, ONE, og_evac, [], 4, before=got, between=pairs)
            table("natural_log_exp_and_others")
            drained = linear_by_token(u_tok, 4, tokens_out(v_tok), [pr.now(pr.c_dve)], [together(scan_steps[n:n + 2]) for n in range(0, len(scan_steps), 2)])
            t_F = st["t"]
            t_row = drained[0]
            for h in range(ML_H):
                sel = sel_all[0:4, h * P:(h + 1) * P]
                b = 2 * (h % 2)
                t1 = mms([t_F, t_row[b]], ps[:, b, :], [(sel, w1)])
                t_row[b] = V([t1], lambda e: e.tensor_copy(M_bc[:, h, :], ps[:, b, :]))
                t2 = mms([t_row[b + 1]], ps[:, b + 1, :], [(sel, w2)])
                t_row[b + 1] = A([t2], lambda e: e.activation(floor_bc[:, h, :], ps[:, b + 1, :], ACT.Copy))
            for b in range(4):
                t2 = T([t_row[0]], lambda e: e.transpose(ps[:, 0, 4 * b:4 * b + 4], rows[0:4, 0, b * P:(b + 1) * P], ident[0:4, 0:4]))
            t_u = V([t2], lambda e: e.tensor_copy(uT[:, :, :], ps[:, 0, 0:16].rearrange("p (b h) -> p b h", h=4)))

            weights, k_h, u_h = area(4096, 2, SPAN), area(6656, 2, S), area(7680, 2, 4)
            v_h, hT = area(20480, 8, ML_DV), area(22528, 4, S)
            den = [acc[:, 0:S], rstd_y[:, 0:S]]
            flat = ps[:, :, :].rearrange("p b n -> p (b n)")
            one = lambda v: v.rearrange("p (o n) -> p o n", o=1)

            def two_heads(i, prev, keep):
                t_k, t_v, t_w, t_s, t_n, t_q, t_r = {}, {}, {}, {}, {}, {}, {}
                B0 = lambda j: 3 * j
                for j in range(2):
                    at = lambda v: v[:, dslice(i, 2, j, 1), :]
                    t_k[j] = A([prev(f"n{j}")], lambda e: e.activation(one(k_h[:, j, :]), at(kT), ACT.Copy))
                    t_u = V([prev(f"n{j}")], lambda e: e.tensor_copy(u_h[:, j, :], uT[:, :, dslice(i, 2, j, 1)].rearrange("p b o -> p (b o)")))
                    for b in range(4):
                        t_w[j] = V([t_u, prev(f"n{j}")], lambda e: e.scalar_tensor_tensor(one(weights[:, j, AT[b]:AT[b] + S - b * P]), at(M_bc)[:, :, b * P:S],
                                                                   u_h[:, j, b:b + 1], zeros_like(S - b * P), ALU.subtract, ALU.max))
                    if not pr.dry:
                        wait_all(pe, [t_k[j], prev(f"h{j}")])
                        for b in range(4):
                            a0 = 512 * B0(j) + AT[b]
                            ins = pe.matmul(flat[:, a0:a0 + S - b * P], k_h[:, j, b * P:(b + 1) * P], at(qT)[:, :, b * P:S].rearrange("p o n -> p (o n)"),
                                            start=b != 3, stop=b != 1, skip_group_check=True)
                    t_s[j] = pr.c_pe.add(None if pr.dry else ins)
                for j in range(2):
                    w = weights[:, j, :]
                    t_w[j] = A([t_w[j]], lambda e: e.activation(w, w, ACT.Exp, scale=-1.0))
                    t_v[j] = A([prev(f"n{j}")], lambda e: e.activation(v_h[:, 4 * j:4 * j + 4, :], v_tok[:, :, dslice(i, 2 * ML_DV, j * ML_DV, ML_DV)], ACT.Copy))
                for j in range(2):
                    w, b0 = weights[:, j, :], 512 * B0(j)
                    t = V([t_w[j], t_s[j]], lambda e: e.tensor_tensor(w, flat[:, b0:b0 + SPAN], w, ALU.mult))
                    for b in range(4):
                        d = weights[:, j, AT[b]:AT[b] + P]
                        t_w[j] = V([t], lambda e: e.tensor_tensor(d, d, const("causal"), ALU.mult))
                    for n, lhs in enumerate((lambda b: ones, lambda b: v_h[:, 4 * j + b, 0:P], lambda b: v_h[:, 4 * j + b, P:2 * P])):
                        if not pr.dry:
                            wait_all(pe, [t_w[j], t_v[j]])
                            for b in range(4):
                                ins = pe.matmul(ps[:, B0(j) + n, b * P:S], lhs(b), weights[:, j, AT[b]:AT[b] + S - b * P],
                                                start=b == 0, stop=b == 3, skip_group_check=True)
                        t_n[j, n] = pr.c_pe.add(None if pr.dry else ins)
                    keep(f"n{j}", t_n[j, 2])
                for j in range(2):
                    at = lambda v: v[:, dslice(i, 2, j, 1), :]
                    h_, b0 = hT[:, 2 * j:2 * j + 2, :], B0(j)
                    t = A([t_n[j, 0], prev(f"den{j}")], lambda e: e.activation(den[j], ps[:, b0, :], ACT.Abs))
                    t = V([t], lambda e: e.tensor_tensor(one(den[j]), one(den[j]), at(floor_bc), ALU.max))
                    t = V([t], lambda e: e.reciprocal(den[j], den[j]))
                    t_h = V([t, t_n[j, 2], prev(f"den{j}")], lambda e: e.tensor_tensor(h_, ps[:, b0 + 1:b0 + 3, :], one(den[j]).broadcast_to([P, 2, S]), ALU.mult))
                    keep(f"h{j}", t_h)
                    t_sq = A([t_h, t_q.get(0) or prev("ss")], lambda e: e.activation(sq[:, :, 0:S], h_, ACT.Square))
                    t_q[j] = mms([t_sq], ps[:, 6 + j, :], [(ones, sq[:, 0, 0:S]), (ones, sq[:, 1, 0:S])])
                    keep("ss", t_q[j])
                    t_r[j] = rsqrt_mean([6 + j], [(0, S)], ML_DV, den[j], [t_q[j]])
                    t_h = pr.G([t_sq], lambda e: e.tensor_tensor(h_, h_, og[:, dslice(i, 4, 2 * j, 2), :], ALU.mult))
                    t_w[j] = t_h
                tiles = [(j, dslice(i, 4, 2 * j + n, 1), one(hT[:, 2 * j + n, :]), dslice(i, 4, VEC["ml_head"] * DT + 2 * j + n, 1))
                         for j in range(2) for n in range(2)]
                t_hi = []
                for m_, (j, kk, hn, gain) in enumerate(tiles):
                    if m_ % 2 == 0:
                        h_ = hT[:, 2 * j:2 * j + 2, :]
                        t_r[j] = V([t_r[j], t_w[j]], lambda e: e.tensor_tensor(h_, h_, one(den[j]).broadcast_to([P, 2, S]), ALU.mult))
                    t = V([t_r[j]], lambda e: e.tensor_scalar(hn, hn, vecs[:, gain], None, ALU.mult))
                    t_hi.append(A([t], lambda e: e.activation(u_hi[:, kk, XS], hn, ACT.Copy)))
                for t, (j, kk, hn, _) in zip(t_hi, tiles):
                    t = V([t], lambda e: e.tensor_tensor(u_lo[:, kk, XS], hn, u_hi[:, kk, XS].bitcast(F32), ALU.subtract))
                    keep(f"den{j}", t)
            all_wait()
            pr.loop(ML_H // 2, two_heads)
            y, memory = area(0, 8, S), memory_steps(0)
            return memory, y, *project_out(y, u_rhs, pr.all_done(), between=memory[0], late=True)

        V([], lambda e: e.memset(zrow[:, :], 0.0))
        def all_wait():
            ts = pr.all_done()
            for e in (pe, act, dve, pool):
                wait_all(e, ts)

        zeros_like = lambda w: zrow[:, 0:1].broadcast_to([P, w])
        ones_row = lambda n: const("ones")[0:n, 0:1].broadcast_to([n, S])


        mem_in = area(4096, DT, MEM)
        m_hi, m_lo = halves("m_hi", 6144, DT, MEM), halves("m_lo", 8192, DT, MEM)
        rstd_m, m_sum, m_sq = tmp[:, 3, 0:MEM], tmp[:, 2, 0:MEM], tmp[:, 0:2, 0:MEM]
        MEM_PART = [(0, MEM)]

        def memory_steps(layer):
            if not pr.dry:
                wait_all(act, pr.all_done())
                act.dma_start(mem_in, memT.rearrange("(k p) n -> p k n", p=P)).then_inc(s_mem, 16)
            after = pr.all_done() + [Tok(c_meml, 16 * (layer + 1))]
            step, t_lo, t_sum = norm_steps(mem_in, "mem", 0, MEM, after, (m_hi, m_lo), m_sum, m_sq)
            steps = [lambda: None] * 3 + [lambda k=k: (step(k), step(k + 1)) for k in range(0, DT, 2)]
            return steps, t_lo, t_sum

        mixed = mlstm()

        def attend_memory(layer, memory, y_in, t_y, finish_y):
            _, t_lo, t_sum = memory
            kT, v_tok, qT = area(10240, DT, MEM), area(12288, 2, D), area(14336, 8, S)
            q_h, v_h, Pn, pT = area(0, 4, S), area(2048, 4, XA_D), area(3072, 8, MEM), area(5120, 4, S)
            m_rhs = lambda k, c0, c1: (m_hi[:, k, c0:c1], m_lo[:, k, c0:c1])
            t_m = mean_square(MEM_PART, m_sum, t_sum[-1], 6, rstd_m)
            x_step, x_lo, x_sum = norm_steps(x, f"g{layer}2", META, N, [], (u_hi, u_lo), acc, sq,
                                             each=add_after(t_y, y_in, f"g{layer}1"), adder=V)
            def k_evac(i, o, banks, ready, prev, keep):
                return V([ready, t_m], lambda e: e.tensor_tensor(kT[:, 4 * i + o, :], ps[:, banks[0], 0:MEM], rstd_m, ALU.mult))
            got = linear(2, square_outs, RING, m_rhs, MEM_PART, k_evac, [t_lo[-1]], 4,
                         between=[finish_y] + [lambda k=k: x_step(k) for k in range(RING + 3)])
            rstd_columns(7, rstd_m, 2, [t_m])
            m_tok = lambda k, b: (m_hi[:, k, b * P:(b + 1) * P], m_lo[:, k, b * P:(b + 1) * P])
            t_x = []
            drained = linear_by_token(m_tok, 2, tokens_out(v_tok), [got["free0"], got["free1"]] + t_y,
                                      [lambda: x_step(DT - 1), lambda: None,
                                       lambda: t_x.append(mean_square(ONE, acc, x_sum[-1], 6, rstd))])
            def q_evac(i, o, banks, ready, prev, keep):
                return V([ready, t_x[0]], lambda e: e.tensor_tensor(qT[:, dslice(i, 4, o, 1), :], ps[:, banks[0]:banks[0] + 1, :],
                                                             rstd[:, XS].rearrange("p (o n) -> p o n", o=1), ALU.mult))
            linear(2, square_outs, RING, u_rhs, ONE, q_evac, drained[0] + [got["free3"], x_lo[-1]], 4)
            all_wait()
            scale = XA_D ** -0.5
            mx, sm = tmp[:, 0, 0:8], tmp[:, 1, 0:8]

            def two_heads(i, prev, keep):
                t_q, t_v, t_s, t_e, t_n, t_p, t_o = {}, {}, {}, {}, {}, {}, {}
                for j in range(2):
                    B0, hs = 4 * j, slice(2 * j, 2 * j + 2)
                    q_, v_ = q_h[:, hs, :], v_h[:, hs, :]
                    t_q = V([prev(f"s{j}")], lambda e: e.tensor_copy(q_, qT[:, dslice(i, 4, 2 * j, 2), :]))
                    t_v[j] = pr.G([prev(f"o{j}")], lambda e: e.tensor_copy(v_, v_tok[:, :, dslice(i, 2 * XA_D, j * XA_D, XA_D)]))
                    for b in range(4):
                        t_s[j] = mms([t_q, prev(f"out{j}")], ps[:, B0 + b // 2, (b % 2) * MEM:(b % 2 + 1) * MEM],
                                     [(q_[:, n, b * P:(b + 1) * P], kT[:, dslice(i, 4, 2 * j + n, 1), :].rearrange("p o n -> p (o n)")) for n in range(2)])
                    keep(f"s{j}", t_s[j])
                for j in range(2):
                    B0, P_ = 4 * j, Pn[:, 4 * j:4 * j + 4, :]
                    m_, s_ = mx[:, 4 * j:4 * j + 4], sm[:, 4 * j:4 * j + 4]
                    t = V([t_s[j], prev(f"e{j}")], lambda e: e.tensor_reduce(m_, ps[:, B0:B0 + 2, :].rearrange("p c (b n) -> p (c b) n", n=MEM), AX.X, ALU.max))
                    t = V([t], lambda e: e.tensor_scalar(m_, m_, -scale, None, ALU.mult))
                    for b in range(4):
                        t_e[j] = A([t, prev(f"p{j}")], lambda e: e.activation(P_[:, b, :], ps[:, B0 + b // 2, (b % 2) * MEM:(b % 2 + 1) * MEM], ACT.Exp,
                                                                        bias=m_[:, b:b + 1], scale=scale, accum_out=s_[:, b:b + 1]))
                    keep(f"e{j}", t_e[j])
                for j in range(2):
                    P_, s_ = Pn[:, 4 * j:4 * j + 4, :], sm[:, 4 * j:4 * j + 4]
                    t = V([t_e[j]], lambda e: e.reciprocal(s_, s_))
                    t_n[j] = V([t], lambda e: e.tensor_tensor(P_, P_, s_.rearrange("p (b o) -> p b o", o=1).broadcast_to([P, 4, MEM]), ALU.mult))
                    for n in range(2):
                        if not pr.dry:
                            wait_all(pe, [t_n[j]])
                            for b in range(4):
                                ins = pe.transpose(ps[:, 4 * j + 2 + n, b * P:(b + 1) * P], P_[:, b, n * P:(n + 1) * P], ident)
                        t = pr.c_pe.add(None if pr.dry else ins)
                        p_ = pT[:, 2 * j + n, :]
                        if n == 0:
                            t_p[j, 0] = V([t, prev(f"o{j}")], lambda e: e.tensor_copy(p_, ps[:, 4 * j + 2, :]))
                        else:
                            t_p[j, 1] = A([t, prev(f"o{j}")], lambda e: e.activation(p_, ps[:, 4 * j + 3, :], ACT.Copy))
                    keep(f"p{j}", t)
                for j in range(2):
                    for n in range(2):
                        t_o[j, n] = mms([t_p[j, 0], t_p[j, 1], t_v[j], t_e[j]], ps[:, 4 * j + n, :],
                                        [(v_h[:, 2 * j + b, n * P:(n + 1) * P], pT[:, 2 * j + b, :]) for b in range(2)])
                    keep(f"o{j}", t_o[j, 1])
                    for n in range(2):
                        bank, k = ps[:, 4 * j + n:4 * j + n + 1, :], dslice(i, 4, 2 * j + n, 1)
                        t_h = A([t_o[j, n]], lambda e: e.activation(u_hi[:, k, XS], bank, ACT.Copy))
                        t = V([t_h], lambda e: e.tensor_tensor(u_lo[:, k, XS], bank, u_hi[:, k, XS].bitcast(F32), ALU.subtract))
                    keep(f"out{j}", t)
            pr.loop(XA_H // 2, two_heads)
            y = area(0, 8, S)
            return y, project_out(y, u_rhs, pr.all_done())

        FFN_OUTS = [[(o * DOWN_UNITS + k // UT, k % UT, k) for k in range(FT)] for o in range(4)]

        def project_down(got, name):
            return project_out(y_ffn, hid_rhs, [got[name + "1 before"]], 2, FFN_OUTS, 4 * DOWN_UNITS, before=got,
                               arrive={FT - 2: got[name + "0"], FT - 1: got[name + "1"]})

        def store_split(t, v, k):
            t2 = A([t], lambda e: e.activation(hid_hi[:, k, :], v, ACT.Copy))
            return V([t2], lambda e: e.tensor_tensor(hid_lo[:, k, :], v, hid_hi[:, k, :].bitcast(F32), ALU.subtract))

        def ffn(layer, y_in, t_y):
            head_in = prenorm(x, f"g{layer}4", ONE, pr.all_done(), each=add_after(t_y + pr.all_done(), y_in, f"g{layer}3"))
            rs = rstd[:, XS]

            def evac(i, o, banks, ready, prev, keep):
                f = o // 2
                g, w = tmp[:, 2 * f, 0:S], tmp[:, 2 * f + 1, 0:S]
                bank = ps[:, banks[0], :]
                if o % 2 == 0:
                    t = V([ready, prev(f"h{f}")], lambda e: e.tensor_tensor(g, bank, rs, ALU.mult))
                    evac.silu = A([t], lambda e: e.activation(g, g, ACT.Silu))
                    return t
                t = V([ready, prev(f"hi{f}")], lambda e: e.tensor_tensor(w, bank, rs, ALU.mult))
                t2 = V([evac.silu, t], lambda e: e.tensor_tensor(w, w, g, ALU.mult))
                keep(f"h{f}", t2)
                k = dslice(i, 2, f, 1)
                one = w.rearrange("p (o n) -> p o n", o=1)
                keep(f"hi{f}", store_split(t2, one, k))
                return t
            got = linear(FT // 2, square_outs, RING, u_rhs, ONE, evac, [], 4, head=head_in)
            return y_ffn, project_down(got, "hi")

        y, t_y = attend_memory(0, *mixed)
        y, t_y = ffn(0, y, t_y)


        def stick_breaking(y_in, t_y):
            head_in = prenorm(x, "g10", ONE, pr.all_done(), each=add_after(t_y + pr.all_done(), y_in, "g05"))
            qT, kT = area(0, 8, S), area(4096, 8, S)
            v_tok = area(12288, 4, D)
            sp_, aT = area(16384, 2, SPAN), area(18944, 2, SPAN)
            sp_hi, sp_lo = halves("sp_hi", 8192, 2, SPAN), halves("sp_lo", 16384, 2, SPAN)
            q_p, k_p, v_p = area(10752, S), area(11264, S), area(21504, 4, P)
            sums_c = sb("sums_c", [P, 4 * P], F32R, over=acc_at)
            linear(2, square_outs, RING, u_rhs, ONE, scaled_to(qT, 4, scale=SB_D ** -0.5), [], 4, head=head_in)
            got = linear(2, square_outs, RING, u_rhs, ONE, scaled_to(kT, 4), [], 4)
            table("natural_log_exp_and_others")
            t_rT = rstd_columns(7, rstd[:, XS], 4, [])
            linear_by_token(u_tok, 4, tokens_out(v_tok), [*got.values(), t_rT])
            t_all = pr.all_done()
            for n, name in enumerate(("neg_ones", "neg_suffix", "ident", "neg_fill")):
                A(t_all, lambda e: e.activation(sums_c[:, n * P:(n + 1) * P], const(name), ACT.Copy))
            neg_ones, neg_suffix, ident_r, neg_fill = (sums_c[:, n * P:(n + 1) * P] for n in range(4))
            all_wait()
            one = lambda v: v.rearrange("p (o n) -> p o n", o=1)
            flat = ps[:, :, :].rearrange("p b n -> p (b n)")
            scores = lambda h: flat[:, 3 * 512 * h:3 * 512 * h + SPAN]
            block = lambda h, b, skip=0: flat[:, 3 * 512 * h + AT[b] + skip:3 * 512 * h + AT[b] + S - b * P]

            def operands(i, t):
                pr.G([t("z1")], lambda e: e.tensor_copy(one(q_p), qT[:, dslice(i, 1, 0, 1), :]))
                t["qk"] = pr.G([], lambda e: e.tensor_copy(one(k_p), kT[:, dslice(i, 1, 0, 1), :]))

            def v_operand(i, t):
                t["v"] = pr.G([t("av1")], lambda e: e.tensor_copy(v_p, v_tok[:, :, dslice(i, P, 0, P)]))

            def scores_of(h, t):
                R = slice(64 * h, 64 * h + 64)
                if not pr.dry:
                    wait_all(pe, [t("qk"), t(f"a_0{h}")])
                    for b in range(4):
                        if b == 1:
                            wait_all(pe, [t(f"a{h}")])
                        ins = pe.matmul(block(h, b), k_p[R, b * P:(b + 1) * P], q_p[R, b * P:S],
                                        start=b != 3, stop=False, skip_group_check=True)
                t[f"z{h}"] = pr.c_pe.add(None if pr.dry else ins)

            def softplus(h, t):
                v = sp_[:, h, :]
                t1 = A([t(f"z{h}"), t(f"c{h}")], lambda e: e.activation(v, scores(h), ACT.Abs))
                t1 = A([t1], lambda e: e.activation(v, v, ACT.Exp, scale=-1.0))
                t1 = A([t1], lambda e: e.activation(v, v, ACT.Ln, bias=1.0))
                t1 = V([t1], lambda e: e.scalar_tensor_tensor(v, scores(h), 0.0, v, ALU.max, ALU.add))
                for b in range(4):
                    d = v[:, AT[b]:AT[b] + P]
                    t[f"sp{h}"] = V([t1], lambda e: e.tensor_tensor(d, d, const("strict"), ALU.mult))

            def softplus_halves(h, t):
                t1 = A([t(f"sp{h}")], lambda e: e.activation(sp_hi[:, h, :], sp_[:, h, :], ACT.Copy))
                t[f"lo{h}"] = V([t1], lambda e: e.tensor_tensor(sp_lo[:, h, :], sp_[:, h, :], sp_hi[:, h, :].bitcast(F32), ALU.subtract))

            def sums(h, t):
                if not pr.dry:
                    wait_all(pe, [t(f"lo{h}")])
                    for b in range(4):
                        for part in (sp_hi, sp_lo):
                            for j in range(3, b, -1):
                                pe.matmul(block(h, b, (j - b) * P), neg_ones, part[:, h, AT[j]:AT[j] + S - j * P],
                                          start=False, stop=False, skip_group_check=True)
                            pe.matmul(block(h, b), neg_suffix, part[:, h, AT[b]:AT[b] + S - b * P],
                                      start=False, stop=False, skip_group_check=True)
                        ins = pe.matmul(block(h, b)[:, 0:P], ident_r, neg_fill, start=False, stop=True, skip_group_check=True)
                t[f"c{h}"] = pr.c_pe.add(None if pr.dry else ins)

            def weights(h, t):
                t[f"a_0{h}"] = A([t(f"c{h}"), t(f"av{h}")], lambda e: e.activation(aT[:, h, 0:512], scores(h)[:, 0:512], ACT.Exp))
                t[f"a{h}"] = A([], lambda e: e.activation(aT[:, h, 512:SPAN], scores(h)[:, 512:SPAN], ACT.Exp))

            def times_v(h, t, blocks=(0, 1, 2, 3)):
                if not pr.dry:
                    wait_all(pe, [t(f"a{h}"), t("v"), t("out")])
                    for b in blocks:
                        ins = pe.matmul(ps[64 * h:64 * h + 64, 6, b * P:S], v_p[:, b, 64 * h:64 * h + 64],
                                        aT[:, h, AT[b]:AT[b] + S - b * P], start=b == 0, stop=b == 3, skip_group_check=True)
                t[f"av{h}"] = pr.c_pe.add(None if pr.dry else ins)

            def output(i, t):
                k = dslice(i, 1, 0, 1)
                t1 = A([t("av1")], lambda e: e.activation(u_hi[:, k, XS], ps[:, 6:7, :], ACT.Copy))
                t["out"] = V([t1], lambda e: e.tensor_tensor(u_lo[:, k, XS], ps[:, 6:7, :], u_hi[:, k, XS].bitcast(F32), ALU.subtract))

            class Last(dict):
                def __init__(self, prev):
                    self.prev = prev
                def __call__(self, name):
                    return self[name] if name in self else self.prev(name)

            def pair(i, t, more):
                v_operand(i, t)
                scores_of(0, t)
                softplus(0, t)
                times_v(0, t, (0, 1))
                sums(1, t)
                times_v(0, t, (2, 3))
                weights(1, t)
                softplus_halves(0, t)
                scores_of(1, t)
                if more:
                    operands(i + 2, t)
                softplus(1, t)
                times_v(1, t, (0, 1))
                sums(0, t)
                times_v(1, t, (2, 3))
                weights(0, t)
                softplus_halves(1, t)
                output(i, t)

            def looped_pair(i, prev, keep):
                t = Last(prev)
                pair(i, t, True)
                for name in t:
                    keep(name, t[name])

            first = Last(lambda name: None)
            operands(0, first)
            for h in range(2):
                scores_of(h, first)
            operands(1, first)
            for h in range(2):
                softplus(h, first)
                softplus_halves(h, first)
            sums(0, first)
            weights(0, first)
            all_wait()
            got = pr.loop(SB_H // 2 - 2, looped_pair)
            last, i = Last(got.get), SB_H // 2 - 1
            pair(i - 1, last, False)
            v_operand(i, last)
            sums(1, last)
            times_v(0, last)
            weights(1, last)
            times_v(1, last)
            output(i, last)
            y, memory = area(0, 8, S), memory_steps(1)
            return memory, y, *project_out(y, u_rhs, pr.all_done(), between=memory[0], late=True)

        mixed = stick_breaking(y, t_y)
        y, t_y = attend_memory(1, *mixed)
        y, t_y = ffn(1, y, t_y)

        HN = HG_H * N
        b_hi, b_lo = halves("b_hi", 2 * HN, DT, N), halves("b_lo", 4 * HN, DT, N)
        SIX_BANKS = [(TWO, [0, 1]), (TWO, [2, 3]), (TWO, [4, 5]), (TWO, [0, 1])]

        def mix(y_in, t_y):
            head_in = prenorm(x, "mix_pre", TWO, pr.all_done(), each=add_after(t_y + pr.all_done(), y_in, "g15"), abreast=2)
            proj = area(0, 20, N)
            f, vp, q, iT, g = (proj[:, 4 * n:4 * n + 4, :] for n in range(5))
            flat = lambda n: area(n * HN, HN)
            kT, aT, low_f = area(5 * HN, 4, N), area(6 * HN, 4, N), area(6 * HN, HN)
            work = 7 * HN
            masks = area(work, len(LEVELS), P).bitcast(I32)
            reset, inv = area(work + 896, N), area(work + 896 + N, 4, META)
            pool_w_sb = area(work + 1488, 4, P)
            at = work + 2000
            bufs = {}
            for name, size in (("e0", 1024), ("e1", 1024), ("a0", 1024), ("a1", 1024), ("sc", 1024), ("state", 512),
                               ("i_tok", 512), ("k_tok", 512), ("k_s", 1024)):
                bufs[name] = area(at, size)
                at += size
            wait_all(act, pr.all_done())
            for dst, src in ((area(work, 896), masks_d), (area(work + 896, 592), consts_d[:, CONST["reset"][0]:CONST_ALL]),
                             (area(work + 1488, 512), pool_w)):
                act.dma_start(dst.bitcast(I32) if src is masks_d else dst, src).then_inc(s_small, 16)
            loaded = Tok(c_small, 32 + 80 + 48)

            low = vecs[:, len(VEC) * DT + 4 * HALF_VEC["lower"]:len(VEC) * DT + 4 * HALF_VEC["lower"] + 4]
            lb, lb1, gam = tmp_small(0), tmp_small(1), tmp_small(2)
            t = V([], lambda e: e.tensor_tensor(gam, low, low, ALU.subtract))
            t = A([t], lambda e: e.activation(gam, gam, ACT.Exp))
            t = V([t], lambda e: e.reciprocal(lb, gam))
            t = V([t], lambda e: e.tensor_tensor(gam, gam, lb, ALU.mult))
            t = V([t], lambda e: e.tensor_tensor(lb, gam, gam, ALU.subtract))
            t = V([t], lambda e: e.tensor_scalar(lb, lb, 0.0, 1.0, ALU.max, ALU.min))
            t_lb = V([t], lambda e: e.tensor_scalar(lb1, lb, -1.0, 1.0, ALU.mult, ALU.add))

            st = {}
            def sigmoids():
                table("sigmoid_and_others")
                t = V([], lambda e: e.memset(bufs["sc"][:, 0:1], 0.0))
                st["k"] = A([t], lambda e: e.activation(flat(5), flat(0), ACT.Sigmoid, scale=-1.0))
                st["f"] = A([st["k"]], lambda e: e.activation(flat(0), flat(0), ACT.Sigmoid))
            def scale_k():
                for h in range(HG_H):
                    V([st["k"], t_lb], lambda e: e.tensor_scalar(kT[:, h, :], kT[:, h, :], lb1[:, h:h + 1], None, ALU.mult))
            def scale_f():
                for h in range(HG_H):
                    st["t"] = V([st["f"], t_lb], lambda e: e.tensor_scalar(f[:, h, :], f[:, h, :], lb1[:, h:h + 1], lb[:, h:h + 1], ALU.mult, ALU.add))
            def low_part():
                t = V([st["t"]], lambda e: e.tensor_scalar(low_f, flat(0), 1e-30, 2.0 ** 60, ALU.max, ALU.mult))
                st["low"] = V([t], lambda e: e.tensor_scalar(low_f, low_f, 1.0, None, ALU.min))
            def high_part():
                t = V([st["low"]], lambda e: e.tensor_scalar(flat(0), flat(0), 2.0 ** -60, None, ALU.max))
                table("natural_log_exp_and_others")
                st["l"] = A([st["low"]], lambda e: e.activation(low_f, low_f, ACT.Ln))
                st["h"] = A([t], lambda e: e.activation(flat(0), flat(0), ACT.Ln))
            def log_f():
                table("sigmoid_and_others")
                st["t"] = V([st["l"], st["h"], loaded], lambda e: e.tensor_tensor(flat(0), flat(0), low_f, ALU.add))
            def decays(h):
                return lambda: V([st["t"]], lambda e: e.tensor_tensor_scan(f[:, h, :], reset, f[:, h, :], 0.0, ALU.mult, ALU.add))

            def pool_sums(gi, width):
                def do():
                    src, d, n, t = vp[:, gi, :], 1, 0, st.get("pool")
                    while d < width:
                        dst = sq[:, n % 2, :]
                        t = V([t], lambda e: e.tensor_copy(dst[:, 0:d], src[:, 0:d]))
                        t = V([t], lambda e: e.tensor_tensor(dst[:, d:N], src[:, d:N], src[:, 0:N - d], ALU.add))
                        src, d, n = dst, 2 * d, n + 1
                    st["src"], st["sums"] = src, t
                return do
            def pool_means(gi, width):
                def do():
                    src = st["src"]
                    t = V([st["sums"], loaded], lambda e: e.tensor_tensor(src[:, 0:META], src[:, 0:META], inv[:, gi, :], ALU.mult))
                    t = V([t], lambda e: e.tensor_scalar(src[:, META:N], src[:, META:N], 1.0 / width, None, ALU.mult))
                    t = V([t], lambda e: e.tensor_tensor(src, src, vp[:, gi, :], ALU.subtract))
                    for b, (c0, c1) in enumerate(TWO):
                        st["mm"] = mms([t, loaded, st.get("pool")], ps[:, 6 + b, 0:HALF], [(pool_w_sb[:, gi, :], src[:, c0:c1])])
                return do
            def pool_out(gi):
                def do():
                    for b, (c0, c1) in enumerate(TWO):
                        st["pool"] = V([st["mm"]], lambda e: e.tensor_scalar(vp[:, gi, c0:c1], ps[:, 6 + b, 0:HALF], half_col("pool_scale", gi), None, ALU.mult))
                return do
            def joined(*steps):
                return lambda: [do() for do in steps]
            nothing = lambda: None
            slots = [nothing] * 4 + [sigmoids, scale_k, scale_f, low_part, high_part, log_f, joined(decays(0), decays(1)), joined(decays(2), decays(3))]
            for gi, width in enumerate(WINDOWS):
                slots += [joined(*([pool_out(gi - 1)] if gi else []), pool_sums(gi, width)), pool_means(gi, width)]
            def g_evac(i, o, banks, ready, prev, keep):
                t = to_proj(i, o, banks, ready, prev, keep)
                if i == 4:
                    v = g[:, o, :]
                    t1 = A([t], lambda e: e.activation(v, v, ACT.Sigmoid))
                    V([t1], lambda e: e.tensor_scalar(v, v, half_col("hg_out", o), None, ALU.mult))
                return t
            to_proj = scaled_to(proj, 4, TWO)
            linear(5, square_outs, RING, u_rhs, TWO, g_evac, [], 4, SIX_BANKS, head=head_in, between=slots)
            pool_out(3)()
            table("natural_log_exp_and_others")

            def tiles(nt, T, cols, first, prev, keep):
                W, w = nt * T, HG_H * nt * T
                sc, state, i_tok, k_tok, k_s = (bufs[n] for n in ("sc", "state", "i_tok", "k_tok", "k_s"))
                o_s = sq[:, :, :].rearrange("p a n -> p (a n)")[:, 0:1024]
                ee, ac = [bufs["e0"], bufs["e1"]], [bufs["a0"], bufs["a1"]]
                by_head = lambda v: v[:, 0:w].rearrange("p (h t) -> p h t", h=HG_H)
                by_tile = lambda v: v[:, 0:w].rearrange("p (h c t) -> p h c t", h=HG_H, t=T)
                of_tile = lambda v, h, c: v[:, (h * nt + c) * T:(h * nt + c + 1) * T]
                q_, k_, b_, i_ = (v[:, :, tile_cols(cols, 0, W)] for v in (q, kT, f, iT))
                tile4 = lambda v: v.rearrange("p h (c t) -> p h c t", t=T)
                sc3 = sc[0:T, 0:w].rearrange("p (g t) -> p g t", t=T)
                in_banks = lambda bank: ps[0:T, bank:bank + nt, 0:HG_H * T].rearrange("p c (h t) -> p (c h) t", t=T) if nt > 1 else \
                    ps[0:T, bank, 0:HG_H * T].rearrange("p (h t) -> p h t", t=T)
                bc = lambda v: v.rearrange("p (o t) -> p o t", o=1).broadcast_to([T, HG_H * nt, T])

                def products(bank, after, a_):
                    if not pr.dry:
                        wait_all(pe, after)
                        for c in range(nt):
                            for h in range(HG_H):
                                ins = pe.matmul(ps[0:T, bank + c, h * T:(h + 1) * T], of_tile(a_, h, c), of_tile(a_, h, c), start=True, stop=True)
                    return pr.c_pe.add(None if pr.dry else ins)

                t_ks = pr.G([prev("end")], lambda e: e.tensor_copy(by_head(k_s), k_))
                t = V([prev("end"), prev("end_act"), prev("end_pe")], lambda e: e.tensor_tensor(by_head(ac[1]), q_, k_, ALU.mult))
                if not pr.dry:
                    wait_all(pe, [t])
                    for c in range(nt):
                        for h in range(HG_H):
                            g_ = 2 * (c * HG_H + h)
                            ins = pe.matmul(ps[0:T, 7, g_:g_ + 2], of_tile(ac[1], h, c), ones[:, 0:2], start=True, stop=True)
                t_d = pr.c_pe.add(None if pr.dry else ins)
                t_i = A([prev("end"), prev("end_pe")], lambda e: e.activation(by_head(o_s), i_, ACT.Copy))
                diagonal = ps[0:T, 7, 0:2 * HG_H * nt].rearrange("p (g o) -> p g o", o=2)[:, :, 0:1].broadcast_to([T, HG_H * nt, T])
                t_sc = None
                t_a, t_k, t_mask = [], [], []
                def masked(n):
                    return V([], lambda e: e.copy_predicated(sc3, bc(masks[0:T, n, 0:T]), in_banks(2 * (n % 2))))
                levels = [B for B in LEVELS if B <= T]
                def level_decays(n):
                    B, e_ = levels[n], ee[n % 2]
                    hb = B // 2
                    blk = lambda v: v.rearrange("p h (n b) -> p h n b", b=B)
                    own = lambda v: blk(by_head(v))
                    t = V([t_k[n - 2] if n >= 2 else prev("end"), t_a[n - 2] if n >= 2 else None],
                          lambda e: e.tensor_tensor(own(e_), blk(b_), blk(b_)[:, :, :, hb - 1:hb].broadcast_to([P, HG_H, W // B, B]), ALU.subtract))
                    t1 = A([t], lambda e: e.activation(own(e_)[:, :, :, 0:hb], own(e_)[:, :, :, 0:hb], ACT.Exp, scale=-1.0))
                    return t1, A([], lambda e: e.activation(own(e_)[:, :, :, hb:B], own(e_)[:, :, :, hb:B], ACT.Exp))
                ahead = level_decays(0)
                for n, B in enumerate(levels):
                    (t1, t2), hb = ahead, B // 2
                    if n + 1 < len(levels):
                        ahead = level_decays(n + 1)
                    blk = lambda v: v.rearrange("p h (n b) -> p h n b", b=B)
                    own = lambda v: blk(by_head(v))
                    e_, a_ = ee[n % 2], ac[n % 2]
                    t_free = t_mask[n - 2] if n >= 2 else t_d
                    t_k.append(pr.G([t1, t_free, t_ks, prev("end_pe")], lambda e: e.tensor_tensor(own(a_)[:, :, :, 0:hb], own(k_s)[:, :, :, 0:hb], own(e_)[:, :, :, 0:hb], ALU.mult)))
                    t = V([t2, t_free, t_m, t_sc] if n else [t2, t_free], lambda e: e.tensor_tensor(own(a_)[:, :, :, hb:B], blk(q_)[:, :, :, hb:B], own(e_)[:, :, :, hb:B], ALU.mult))
                    t_a.append(t)
                    if n:
                        t_sc = masked(n - 1)
                        t_mask.append(t_sc)
                    else:
                        t_sc = V([t_d], lambda e: e.tensor_tensor(sc3, diagonal, bc(ident[0:T, 0:T]), ALU.mult))
                    t_m = products(2 * (n % 2), [t, t_k[n], t_mask[n - 2] if n >= 2 else None], a_)
                last = tile4(b_)[:, :, :, T - 1:T]
                t = V([t_a[-1], t_k[-1], t_m, t_sc], lambda e: e.tensor_tensor(by_tile(ee[0]), last.broadcast_to([P, HG_H, nt, T]), tile4(b_), ALU.subtract))
                t_sc = masked(n)
                t1 = A([t], lambda e: e.activation(ee[0][:, 0:w], ee[0][:, 0:w], ACT.Exp))
                A([], lambda e: e.activation(decay_all[:, 0:HG_H * nt].rearrange("p (h c o) -> p h c o", h=HG_H, o=1), last, ACT.Exp))
                t2 = A([], lambda e: e.activation(by_head(ee[1]), b_, ACT.Exp))
                t_ke = V([t1, t_sc], lambda e: e.tensor_tensor(by_head(ac[0]), k_, by_head(ee[0]), ALU.mult))
                t_qe = V([t2], lambda e: e.tensor_tensor(by_head(ac[1]), q_, by_head(ee[1]), ALU.mult))

                def turned(bank, src, dst, c, after, copied_after):
                    if not pr.dry:
                        wait_all(pe, after)
                        for h in range(HG_H):
                            ins = pe.transpose(ps[0:T, bank, h * P:(h + 1) * P], of_tile(src, h, c), ident)
                    t = pr.c_pe.add(None if pr.dry else ins)
                    return A([t, copied_after], lambda e: e.activation(dst[0:T, :], ps[0:T, bank, :], ACT.Copy))
                t_o, t_st, t_it, t_kt = None, None, None, None
                for c in range(nt):
                    t_it = turned(4, o_s, i_tok, c, [t_i, t_it], t_o)
                    t_kt = turned(5, ac[0], k_tok, c, [t_ke, t_kt], t_o)
                    if not pr.dry:
                        wait_all(pe, [t_sc, t_it, t_kt, t_qe, t_st])
                        for h in range(HG_H):
                            at_ = (c * HG_H + h) * T
                            ins = pe.matmul(ps[:, 6 + c, h * T:(h + 1) * T], i_tok[0:T, h * P:(h + 1) * P], sc[0:T, at_:at_ + T], start=True, stop=first)
                            if not first:
                                ins = pe.matmul(ps[:, 6 + c, h * T:(h + 1) * T], state[:, h * P:(h + 1) * P], of_tile(ac[1], h, c), start=False, stop=True)
                        for h in range(HG_H):
                            ins = pe.matmul(ps[:, c, h * P:(h + 1) * P], k_tok[0:T, h * P:(h + 1) * P], i_tok[0:T, h * P:(h + 1) * P], start=True, stop=True)
                    t_o = pr.c_pe.add(None if pr.dry else ins)
                    for h in range(HG_H):
                        hs, dc = slice(h * P, (h + 1) * P), h * nt + c
                        if first:
                            t_st = V([t_o], lambda e: e.tensor_copy(state[:, hs], ps[:, c, hs]))
                        else:
                            t_st = V([t_o], lambda e: e.scalar_tensor_tensor(state[:, hs], state[:, hs], decay_all[:, dc:dc + 1], ps[:, c, hs], ALU.mult, ALU.add))
                flat_o = o_s[:, 0:w]
                src = ps[:, 6:6 + nt, 0:HG_H * T] if nt > 1 else ps[:, 6, 0:w]
                t = A([t_o], lambda e: e.activation(flat_o.rearrange("p (c m) -> p c m", c=nt) if nt > 1 else flat_o, src, ACT.Copy))
                t = A([t], lambda e: e.activation(ee[0][:, 0:w], flat_o, ACT.Square))
                spans = [(c * HG_H * T, (c + 1) * HG_H * T) for c in range(nt)]
                for c, (c0, c1) in enumerate(spans):
                    t_ss = mms([t, t_sc], ps[:, 2 + c, 0:c1 - c0], [(ones, ee[0][:, c0:c1])])
                t = rsqrt_mean([2 + c for c in range(nt)], spans, P, ee[1], [t_ss])
                t = V([t], lambda e: e.tensor_tensor(flat_o, flat_o, ee[1][:, 0:w], ALU.mult))
                for c in range(nt):
                    out_ = aT[:, :, tile_cols(cols, c, T)]
                    g_ = g[:, :, tile_cols(cols, c, T)]
                    o_c = flat_o[:, c * HG_H * T:(c + 1) * HG_H * T].rearrange("p (h t) -> p h t", h=HG_H)
                    t2 = V([t], lambda e: e.tensor_tensor(out_, o_c, g_, ALU.mult))
                keep("end", t2)
                keep("end_act", pr.now(pr.c_act))
                keep("end_pe", pr.now(pr.c_pe))

            def tile_cols(cols, c, T):
                i, step, j = cols
                return dslice(i, step, j + c * T, T)

            all_wait()
            tiles(1, META, (0, META, 0), True, lambda n: None, lambda n, t: None)
            all_wait()
            def looped_tiles(i, prev, keep):
                tiles(2, P, (i, 2 * P, META), False, prev, keep)
            pr.loop(S // P // 2, looped_tiles)

            table("sigmoid_and_others")
            sg = area(7 * HN, 16, N)
            to_sg = scaled_to(sg, 4, TWO)
            def sg_evac(i, o, banks, ready, prev, keep):
                t = to_sg(i, o, banks, ready, prev, keep)
                v = sg[:, dslice(i, 4, o, 1), :]
                A([t], lambda e: e.activation(v, v, ACT.Sigmoid))
                return t
            t_b = []
            def split_branch(k):
                def do():
                    src = aT[:, k, :] if k < 4 else vp[:, k - 4, :]
                    t = A([], lambda e: e.activation(b_hi[:, k, :], src, ACT.Copy))
                    t_b.append(V([t], lambda e: e.tensor_tensor(b_lo[:, k, :], src, b_hi[:, k, :].bitcast(F32), ALU.subtract)))
                return do
            ts = pr.all_done()
            wait_all(act, ts)
            linear(4, square_outs, RING, u_rhs, TWO, sg_evac, ts, 4, between=[split_branch(k) for k in range(DT)])
            wait_all(dve, [pr.now(pr.c_act)])
            b_rhs = lambda k, c0, c1: (b_hi[:, k, c0:c1], b_lo[:, k, c0:c1])

            def z_evac(i, o, banks, ready, prev, keep):
                m, br = o // 2, o % 2
                s_ = sg[:, dslice(i, 8, o, 1), :]
                zt = sq[:, br:br + 1, :]
                for (c0, c1), b in zip(TWO, banks):
                    t = V([ready, prev("z7") if o < 2 else z_evac.z.get(o - 1 - br)], lambda e: e.tensor_tensor(zt[:, :, c0:c1], ps[:, b:b + 1, 0:HALF], s_[:, :, c0:c1], ALU.mult))
                if br:
                    k = dslice(i, 4, m, 1)
                    t2 = V([t], lambda e: e.tensor_tensor(zt, zt, sq[:, 0:1, :], ALU.add))
                    t2 = A([t2], lambda e: e.activation(u_hi[:, k, :], zt, ACT.Copy))
                    t2 = V([t2], lambda e: e.tensor_tensor(u_lo[:, k, :], zt, u_hi[:, k, :].bitcast(F32), ALU.subtract))
                    z_evac.z[o] = t2
                    keep(f"z{o}", t2)
                return t
            z_evac.z = {}
            outs = [[(o // 2, 4 * (o % 2) + k, 4 * (o % 2) + k) for k in range(4)] for o in range(2 * RING)]
            linear(2, outs, RING, b_rhs, TWO, z_evac, [pr.now(pr.c_dve)], 4)
            y = area(2 * DT * N, DT, N)
            return y, project_out(y, u_rhs, pr.all_done(), parts=TWO)

        tmp_small = lambda n: small[:, n, :]
        decay_all = small[:, 2:4, :].rearrange("p a b -> p (a b)")

        G0 = META - 4
        GW = N - G0
        CONV_LAYOUT = [([(G0, G0 + GW // 2), (G0 + GW // 2, N)], [0, 1]), (ONE, [2]),
                       ([(G0, G0 + GW // 2), (G0 + GW // 2, N)], [3, 4]), (ONE, [5])]

        def conv_ffn(y_in, t_y):
            table("natural_log_exp_and_others")
            head_in = prenorm(x, "ffn_pre", TWO, pr.all_done(), each=add_after(t_y + pr.all_done(), y_in, "mix_post", slice(0, N)))
            table("gelu_apprx_tanh_and_others")

            def evac(i, o, banks, ready, prev, keep):
                f_ = o // 2
                gt, w = tmp[:, 2 * f_, 0:GW], tmp[:, 2 * f_ + 1, 0:S]
                if o % 2 == 0:
                    for (c0, c1), b in zip(CONV_LAYOUT[0][0], banks):
                        t = V([ready, prev(f"done{f_}")], lambda e: e.tensor_tensor(gt[:, c0 - G0:c1 - G0], ps[:, b, 0:c1 - c0], rstd[:, c0:c1], ALU.mult))
                    one = lambda v: v.rearrange("p (o n) -> p o n", o=1)
                    tap = lambda j: conv[:, dslice(i, 2, f_, 1), j:j + 1].rearrange("p o n -> p (o n)")
                    c = sq[:, f_, 0:S]
                    lag = lambda j: gt[:, META - G0 - j:META - G0 - j + S]
                    t2 = V([t], lambda e: e.tensor_scalar(c, lag(0), tap(2), tap(3), ALU.mult, ALU.add))
                    t2 = V([t2], lambda e: e.scalar_tensor_tensor(c, lag(1), tap(1), c, ALU.mult, ALU.add))
                    t2 = V([t2], lambda e: e.scalar_tensor_tensor(c, lag(2), tap(0), c, ALU.mult, ALU.add))
                    evac.gelu = A([t2], lambda e: e.activation(c, c, ACT.Gelu_apprx_tanh))
                    return t
                c = sq[:, f_, 0:S]
                t = V([ready, prev(f"done{f_}")], lambda e: e.tensor_tensor(w, ps[:, banks[0], :], rstd[:, XS], ALU.mult))
                t2 = V([evac.gelu, t], lambda e: e.tensor_tensor(w, w, c, ALU.mult))
                k = dslice(i, 2, f_, 1)
                keep(f"done{f_}", store_split(t2, w.rearrange("p (o n) -> p o n", o=1), k))
                return t
            got = linear(FT // 2, square_outs, RING, u_rhs, ONE, evac, [], 4, CONV_LAYOUT, head=head_in)
            return y_ffn, project_down(got, "done")

        y, t_y = mix(y, t_y)
        y, t_y = conv_ffn(y, t_y)
        add = add_after(t_y, y, "ffn_post")
        for k in range(DT):
            add(k).wait(sp)
            sp.dma_start(out[k * P:(k + 1) * P, :], x[:, k, XS]).then_inc(s_out, 16)
        wait_all(sp, pr.all_done())
        sp.wait_ge(s_out, 16 * DT)


def tiles_of(w, tiles):
    k, m = w.shape[0] // P, w.shape[1] // P
    t = np.asarray(w).reshape(k, P, m, P).transpose(0, 2, 1, 3)
    return [t[a, b] for a, b in tiles]


def pack(*tile_lists):
    flat = [t for ts in tile_lists for t in ts]
    blank = np.zeros((P, P), np.float32)
    flat = [blank if t is None else t for t in flat]
    a = np.stack(flat).reshape(-1, UT, P, P)
    return a.transpose(0, 2, 1, 3).reshape(-1, P, UT * P)


def by_output(w, cols=None):
    k, m = w.shape[0] // P, w.shape[1] // P
    return tiles_of(w, [(a, b) for b in (cols or range(m)) for a in range(k)])


def by_token(w):
    return tiles_of(w, [(a, 4 * g + b) for g in range(2) for a in range(DT) for b in range(4)])


def down_tiles(w):
    out = []
    for b in range(w.shape[1] // P):
        out += tiles_of(w, [(a, b) for a in range(FT)]) + [None] * (DOWN_UNITS * UT - FT)
    return out


def pairs_of(a, b):
    out = []
    for c in range(a.shape[1] // P):
        out += by_output(a, [c]) + by_output(b, [c])
    return out


def kernel(**inputs):
    import concourse.bacc as bacc
    from concourse.bass_utils import run_bass_kernel_spmd
    a = {k: np.asarray(v) for k, v in inputs.items()}
    stream = []
    w = a["ml_w_in"][0]
    stream += [by_output(w[:, 0:1024]), by_output(w[:, 2048:3072]), by_token(w[:, 1024:2048])]
    gates_w = w[:, 3072:3080]
    stream += [by_output(a["ml_w_out"][0])]
    for layer in range(2):
        if layer == 1:
            qkv = a["sb_w_qkv"][0]
            stream += [by_output(qkv[:, :2 * D]), by_token(qkv[:, 2 * D:]), by_output(a["sb_w_out"][0])]
        kv = a["xa_w_kv"][layer]
        stream += [by_output(kv[:, :D]), by_token(kv[:, D:]), by_output(a["xa_w_q"][layer]), by_output(a["xa_w_o"][layer])]
        gu = a["ffn_w_gate_up"][layer]
        stream += [pairs_of(gu[:, :FF], gu[:, FF:]), down_tiles(a["ffn_w_down"][layer])]
    w2 = a["w_in_2"][0]
    stream += [by_output(w2[:, 512:1024]), by_output(w2[:, 2048:2560]), by_output(w2[:, 0:512]), by_output(w2[:, 1024:2048])]
    stream += [pairs_of(w2[:, 2560:3584], w2[:, 3584:4608])]
    stream += [pairs_of(a["w_branch_hgrn_2"][0], a["w_branch_pool_2"][0]), by_output(a["w_out_2"][0])]
    stream += [pairs_of(a["ffn_w_gate_2"][0], a["ffn_w_up_2"][0]), down_tiles(a["ffn_w_down_2"][0])]
    units = pack(*stream)
    xT = np.concatenate([a["meta_tokens_2"].T, a["x"][0].T], axis=1)
    col = lambda v: v.reshape(-1, P).T
    full = [a["norm_gains"][l, n] for l in range(2) for n in range(6)]
    full += [a["mem_norm_gain"], a["ml_head_gain"][0], a["mix_norm_pre_2"][0], a["mix_norm_post_2"][0],
             a["ffn_norm_pre_2"][0], a["ffn_norm_post_2"][0]]
    half = [a["hgrn_out_norm_2"][0], a["pool_scale_2"][0], a["hgrn_lower_bounds_2"][0]]
    vecs = np.concatenate([col(v) for v in full + half], axis=1)
    conv = np.stack([col(a["ffn_conv_w_2"][0, j]) for j in range(CONV)] + [col(a["ffn_conv_b_2"][0])], axis=2)
    consts, masks = shape_constants()
    arrays = {"units": units, "xT": xT, "memT": a["mem"][0].T, "vecs": vecs, "gates_w": gates_w,
              "gates_b": a["ml_b_gate"][0].reshape(8, 1), "pool_w": a["pool_proj_2"][0].transpose(1, 0, 2).reshape(P, -1),
              "conv": conv.reshape(P, -1), "consts": consts, "masks": masks}
    arrays = {k: np.ascontiguousarray(v) for k, v in arrays.items()}
    nc = bacc.Bacc("TRN2", target_bir_lowering=False, num_devices=1)
    args = [nc.dram_tensor(f"in_{k}", v.shape, mybir.dt.from_np(v.dtype), kind="ExternalInput").ap() for k, v in arrays.items()]
    o = nc.dram_tensor("outT", (D, S), F32, kind="ExternalOutput").ap()
    build(nc, *args, o)
    r = run_bass_kernel_spmd(nc, [{f"in_{k}": v for k, v in arrays.items()}], core_ids=[0])
    return np.ascontiguousarray(r.results[0]["outT"].T)[None]
```
